# Optimizing a Trainium2 kernel written in Bass

```python
import jax, jax.numpy as jnp
from jax import lax
import numpy as np

D_MODEL = 2048
BATCH = 1
SEQ = 256
DEPTH = 1

CHUNK = 64
Q_BLOCK = 128
HEAD_DIM = 128
N_HEADS = 4
BRANCH_W = N_HEADS * HEAD_DIM
N_BRANCH = 3
LEFT_CHUNKS = 8
BAND = (LEFT_CHUNKS + 1) * CHUNK
MAX_REL = 128
N_REL = 2 * MAX_REL + 1
QKVG_COLS = N_BRANCH * 4 * BRANCH_W
IN_COLS = QKVG_COLS + N_HEADS + N_BRANCH * D_MODEL
EPS = 1e-6
NEG = -1e30


def rmsnorm(x, g):
    xf = x.astype(jnp.float32)
    y = xf * lax.rsqrt(jnp.mean(xf * xf, axis=-1, keepdims=True) + EPS)
    return (y * g.astype(jnp.float32)).astype(x.dtype)

def to_heads(t):
    b, s, _ = t.shape
    return t.reshape(b, s, N_HEADS, HEAD_DIM).transpose(0, 2, 1, 3)

def from_heads(o):
    b, h, s, d = o.shape
    return o.transpose(0, 2, 1, 3).reshape(b, s, h * d)

def to_blocks(t, size):
    b, h, s, d = t.shape
    return t.reshape(b, h, s // size, size, d).transpose(2, 0, 1, 3, 4)

def from_blocks(o):
    nb, b, h, size, d = o.shape
    return o.transpose(1, 2, 0, 3, 4).reshape(b, h, nb * size, d)

def forgetting_attention(q, k, v, f_logit):
    b, h, s, d = q.shape
    nb = s // Q_BLOCK
    scale = d ** -0.5
    log_f = jax.nn.log_sigmoid(f_logit.astype(jnp.float32))
    c = jnp.cumsum(log_f, axis=1).transpose(0, 2, 1)
    outs = []
    for i in range(nb):
        lo, hi = i * Q_BLOCK, (i + 1) * Q_BLOCK
        logits = jnp.einsum('bhqd,bhkd->bhqk', q[:, :, lo:hi], k[:, :, :hi]).astype(jnp.float32) * scale
        logits = logits + c[:, :, lo:hi, None] - c[:, :, None, :hi]
        mask = jnp.arange(hi)[None, :] <= jnp.arange(lo, hi)[:, None]
        logits = jnp.where(mask, logits, NEG)
        p = jax.nn.softmax(logits, axis=-1).astype(v.dtype)
        outs.append(jnp.einsum('bhqk,bhkd->bhqd', p, v[:, :, :hi]))
    return jnp.concatenate(outs, axis=2)

def chunked_relpos_attention(q, k, v, rel_bias):
    b, h, s, d = q.shape
    nc = s // CHUNK
    scale = d ** -0.5
    pad = LEFT_CHUNKS * CHUNK
    kp = jnp.pad(k, ((0, 0), (0, 0), (pad, 0), (0, 0)))
    vp = jnp.pad(v, ((0, 0), (0, 0), (pad, 0), (0, 0)))
    qi_pos = jnp.arange(CHUNK)
    band_pos = jnp.arange(BAND)
    rel = pad + qi_pos[:, None] - band_pos[None, :]
    idx = jnp.clip(rel, -MAX_REL, MAX_REL) + MAX_REL
    bias = rel_bias[:, idx].astype(jnp.float32)

    def chunk(args):
        qc, ci = args
        start = ci * CHUNK
        kb = lax.dynamic_slice_in_dim(kp, start, BAND, axis=2)
        vb = lax.dynamic_slice_in_dim(vp, start, BAND, axis=2)
        logits = jnp.einsum('bhqd,bhkd->bhqk', qc, kb).astype(jnp.float32) * scale + bias
        valid = (start - pad + band_pos) >= 0
        logits = jnp.where(valid, logits, NEG)
        p = jax.nn.softmax(logits, axis=-1).astype(v.dtype)
        return jnp.einsum('bhqk,bhkd->bhqd', p, vb)

    o = lax.map(chunk, (to_blocks(q, CHUNK), jnp.arange(nc)))
    return from_blocks(o)

def stick_breaking_attention(q, k, v):
    b, h, s, d = q.shape
    nb = s // Q_BLOCK
    scale = d ** -0.5
    ar = jnp.arange(Q_BLOCK)
    upper = (ar[:, None] >= ar[None, :]).astype(jnp.float32)
    hp = lax.Precision.HIGHEST
    outs = []
    for i in range(nb):
        nk = i + 1
        lo, hi = i * Q_BLOCK, nk * Q_BLOCK
        z = jnp.einsum('bhqd,bhkd->bhqk', q[:, :, lo:hi], k[:, :, :hi]).astype(jnp.float32) * scale
        mask = jnp.arange(hi)[None, :] < jnp.arange(lo, hi)[:, None]
        lk = jnp.where(mask, jax.nn.log_sigmoid(-z), 0.0).reshape(b, h, Q_BLOCK, nk, Q_BLOCK)
        r_in = jnp.einsum('bhqnk,kj->bhqnj', lk, upper, precision=hp)
        tot = r_in[..., 0]
        nbk = jnp.arange(nk)
        later_m = (nbk[:, None] > nbk[None, :]).astype(jnp.float32)
        later = jnp.einsum('bhqm,mn->bhqn', tot, later_m, precision=hp)
        r = (r_in + later[..., None]).reshape(b, h, Q_BLOCK, hi)
        a = jnp.where(mask, jnp.exp(z + r), 0.0).astype(v.dtype)
        outs.append(jnp.einsum('bhqk,bhkd->bhqd', a, v[:, :, :hi]))
    return jnp.concatenate(outs, axis=2)

def hybrid_layer(x, norm_g, w_in, b_f, b_gate, qk_norm_g, rel_bias, w_up, w_out):
    b, s, _ = x.shape
    hn = rmsnorm(x, norm_g)
    proj = jnp.einsum('bsd,dc->bsc', hn, w_in)
    br = proj[..., :QKVG_COLS].reshape(b, s, N_BRANCH, 4, BRANCH_W)
    f_logit = proj[..., QKVG_COLS:QKVG_COLS + N_HEADS] + b_f
    gates = jax.nn.sigmoid(proj[..., QKVG_COLS + N_HEADS:] + b_gate).reshape(b, s, N_BRANCH, D_MODEL)

    qa = rmsnorm(to_heads(br[:, :, 0, 0]), qk_norm_g[0])
    ka = rmsnorm(to_heads(br[:, :, 0, 1]), qk_norm_g[1])
    ya = forgetting_attention(qa, ka, to_heads(br[:, :, 0, 2]), f_logit)
    qb = rmsnorm(to_heads(br[:, :, 1, 0]), qk_norm_g[2])
    kb = rmsnorm(to_heads(br[:, :, 1, 1]), qk_norm_g[3])
    yb = chunked_relpos_attention(qb, kb, to_heads(br[:, :, 1, 2]), rel_bias)
    yc = stick_breaking_attention(to_heads(br[:, :, 2, 0]), to_heads(br[:, :, 2, 1]),
                                  to_heads(br[:, :, 2, 2]))

    ys = jnp.stack([from_heads(ya), from_heads(yb), from_heads(yc)], axis=2)
    ys = ys * jax.nn.silu(br[:, :, :, 3])
    up = jnp.einsum('bsnw,nwd->bsnd', ys, w_up)
    merged = jnp.sum(gates * up, axis=2)
    return x + jnp.einsum('bsd,de->bse', merged, w_out)

def first_inputs(seed: int = 0) -> dict:
    key = jax.random.key(seed)
    ks = jax.random.split(key, 10)
    f32 = jnp.float32
    x = jax.random.normal(ks[0], (BATCH, SEQ, D_MODEL), f32)
    norm_g = 1.0 + 0.02 * jax.random.normal(ks[1], (DEPTH, D_MODEL), f32)
    w_in = jax.random.normal(ks[2], (DEPTH, D_MODEL, IN_COLS), f32) * D_MODEL ** -0.5
    b_f = 3.0 + 0.1 * jax.random.normal(ks[3], (DEPTH, N_HEADS), f32)
    b_gate = 0.02 * jax.random.normal(ks[4], (DEPTH, N_BRANCH * D_MODEL), f32)
    qk_norm_g = 1.0 + 0.02 * jax.random.normal(ks[5], (DEPTH, 4, HEAD_DIM), f32)
    rel_bias = 0.5 * jax.random.normal(ks[6], (DEPTH, N_HEADS, N_REL), f32)
    w_up = jax.random.normal(ks[7], (DEPTH, N_BRANCH, BRANCH_W, D_MODEL), f32) * BRANCH_W ** -0.5
    w_out = jax.random.normal(ks[8], (DEPTH, D_MODEL, D_MODEL), f32) * D_MODEL ** -0.5
    return {"x": x, "norm_g": norm_g, "w_in": w_in, "b_f": b_f, "b_gate": b_gate,
            "qk_norm_g": qk_norm_g, "rel_bias": rel_bias, "w_up": w_up, "w_out": w_out}

def first_block(x, norm_g, w_in, b_f, b_gate, qk_norm_g, rel_bias, w_up, w_out):
    for layer in range(DEPTH):
        x = hybrid_layer(x, norm_g[layer], w_in[layer], b_f[layer], b_gate[layer],
                         qk_norm_g[layer], rel_bias[layer], w_up[layer], w_out[layer])
    return x


CTX_LEN = 256
GRID_W = 64
N_DIR = 2
MIX_WIDTH = D_MODEL
GLA_HEADS = 4
GLA_WIDTH = MIX_WIDTH // 2
GLA_DV = GLA_WIDTH // GLA_HEADS
GLA_DK = GLA_DV // 2
GLA_LR = 16
GLA_NORMALIZER = 16.0
MLSTM_HEADS = 4
MLSTM_WIDTH = MIX_WIDTH - GLA_WIDTH
MLSTM_DV = MLSTM_WIDTH // MLSTM_HEADS
MLSTM_DK = MLSTM_DV // 2
D_FF = 128 * ((8 * D_MODEL // 3 + 127) // 128)
CONV_K = 3

PROJ_SIZES = (GLA_HEADS * GLA_DK, GLA_HEADS * GLA_DK, GLA_WIDTH, GLA_WIDTH, GLA_LR,
              MLSTM_HEADS * MLSTM_DK, MLSTM_HEADS * MLSTM_DK, MLSTM_WIDTH, MLSTM_WIDTH,
              N_DIR * 2 * MLSTM_HEADS)
PROJ_WIDTH = sum(PROJ_SIZES)
PROJ_SPLITS = tuple(int(s) for s in np.cumsum(PROJ_SIZES)[:-1])


def rmsnorm_2(x, g):
    xf = x.astype(jnp.float32)
    y = xf * lax.rsqrt(jnp.mean(jnp.square(xf), axis=-1, keepdims=True) + EPS)
    return (y * g.astype(jnp.float32)).astype(x.dtype)

def _rev(t, d):
    return jnp.flip(t, axis=1) if d == 1 else t

def _chunk(t):
    b, t_len = t.shape[:2]
    t = t.reshape((b, t_len // CHUNK, CHUNK) + t.shape[2:])
    return jnp.swapaxes(jnp.moveaxis(t, 1, 0), 2, 3)

def _unchunk(t):
    n, b, h, c, d = t.shape
    return jnp.moveaxis(jnp.swapaxes(t, 2, 3), 0, 1).reshape(b, n * c, h, d)

def gla_scan(k, v, log_a, s0, q=None):
    tril = jnp.tril(jnp.ones((CHUNK, CHUNK), dtype=bool))
    xs = (_chunk(k), _chunk(v), _chunk(log_a)) + ((_chunk(q),) if q is not None else ())

    def step(s, inp):
        kc, vc, ac = inp[:3]
        bcum = jnp.cumsum(ac, axis=2)
        b_end = bcum[:, :, -1, :]
        k_to_end = kc * jnp.exp(b_end[:, :, None, :] - bcum)
        s_new = jnp.exp(b_end)[..., None] * s + jnp.einsum('bhik,bhiv->bhkv', k_to_end, vc)
        if q is None:
            return s_new, None
        qc = inp[3]
        rel = jnp.where(tril[:, :, None], bcum[:, :, :, None, :] - bcum[:, :, None, :, :], -jnp.inf)
        scores = jnp.einsum('bhjk,bhik,bhjik->bhji', qc, kc, jnp.exp(rel))
        o = (jnp.einsum('bhji,bhiv->bhjv', scores, vc)
             + jnp.einsum('bhjk,bhkv->bhjv', qc * jnp.exp(bcum), s))
        return s_new, o

    s_fin, o = lax.scan(step, s0, xs)
    return s_fin, (None if q is None else _unchunk(o))

def mlstm_scan(k, v, log_i, log_f, state0, q=None):
    tril = jnp.tril(jnp.ones((CHUNK, CHUNK), dtype=bool))
    xs = (_chunk(k), _chunk(v), _chunk(log_i), _chunk(log_f)) + ((_chunk(q),) if q is not None else ())

    def step(carry, inp):
        c, n, m = carry
        kc, vc, ic, fc = inp[:4]
        fcum = jnp.cumsum(fc, axis=-1)
        f_end = fcum[..., -1]
        w_log = f_end[..., None] - fcum + ic
        m_new = jnp.maximum(f_end + m, jnp.max(w_log, axis=-1))
        carry_scale = jnp.exp(f_end + m - m_new)
        w = jnp.exp(w_log - m_new[..., None])
        c_new = carry_scale[..., None, None] * c + jnp.einsum('bhi,bhik,bhiv->bhkv', w, kc, vc)
        n_new = carry_scale[..., None] * n + jnp.einsum('bhi,bhik->bhk', w, kc)
        if q is None:
            return (c_new, n_new, m_new), None
        qc = inp[4]
        d_log = jnp.where(tril, fcum[..., :, None] - fcum[..., None, :] + ic[..., None, :], -jnp.inf)
        inter_log = fcum + m[..., None]
        m_q = jnp.maximum(inter_log, jnp.max(d_log, axis=-1))
        s = jnp.einsum('bhjk,bhik->bhji', qc, kc) * jnp.exp(d_log - m_q[..., None])
        inter = jnp.exp(inter_log - m_q)
        num = (jnp.einsum('bhji,bhiv->bhjv', s, vc)
               + inter[..., None] * jnp.einsum('bhjk,bhkv->bhjv', qc, c))
        den = jnp.sum(s, axis=-1) + inter * jnp.einsum('bhjk,bhk->bhj', qc, n)
        h = num / jnp.maximum(jnp.abs(den), jnp.exp(-m_q))[..., None]
        return (c_new, n_new, m_new), h

    st_fin, h = lax.scan(step, state0, xs)
    return st_fin, (None if q is None else _unchunk(h))

def project_heads(h, w_in, gla_w_lr, gla_b_lr, mlstm_b_gate):
    b, t, _ = h.shape
    f32 = jnp.float32
    z = jnp.einsum('btd,dp->btp', h, w_in)
    gq, gk, gv, gg, glr, mq, mk, mv, mo, mgate = jnp.split(z, PROJ_SPLITS, axis=-1)
    gla_q = gq.reshape(b, t, GLA_HEADS, GLA_DK).astype(f32) * (GLA_DK ** -0.5)
    gla_k = gk.reshape(b, t, GLA_HEADS, GLA_DK).astype(f32)
    gla_v = gv.reshape(b, t, GLA_HEADS, GLA_DV).astype(f32)
    gla_gate = gg.reshape(b, t, GLA_HEADS, GLA_DV)
    dec = jnp.einsum('btr,zrk->zbtk', glr, gla_w_lr) + gla_b_lr[:, None, None, :]
    gla_loga = (jax.nn.log_sigmoid(dec.astype(f32)) / GLA_NORMALIZER).reshape(N_DIR, b, t, GLA_HEADS, GLA_DK)
    ml_q = mq.reshape(b, t, MLSTM_HEADS, MLSTM_DK).astype(f32)
    ml_k = mk.reshape(b, t, MLSTM_HEADS, MLSTM_DK).astype(f32) * (MLSTM_DK ** -0.5)
    ml_v = mv.reshape(b, t, MLSTM_HEADS, MLSTM_DV).astype(f32)
    ml_ogate = mo.reshape(b, t, MLSTM_HEADS, MLSTM_DV)
    pre = (mgate.reshape(b, t, N_DIR, 2, MLSTM_HEADS) + mlstm_b_gate).astype(f32)
    ml_logi = jnp.moveaxis(pre[:, :, :, 0], 2, 0)
    ml_logf = jnp.moveaxis(jax.nn.log_sigmoid(pre[:, :, :, 1]), 2, 0)
    scan_in = (gla_q, gla_k, gla_v, gla_loga, ml_q, ml_k, ml_v, ml_logi, ml_logf)
    return scan_in, (gla_gate, ml_ogate)

def recurrent_groups(lat, ctx, with_ctx_out):
    gq, gk, gv, ga, mq, mk, mv, mi, mf = lat
    cq, ck, cv, ca, cmq, cmk, cmv, cmi, cmf = ctx
    b = gq.shape[0]
    f32 = jnp.float32
    gla_lat, ml_lat, gla_ctx, ml_ctx = [], [], [], []
    for d in range(N_DIR):
        s0 = jnp.zeros((b, GLA_HEADS, GLA_DK, GLA_DV), f32)
        s_ctx, o_ctx = gla_scan(_rev(ck, d), _rev(cv, d), _rev(ca[d], d), s0,
                                _rev(cq, d) if with_ctx_out else None)
        _, o_lat = gla_scan(_rev(gk, d), _rev(gv, d), _rev(ga[d], d), s_ctx, _rev(gq, d))
        gla_lat.append(_rev(o_lat, d))
        st0 = (jnp.zeros((b, MLSTM_HEADS, MLSTM_DK, MLSTM_DV), f32),
               jnp.zeros((b, MLSTM_HEADS, MLSTM_DK), f32),
               jnp.zeros((b, MLSTM_HEADS), f32))
        st_ctx, h_ctx = mlstm_scan(_rev(cmk, d), _rev(cmv, d), _rev(cmi[d], d), _rev(cmf[d], d), st0,
                                   _rev(cmq, d) if with_ctx_out else None)
        _, h_lat = mlstm_scan(_rev(mk, d), _rev(mv, d), _rev(mi[d], d), _rev(mf[d], d), st_ctx, _rev(mq, d))
        ml_lat.append(_rev(h_lat, d))
        if with_ctx_out:
            gla_ctx.append(_rev(o_ctx, d))
            ml_ctx.append(_rev(h_ctx, d))
    lat_out = (gla_lat[0] + gla_lat[1], ml_lat[0] + ml_lat[1])
    ctx_out = (gla_ctx[0] + gla_ctx[1], ml_ctx[0] + ml_ctx[1]) if with_ctx_out else None
    return lat_out, ctx_out

def merge_groups(gla_o, ml_h, gla_gate, ml_ogate, gla_g_norm, mlstm_g_norm, w_out, dtype):
    b, t = gla_o.shape[:2]
    f32 = jnp.float32
    y_gla = rmsnorm_2(gla_o, gla_g_norm) * jax.nn.silu(gla_gate.astype(f32))
    y_ml = jax.nn.sigmoid(ml_ogate.astype(f32)) * rmsnorm_2(ml_h, mlstm_g_norm)
    y = jnp.concatenate([y_gla.reshape(b, t, GLA_WIDTH), y_ml.reshape(b, t, MLSTM_WIDTH)], axis=-1)
    return jnp.einsum('btm,md->btd', y.astype(dtype), w_out)

def conv_ffn(h, rows, cols, w_up, conv_w, conv_b, w_down):
    b, t, _ = h.shape
    u = jnp.einsum('btd,df->btf', h, w_up)
    u_gate, u_val = jnp.split(u, 2, axis=-1)
    g = lax.conv_general_dilated(u_gate.reshape(b, rows, cols, D_FF), conv_w[:, :, None, :],
                                 window_strides=(1, 1), padding='SAME',
                                 dimension_numbers=('NHWC', 'HWIO', 'NHWC'),
                                 feature_group_count=D_FF)
    g = g.reshape(b, t, D_FF) + conv_b
    return jnp.einsum('btf,fd->btd', jax.nn.silu(g) * u_val, w_down)

def trunk_layer(x, ctx, c_act, cc_act, w_mod, b_mod, g_norm1, g_norm2, w_in, gla_w_lr, gla_b_lr,
                mlstm_b_gate, gla_g_norm, mlstm_g_norm, w_out, w_up, conv_w, conv_b, w_down, update_ctx):
    b, t, _ = x.shape
    rows = t // GRID_W
    mod = (c_act @ w_mod + b_mod)[:, None, :]
    mod_c = (cc_act @ w_mod + b_mod)[None, None, :]
    sh1, sc1, gt1, sh2, sc2, gt2 = jnp.split(mod, 6, axis=-1)
    csh1, csc1, cgt1, csh2, csc2, cgt2 = jnp.split(mod_c, 6, axis=-1)

    h = rmsnorm_2(x, g_norm1) * (1 + sc1) + sh1
    hc = rmsnorm_2(ctx, g_norm1) * (1 + csc1) + csh1
    lat_in, lat_gates = project_heads(h, w_in, gla_w_lr, gla_b_lr, mlstm_b_gate)
    ctx_in, ctx_gates = project_heads(hc, w_in, gla_w_lr, gla_b_lr, mlstm_b_gate)
    (lat_gla, lat_ml), ctx_out = recurrent_groups(lat_in, ctx_in, update_ctx)
    x = x + gt1 * merge_groups(lat_gla, lat_ml, lat_gates[0], lat_gates[1],
                               gla_g_norm, mlstm_g_norm, w_out, x.dtype)

    h2 = rmsnorm_2(x, g_norm2) * (1 + sc2) + sh2
    x = x + gt2 * conv_ffn(h2, rows, GRID_W, w_up, conv_w, conv_b, w_down)

    if update_ctx:
        ctx = ctx + cgt1 * merge_groups(ctx_out[0], ctx_out[1], ctx_gates[0], ctx_gates[1],
                                        gla_g_norm, mlstm_g_norm, w_out, ctx.dtype)
        hc2 = rmsnorm_2(ctx, g_norm2) * (1 + csc2) + csh2
        ctx = ctx + cgt2 * conv_ffn(hc2, 1, ctx.shape[1], w_up, conv_w, conv_b, w_down)
    return x, ctx

def second_inputs(seed: int = 0) -> dict:
    key = jax.random.key(seed)
    ks = jax.random.split(key, 20)
    f32 = jnp.float32
    L = DEPTH

    def nrm(k, shape, s):
        return jax.random.normal(k, shape, f32) * s

    gate_base = jnp.array([0.0, 3.0], f32)[None, None, :, None]
    return {
        'x': nrm(ks[0], (BATCH, SEQ, D_MODEL), 1.0),
        'c': nrm(ks[1], (BATCH, D_MODEL), 1.0),
        'ctx': nrm(ks[2], (BATCH, CTX_LEN, D_MODEL), 1.0),
        'c_ctx': nrm(ks[3], (D_MODEL,), 1.0),
        'w_mod': nrm(ks[4], (L, D_MODEL, 6 * D_MODEL), D_MODEL ** -0.5),
        'b_mod': nrm(ks[5], (L, 6 * D_MODEL), 0.01),
        'g_norm1': 1.0 + nrm(ks[6], (L, D_MODEL), 0.05),
        'g_norm2': 1.0 + nrm(ks[7], (L, D_MODEL), 0.05),
        'w_in': nrm(ks[8], (L, D_MODEL, PROJ_WIDTH), D_MODEL ** -0.5),
        'gla_w_lr': nrm(ks[9], (L, N_DIR, GLA_LR, GLA_HEADS * GLA_DK), GLA_LR ** -0.5),
        'gla_b_lr': nrm(ks[10], (L, N_DIR, GLA_HEADS * GLA_DK), 0.1),
        'mlstm_b_gate': gate_base + nrm(ks[11], (L, N_DIR, 2, MLSTM_HEADS), 0.1),
        'gla_g_norm': 1.0 + nrm(ks[12], (L, GLA_DV), 0.05),
        'mlstm_g_norm': 1.0 + nrm(ks[13], (L, MLSTM_DV), 0.05),
        'w_out': nrm(ks[14], (L, MIX_WIDTH, D_MODEL), MIX_WIDTH ** -0.5),
        'w_up': nrm(ks[15], (L, D_MODEL, 2 * D_FF), D_MODEL ** -0.5),
        'conv_w': nrm(ks[16], (L, CONV_K, CONV_K, D_FF), 1.0 / CONV_K),
        'conv_b': nrm(ks[17], (L, D_FF), 0.01),
        'w_down': nrm(ks[18], (L, D_FF, D_MODEL), D_FF ** -0.5),
        'g_final': 1.0 + nrm(ks[19], (D_MODEL,), 0.05),
    }

def second_block(x, c, ctx, c_ctx, w_mod, b_mod, g_norm1, g_norm2, w_in, gla_w_lr, gla_b_lr, mlstm_b_gate,
              gla_g_norm, mlstm_g_norm, w_out, w_up, conv_w, conv_b, w_down, g_final):
    c_act = jax.nn.silu(c)
    cc_act = jax.nn.silu(c_ctx)
    for l in range(DEPTH):
        x, ctx = trunk_layer(x, ctx, c_act, cc_act, w_mod[l], b_mod[l], g_norm1[l], g_norm2[l], w_in[l],
                             gla_w_lr[l], gla_b_lr[l], mlstm_b_gate[l], gla_g_norm[l], mlstm_g_norm[l],
                             w_out[l], w_up[l], conv_w[l], conv_b[l], w_down[l],
                             update_ctx=(l < DEPTH - 1))
    return rmsnorm_2(x, g_final)


def setup_inputs(seed=0):
    out = dict(first_inputs(seed))
    for name, value in second_inputs(seed + 1).items():
        if name != "x":
            out[name + "_2"] = value
    return out


def reference(
    x, norm_g, w_in, b_f, b_gate, qk_norm_g, rel_bias, w_up, w_out, c_2, ctx_2, c_ctx_2,
    w_mod_2, b_mod_2, g_norm1_2, g_norm2_2, w_in_2, gla_w_lr_2, gla_b_lr_2, mlstm_b_gate_2,
    gla_g_norm_2, mlstm_g_norm_2, w_out_2, w_up_2, conv_w_2, conv_b_2, w_down_2, g_final_2,
):
    x = first_block(
        x, norm_g, w_in, b_f, b_gate, qk_norm_g, rel_bias, w_up, w_out,
    )
    return second_block(
        x, c_2, ctx_2, c_ctx_2, w_mod_2, b_mod_2, g_norm1_2, g_norm2_2, w_in_2, gla_w_lr_2,
        gla_b_lr_2, mlstm_b_gate_2, gla_g_norm_2, mlstm_g_norm_2, w_out_2, w_up_2, conv_w_2,
        conv_b_2, w_down_2, g_final_2,
    )


_drawn_inputs = setup_inputs


def setup_inputs(seed=0):
    import zlib

    import numpy as np

    out = dict(_drawn_inputs(seed))
    spreads = {}
    factors = {'norm_g': 5.242,
     'b_f': 51.096,
     'b_gate': 8.0,
     'qk_norm_g': 8.0,
     'b_mod_2': 18.256,
     'gla_g_norm_2': 26.152,
     'mlstm_g_norm_2': 200.0,
     'conv_b_2': 64.0,
     'ctx_2': 4.028,
     'c_ctx_2': 3.323,
     'g_norm1_2': 6.475,
     'g_norm2_2': 8.0,
     'gla_w_lr_2': 3.074,
     'gla_b_lr_2': 8.0}
    for name, (base, spread) in spreads.items():
        noise = np.random.default_rng([zlib.crc32(name.encode()), seed]).standard_normal(out[name].shape)
        drawn = base * np.exp(spread * noise) if base else spread * noise
        out[name] = __import__('jax').numpy.asarray(drawn.astype(out[name].dtype))
    for name, factor in factors.items():
        out[name] = (out[name] * factor).astype(out[name].dtype)
    return out
```

```python
import concourse.bass as bass
from concourse import mybir
import numpy as np

F32 = mybir.dt.float32
F32R = mybir.dt.float32r
ALU = mybir.AluOpType
ACT = mybir.ActivationFunctionType
AX_X = mybir.AxisListType.X

P = 128
T = 256
RT = T // P
D = 2048
KC = D // P
NBLK = 512
UK = 2
SLOTS = 4
BU = KC // UK
HD = 128
HEADS = 4
BW = HEADS * HD
NBR = 3
MAX_REL = 128
CHUNK = 64
EPS = 1e-6
NEG = -1e30
SCALE = float(HD) ** -0.5
FF = 5504
FCH = FF // P
GDV = 256
NORMALIZER = 16.0
DC = D // NBLK

U_QKVG = 0
UPU = BW // P // UK
PAIR = BU + UPU
U_GATE0 = U_QKVG + 12 * BU
U_UP0 = U_GATE0 + DC * BU
U_PAIRS = U_UP0 + DC * UPU
U_OUT = U_PAIRS + 2 * DC * PAIR
U_CTX = U_OUT + DC * BU
U_X = U_CTX + 6 * BU
U_OUT2 = U_X + 12 * BU
U_FFN = U_OUT2 + DC * BU
FB = 22
U_DOWN = U_FFN + FB * BU
DU = (FCH + 1) // UK
U_END = U_DOWN + DC * DU

B_GATE0, B_UP0, B_PAIRS, B_OUT, B_CTX, B_X, B_OUT2, B_FFN, B_DOWN = 12, 16, 20, 36, 40, 46, 58, 62, 84


def constants():
    t = np.arange(P)
    row, col = t[:, None], t[None, :]
    one = np.ones((P, P), np.float32)
    c = {}
    c["ident"] = (row == col)
    c["anti"] = (row + col == P - 1)
    c["pre_in"] = (row <= col) / NORMALIZER
    c["suf_in"] = (row >= col) / NORMALIZER
    c["pre_ex"] = (row < col) / NORMALIZER
    c["suf_ex"] = (row > col) / NORMALIZER
    c["all"] = one / NORMALIZER
    c["neg_pre_in"] = -1.0 * (row <= col)
    c["neg_suf_in"] = -1.0 * (row >= col)
    c["neg_all"] = -one
    c["m_causal"] = NEG * (col > row)
    c["m_chunk"] = NEG * (col // CHUNK > row // CHUNK)
    c["m_strict"] = NEG * (row >= col)
    c["strict"] = np.concatenate([row < col, one, row < col], 1)
    sel = np.zeros((P, 8 * P))
    for r in range(8):
        sel[r, r * P:(r + 1) * P] = 1.0
    c["sel"] = sel
    c["ge"] = (row <= col)
    c["le"] = (row >= col)
    two = np.zeros((P, 32))
    two[:, 0:2] = 1.0
    c["two"] = two
    order, at, parts = {}, 0, []
    for k, v in c.items():
        v = np.asarray(v, np.float32)
        order[k] = (at, v.shape[1])
        at += v.shape[1]
        parts.append(v)
    return order, np.concatenate(parts, 1)


def level_constants():
    t = np.arange(P)
    row, col = t[:, None], t[None, :]
    sums, pairs = [], []
    for d in range(2):
        for size in (128, 64, 32, 16, 8, 4, 2):
            mid = col // size * size + size // 2
            if d == 0:
                m = np.where(col >= mid, (row >= mid) & (row <= col), (row > col) & (row < mid))
                pair = (row // size == col // size) & (row % size < size // 2) & (col % size >= size // 2)
            else:
                m = np.where(col < mid, (row >= col) & (row < mid), (row >= mid) & (row < col))
                pair = (row // size == col // size) & (row % size >= size // 2) & (col % size < size // 2)
            sums.append(m / NORMALIZER)
            pairs.append(pair)
        sums.append(np.zeros((P, P)))
        pairs.append(row == col)
    return np.concatenate(sums, 1).astype(np.float32), np.concatenate(pairs, 1).astype(np.float32)


CONST_AT, CONST = constants()
LSUM, LPAIR = level_constants()
LEVELS = 8

KB = 1024

GQ, GK, GV, GG, GLR, MQ, MK, MV, MO, MG = 0, 512, 1024, 2048, 3072, 3088, 3600, 4112, 5136, 6160
CTX_COLS = (MK, MV, MV + NBLK, GK, GV, GV + NBLK)
X_COLS = (MQ, MK, MV, MV + NBLK, GQ, GK, GV, GV + NBLK, GG, GG + NBLK, MO, MO + NBLK)
LR = 16
MODS = 24
MODC = 6 * D


class Count:

    def __init__(self, eng, sem):
        self.eng, self.sem, self.n, self.off = eng, sem, 0, 0

    def __call__(self, ins):
        self.n += 1
        ins.then_inc(self.sem, 1)
        self.eng.wait_ge(self.sem, self.n + self.off)

    def iteration(self, first, i):
        self.n, self.off = first, i



def build(nc, a):
    base = (nc.sbuf_base + 31) // 32 * 32

    def at(name, shape, dtype, kb):
        return nc.alloc_sbuf_tensor_at(name, shape, dtype, offset=base + int(kb * KB))

    raw = at("w_raw", [P, SLOTS, UK, NBLK], F32, 0)
    w_hi = at("w_hi", [P, SLOTS, UK, NBLK], F32R, 16)
    w_lo = at("w_lo", [P, SLOTS, UK, NBLK], F32R, 32)
    a_hi = at("a_hi", [P, KC, T], F32R, 48)
    a_lo = at("a_lo", [P, KC, T], F32R, 64)
    cst = at("cst", [P, CONST.shape[1]], F32, 80)
    cs = at("cs", [P, KC, 32], F32, 93.5)
    mrow = at("mrow", [P, NBLK], F32, 95.5)
    x_sb = at("x_sb", [P, RT, D], F32, 97.5)
    mraw = at("mraw", [P, SLOTS, UK, NBLK], F32, 97.5)
    xn = at("xn", [P, RT, D], F32, 113.5)
    br = [at(f"br{i}", [P, RT, 4 * BW], F32, 129.5 + 16 * i) for i in range(2)]
    ys_hi = at("ys_hi", [P, NBR * HEADS, T], F32R, 161.5)
    ys_lo = at("ys_lo", [P, NBR * HEADS, T], F32R, 173.5)
    brow = at("brow", [P, 2, NBLK], F32, 185.5)
    relb = at("relb", [P, HEADS, T], F32, 189.5)
    tmpT = at("tmpT", [P, 2, UK, T], F32, 193.5)
    sg = at("sg", [P, RT, NBLK], F32, 193.5)
    qkn = at("qkn", [P, RT, 2, HD], F32, 193.5)
    qkgT = at("qkgT", [P, 3, T], F32, 195.5)
    probs = at("probs", [P, RT, T], F32, 198.5)
    zwork = at("zwork", [P, 2, 3 * P], F32, 198.5)
    probsT = at("probsT", [P, 3 * P], F32, 201.5)
    yT = at("yT", [P, T], F32, 203)
    cneg = at("cneg", [P, T], F32, 205)
    wf = at("wf", [P, KC, HEADS], F32, 206)
    fl = at("fl", [P, 8, 8], F32, 206.25)
    gbias = at("gbias", [P, 1], F32, 206.5)
    stat = at("stat", [P, 64], F32, 206.625)
    vec = at("vec", [P, 160], F32, 207)
    merged = br[0]
    vrows = sg[:, 0, 0:P]
    rel_ext = probs[0:HEADS].rearrange('p a b -> p (a b)')[:, 0:384]
    rrows = sg[:, 1, 0:512]

    BF16 = mybir.dt.bfloat16
    ctx_sb = at("ctx_sb", [P, RT, D], F32, 129.5)
    mvr = at("mvr", [P, 2, P], F32, 153.5)
    xres = at("xres", [P, RT, D], F32, 161.5)
    wsm = at("wsm", [P, KC, 2 * LR], F32, 185.5)
    y = xn
    cm = at("cm", [P, RT, 3 * NBLK], F32, 129.5)
    cg = at("cg", [P, RT, 3 * NBLK], F32, 141.5)
    xm = at("xm", [P, RT, 4 * NBLK], F32, 153.5)
    xg = at("xg", [P, RT, 4 * NBLK], F32, 169.5)
    la = at("la", [P, RT, 2, NBLK], F32, 189.5)
    glrT = at("glrT", [32, 2 * T], F32, 169.5)
    spd = at("spd", [P, 2, NBLK], F32, 171.5)
    kexp = [at("kexp0", [P, NBLK], F32, 175.5), at("kexp1", [P, NBLK], F32, 181.5)]
    wlr = at("wlr", [32, 2, NBLK], F32, 177.5)
    mrows = at("mrows", [8, 2, T], F32, 185.5)
    grows = at("grows", [8, 2 * T], F32, 198.5)
    mqT = at("mqT", [P, T], F32, 197.5)
    mkT = at("mkT", [P, 2 * T], F32, 198.5)
    mpT = at("mpT", [P, 7 * P], F32, 200.5)
    sm = at("sm", [P, 4, 2 * LR], F32, 204)
    sx = at("sx", [P, 12, 32], F32, 204.5)
    gates = at("gates", [P, RT, D], F32, 153.5)
    state = at("state", [P, 2, HEADS, GDV], F32, 129.5)
    gqT = at("gqT", [P, 2, T], F32, 137.5)
    cr = at("cr", [P, RT, P], F32, 139.5)
    fq = at("fq", [P, 2, P], F32, 140.5)
    lsum = at("lsum", [P, 2, LEVELS, P], F32, 141.5)
    lpair = at("lpair", [P, 2, LEVELS, P], BF16, 149.5)
    masked = at("masked", [P, 4, P], F32, 185.5)
    ek = at("ek", [P, 2, 4, P], F32, 197.5)
    rk = at("rk", [P, 4, P], F32, 201.5)
    sc = at("sc", [P, 3, P], F32, 203.5)
    gtb = at("gtb", [P, D], F32, 129.5)
    gtr = at("gtr", [4, D], F32, 137.5)
    tmp_dn = at("tmp_dn", [P, RT, NBLK], F32, 191.5)
    ft_hi = at("ft_hi", [P, FCH, T], F32R, 97.5)
    ft_lo = at("ft_lo", [P, FCH, T], F32R, 140.5)
    ub = at("ub", [P, 2, RT, NBLK], F32, 183.5)
    gp = at("gp", [P, 2, 6, 66], F32, 191.5)
    acc = at("acc", [P, 2, T], F32, 194.75)
    sil = at("sil", [P, 2, T], F32, 196.75)
    fv = at("fv", [P, 2, T], F32, 198.75)
    cw = at("cw", [P, 10 * FCH], F32, 200.75)
    cwr = at("cwr", [P, 4, P], F32, 202.5)
    x2_sb = at("x2_sb", [P, RT, D], F32, 48)
    squares = at("squares", [P, RT, D], F32, 97.5)
    gt2b = at("gt2b", [P, D], F32, 64)
    gfin = at("gfin", [P, D], F32, 72)
    gtr2 = at("gtr2", [4, D], F32, 183.5)

    def C(name, rows=P, lo=0, n=None):
        s, width = CONST_AT[name]
        return cst[0:rows, s + lo:s + lo + (width if n is None else n)]

    gemm_ps = nc.alloc_psum_tensor("gemm_ps", [P, 2, RT, NBLK], F32)
    ps = nc.alloc_psum_tensor("ps", [P, 4, NBLK], F32)
    pA, pB, pC, pD = (ps[:, i] for i in range(4))
    ident = C("ident")

    x1_d = nc.dram_tensor("x1_d", [T, D], F32, kind="Internal").ap().rearrange("(r p) d -> p r d", p=P)
    x2_d = nc.dram_tensor("x2_d", [T, D], F32, kind="Internal").ap().rearrange("(r p) d -> p r d", p=P)
    mod_d = nc.dram_tensor("mod_d", [4, 2, MODC], F32, kind="Internal").ap()
    out_v = a["out"].rearrange("o (r p) d -> p (o r) d", p=P)
    ext_d = nc.dram_tensor("ext_d", [HEADS, 384], F32, kind="Internal").ap()

    sems = {}

    def S(name):
        if name not in sems:
            sems[name] = nc.alloc_semaphore(name)
        return sems[name]

    raw_in = [S(f"raw_in{i}") for i in range(SLOTS)]
    brow_in = S("brow_in")
    mod_in = [S(f"mod_in{i}") for i in range(SLOTS)]
    mod_used, mod_evac, mod_out = S("mod_used"), S("mod_evac"), S("mod_out")
    tr_use = {"x": 0, "merged": 1, "ctx": 2, "x1": 3, "y": 4, "x2": 5}
    TR = lambda use: BU * (tr_use[use] + 1)
    hi_done, lo_done, used = S("hi_done"), S("lo_done"), S("used")
    evac_act, evac_dve = S("evac_act"), S("evac_dve")

    w_in = a["w_in"].rearrange("o (j p) c -> p (o j) c", p=P)
    w_up = a["w_up"].rearrange("o n (j p) c -> p (o n j) c", p=P)
    w_out = a["w_out"].rearrange("o (j p) c -> p (o j) c", p=P)
    w_mod = a["w_mod_2"].rearrange("o (j p) c -> p (o j) c", p=P)
    w_in2 = a["w_in_2"].rearrange("o (j p) c -> p (o j) c", p=P)
    w_out2 = a["w_out_2"].rearrange("o (j p) c -> p (o j) c", p=P)
    w_up2 = a["w_up_2"].rearrange("o (j p) (s c) -> p (o j) s c", p=P, s=2)
    w_dn = a["w_down_2"].rearrange("o (j p) c -> p (o j) c", p=P)
    xv = a["x"].rearrange("o (r p) d -> p (o r) d", p=P)
    QKVG_COLS = NBR * 4 * BW
    GATE0 = QKVG_COLS + HEADS

    block = nc.Block()
    block.__enter__()

    @block.sync
    def _(sp):
        def unit(q, slot, src):
            if not (isinstance(q, int) and q == 0):
                sp.wait_ge(lo_done, 4 * q + slot + 1 - SLOTS)
            sp.dma_start(raw[:, slot, 0:src.shape[1], 0:src.shape[2]], src).then_inc(raw_in[slot], 16)

        def mod_unit(m, i):
            q = 2 * m + i // SLOTS
            if i == 0:
                if not (isinstance(m, int) and m == 0):
                    sp.wait_ge(mod_used, BU * (m - 1) + 1)
                sp.dma_start(brow[0:1, 1], a["b_mod_2"][:, bass.ds(m * NBLK, NBLK)]).then_inc(S("bmod_in"), 16)
            if not (isinstance(m, int) and 2 * m + i // SLOTS == 0):
                sp.wait_ge(mod_used, BU * m + i + 1 - SLOTS)
            sp.dma_start(mraw[:, i % SLOTS], w_mod[:, UK * i:UK * i + UK, bass.ds(m * NBLK, NBLK)]).then_inc(mod_in[i % SLOTS], 16)

        def units(w, q, col, first=0, count=BU, row=0, mod=None):
            for i in range(count):
                s = first + i
                unit(q + s // SLOTS, s % SLOTS, w[:, row + UK * i:row + UK * i + UK, bass.ds(col, NBLK)])
                if mod:
                    mod(i)

        def every_other(m, half):
            return lambda i: mod_unit(m, 4 * half + i // 2) if i % 2 else None

        sp.dma_start(x_sb[:], xv).then_inc(S("x_in"), 16)
        sp.dma_start(cst[:, :], a["const"]).then_inc(S("const_in"), 16)
        for i, name in enumerate(("norm_g", "g_norm1_2", "g_norm2_2")):
            sp.dma_start(vrows[16 * i:16 * i + 16, :], a[name].rearrange("o (j p) -> (o j) p", p=P)).then_inc(S("vec_in"), 16)
        sp.dma_start(vrows[48:52, :], a["qk_norm_g"].rearrange("o g p -> (o g) p")).then_inc(S("vec_in"), 16)
        sp.dma_start(vrows[52:54, :], a["gla_g_norm_2"].rearrange("o (j p) -> (o j) p", p=P)).then_inc(S("vec_in"), 16)
        sp.dma_start(vrows[54:56, :], a["mlstm_g_norm_2"].rearrange("o (j p) -> (o j) p", p=P)).then_inc(S("vec_in"), 16)
        sp.dma_start(vrows[56:72, :], a["c_2"].rearrange("o (j p) -> (o j) p", p=P)).then_inc(S("vec_in"), 16)
        sp.dma_start(vrows[72:88, :], a["c_ctx_2"].rearrange("(j p) -> j p", p=P)).then_inc(S("vec_in"), 16)
        sp.dma_start(rrows[0:HEADS, 0:2 * MAX_REL + 1], a["rel_bias"].rearrange("o h m -> (o h) m")).then_inc(S("vec_in"), 16)
        units(w_in, 0, 0)
        sp.dma_start(fl[:, 0, 0:HEADS], a["b_f"][0].partition_broadcast(P)).then_inc(S("wf_in"), 16)
        sp.dma_start(wf[:], w_in[:, :, QKVG_COLS:GATE0]).then_inc(S("wf_in"), 16)
        sp.wait_ge(S("rel_ext"), 1)
        sp.dma_start(ext_d, rel_ext).then_inc(S("rel_out"), 16)
        sp.wait_ge(S("n_xn"), 2)
        for i in range(4):
            mod_unit(0, i)
        units(w_in, 2, NBLK, mod=every_other(0, 1))
        sp.wait_ge(S("rel_out"), 16)
        diagonals = bass.AP(tensor=ext_d.tensor, offset=1, ap=[[1, P], [384, HEADS], [1, T]])
        sp.dma_start(relb[:], diagonals).then_inc(S("rel_in"), 16)
        for b in range(2, 12):
            units(w_in, 2 * b, b * NBLK, mod=every_other(b // 2, b % 2))
        bg = a["b_gate"]
        for g in range(DC):
            if g:
                sp.wait_ge(used, U_GATE0 + BU * (g - 1) + 1)
            sp.dma_start(brow[0:1, 0], bg[:, g * NBLK:(g + 1) * NBLK]).then_inc(brow_in, 16)
            b = 12 + g
            units(w_in, 2 * b, GATE0 + g * NBLK, mod=every_other(b // 2, b % 2))
        for c in range(DC):
            s = UPU * c
            units(w_up, U_UP0 // SLOTS + s // SLOTS, c * NBLK, s % SLOTS, UPU)
        with sp.Fori(0, DC) as c:
            for j in range(2):
                sp.wait_ge(used, U_PAIRS + 2 * PAIR * c + (1 if j else 1 - PAIR))
                sp.dma_start(brow[0:1, 0], bg[:, bass.ds((j + 1) * D + c * NBLK, NBLK)]).then_inc(brow_in, 16)
                q = U_PAIRS // SLOTS + 2 * PAIR // SLOTS * c
                units(w_in, q, GATE0 + (j + 1) * D + c * NBLK, PAIR * j, mod=every_other(8 + c, j))
                units(w_up, q, c * NBLK, PAIR * j + BU, UPU, row=4 * (j + 1))
        with sp.Fori(0, DC) as c:
            units(w_out, U_OUT // SLOTS + 2 * c, c * NBLK)
        for i, col in enumerate(CTX_COLS):
            units(w_in2, U_CTX // SLOTS + 2 * i, col, mod=lambda u: mod_unit(12 + i, u))
        for i, col in enumerate(X_COLS):
            units(w_in2, U_X // SLOTS + 2 * i, col, mod=every_other(18 + i // 2, i % 2) if i < 4 else None)
        with sp.Fori(0, DC) as c:
            units(w_out2, U_OUT2 // SLOTS + 2 * c, c * NBLK, mod=lambda u: mod_unit(20 + c, u))

        def ffn_units(q, f, n):
            for i in range(BU):
                slot = i % SLOTS
                sp.wait_ge(lo_done, 4 * q + i + 1 - SLOTS)
                dst = raw[:, slot, :, 0:2 * n].rearrange("p k (s c) -> p k s c", s=2)
                for s in range(2):
                    sp.dma_start(dst[:, :, s], w_up2[:, UK * i:UK * i + UK, s, bass.ds(f, n)]).then_inc(raw_in[slot], 16)

        with sp.Fori(0, FB - 1) as i:
            ffn_units(U_FFN // SLOTS + 2 * i, T * i, T)
        ffn_units(U_FFN // SLOTS + 2 * (FB - 1), T * (FB - 1), P)
        with sp.Fori(0, DC // 2) as i:
            for k in range(2):
                for u in range(DU):
                    s = DU * k + u
                    q = U_DOWN // SLOTS + 2 * DU // SLOTS * i + s // SLOTS
                    rows = w_dn[:, UK * u:min(UK * u + UK, FCH), bass.ds((2 * i + k) * NBLK, NBLK)]
                    unit(q, s % SLOTS, rows)
        sp.wait_ge(S("out_done"), 2)
        sp.dma_start(out_v, x2_sb[:]).then_inc(S("out_in"), 16)
        sp.wait_ge(S("out_in"), 16)

    @block.gpsimd
    def _(pool):
        def mod_store(lo, hi):
            with pool.Fori(lo, hi) as m:
                pool.wait_ge(mod_evac, m + 1)
                for g in range(4):
                    pool.dma_start(mod_d[g, :, bass.ds(m * NBLK, NBLK)], mrow[32 * g:32 * g + 2, :]).then_inc(mod_out, 16)
                pool.wait_ge(mod_out, 64 * (m + 1))

        mod_store(0, 12)
        pool.wait_ge(evac_dve, 12)
        pool.dma_start(xres[:], xv).then_inc(S("xres_in"), 16)
        for r in range(2):
            for v in range(2):
                for g in range(4):
                    at_row = 64 * v + 16 * g
                    pool.dma_start(mvr[at_row:at_row + 16, r], mod_d[g, r, v * D:(v + 1) * D].rearrange("(j p) -> j p", p=P)).then_inc(S("mvr_in"), 16)
        pool.wait_ge(S("tr_ps"), TR("merged"))
        pool.dma_start(ctx_sb[:], a["ctx_2"].rearrange("o (r p) d -> p (o r) d", p=P)).then_inc(S("ctx_in"), 16)
        pool.dma_start(wsm[:, :, 0:LR], w_in2[:, :, GLR:GLR + LR]).then_inc(S("wsm_in"), 16)
        pool.dma_start(wsm[:, :, LR:2 * LR], w_in2[:, :, MG:MG + LR]).then_inc(S("wsm_in"), 16)
        pool.dma_start(sx[:, 11, 0:LR], a["mlstm_b_gate_2"].rearrange("o d g h -> o (d g h)")[0].partition_broadcast(P)).then_inc(S("wsm_in"), 16)
        pool.dma_start(wlr[0:LR], a["gla_w_lr_2"].rearrange("o d r k -> r (o d) k")).then_inc(S("wlr_in"), 16)
        pool.dma_start(wlr[LR:LR + 1], a["gla_b_lr_2"]).then_inc(S("wlr_in"), 16)
        pool.wait_ge(evac_dve, 16)
        pool.dma_start(x1_d, xres[:]).then_inc(S("x1_out"), 16)
        mod_store(12, 20)
        pool.wait_ge(S("g_state"), 2)
        pool.dma_start(lsum[:], a["lsum"].rearrange("p (d l t) -> p d l t", d=2, l=LEVELS)).then_inc(S("lsum_in"), 16)
        pool.dma_start(lpair[:], a["lpair"].rearrange("p (d l t) -> p d l t", d=2, l=LEVELS)).then_inc(S("lsum_in"), 16)
        pool.wait_ge(S("y_done"), 1)
        pool.wait_ge(S("x1_out"), 16)
        pool.dma_start(gtr[:], mod_d[:, 0, 2 * D:3 * D]).then_inc(S("gtr_in"), 16)
        pool.dma_start(xres[:], x1_d).then_inc(S("xres_in2"), 16)
        for v in range(2):
            for g in range(4):
                at_row = 64 * v + 16 * g
                pool.dma_start(mvr[at_row:at_row + 16, 0], mod_d[g, 0, (3 + v) * D:(4 + v) * D].rearrange("(j p) -> j p", p=P)).then_inc(S("mvr_in2"), 16)
        wrows = a["conv_w_2"].rearrange("o y x (f p) -> (o y x f) p", p=P)
        n = 9 * FCH
        for t in range(4):
            k = min(P, n - P * t)
            pool.dma_start(cwr[0:k, t], wrows[P * t:P * t + k, :]).then_inc(S("cw_in"), 16)
        pool.dma_start(cwr[n - 3 * P:n - 3 * P + FCH, 3], a["conv_b_2"].rearrange("o (f p) -> (o f) p", p=P)).then_inc(S("cw_in"), 16)
        mod_store(20, 24)
        pool.wait_ge(evac_dve, 20)
        pool.dma_start(x2_d, xres[:]).then_inc(S("x2_out"), 16)
        pool.wait_ge(S("x2_out"), 16)
        pool.wait_ge(used, U_DOWN)
        pool.dma_start(x2_sb[:], x2_d).then_inc(S("x2_in"), 16)
        pool.dma_start(gfin[:], a["g_final_2"].partition_broadcast(P)).then_inc(S("x2_in"), 16)
        pool.wait_ge(S("f_fv"), FB)
        pool.dma_start(gtr2[:], mod_d[:, 0, 5 * D:6 * D]).then_inc(S("gtr2_in"), 16)

    @block.scalar
    def _(act):
        me = Count(act, S("act_own"))

        def arrived(q):
            if isinstance(q, int) and q < U_FFN // SLOTS:
                return 16 * (q + 1)
            if isinstance(q, int) and q >= U_DOWN // SLOTS:
                return 16 * (q + 1) + 4 * (U_DOWN - U_FFN)
            return 16 * (q + 1) + 16 * (q + 1 - U_FFN // SLOTS) if isinstance(q, int) or in_ffn[0] else 16 * (q + 1)

        in_ffn = [False]

        def split(q, slot):
            act.wait_ge(raw_in[slot], arrived(q))
            if not (isinstance(q, int) and q == 0):
                act.wait_ge(used, 4 * q + slot + 1 - SLOTS)
            act.activation(w_hi[:, slot], raw[:, slot], ACT.Copy).then_inc(hi_done, 1)

        def splits(q, lo, hi):
            for i in range(lo, hi):
                split(q + i // SLOTS, i % SLOTS)

        def exp_ln_rsqrt(ss, n, mean_of, out):
            me(act.activation(out, ss, ACT.Ln, scale=1.0 / mean_of, bias=gbias[:, 0:1]))
            return act.activation(out, out, ACT.Exp, scale=-0.5)

        def to_act(use, count=BU):
            for g in range(count):
                G = BU * tr_use[use] + g
                act.wait_ge(S("tr_val"), G + 1)
                act.activation(a_hi[:, UK * g:UK * g + UK], tmpT[:, g % 2], ACT.Copy).then_inc(S("tr_hi"), 1)

        def head(r, h, i):
            hh = HEADS * r + h
            src = br[r % 2]
            if i == 3:
                if r < 2:
                    act.wait_ge(S("h_ss"), 4 * r + h + 1)
                    exp_ln_rsqrt(stat[:, 0:4], 4, HD, stat[:, 4:8]).then_inc(S("h_rs"), 1)
            if i == 5:
                act.wait_ge(S("h_T"), hh + 1)
                qs = vec[:, 52 + 2 * r:53 + 2 * r] if r < 2 else SCALE
                ks = vec[:, 53 + 2 * r:54 + 2 * r] if r < 2 else 1.0
                act.activation(qkgT[:, 0], pA[:, 0:T], ACT.Copy if r == 2 else ACT.Identity, scale=qs)
                act.activation(qkgT[:, 1], pA[:, T:2 * T], ACT.Copy if r == 2 else ACT.Identity,
                               scale=ks).then_inc(S("h_qkT"), 1)
            if i == 6:
                if r < 2:
                    act.wait_ge(S("h_mx"), 4 * r + h + 1)
                    for rt in range(RT):
                        n = P * (rt + 1)
                        ins = act.activation(probs[:, rt, 0:n], pC[:, rt * T:rt * T + n], ACT.Exp,
                                             bias=stat[:, 16 + rt:17 + rt], accum_out=stat[:, 20 + rt:21 + rt])
                    ins.then_inc(S("h_exp"), 1)
                else:
                    act.wait_ge(S("h_L"), hh + 1)
                    me(act.activation(zwork[:, 0], pC[:, 0:3 * P], ACT.Abs))
                    me(act.activation(zwork[:, 0], zwork[:, 0], ACT.Exp, scale=-1.0))
                    act.activation(zwork[:, 0], zwork[:, 0], ACT.Ln, bias=1.0).then_inc(S("h_sp"), 1)
            if i == 8 and r == 2:
                act.wait_ge(S("h_R"), h + 1)
                act.activation(probsT[:, :], pC[:, 0:3 * P], ACT.Exp).then_inc(S("h_PTs"), 1)
            if i == 9:
                act.wait_ge(S("h_y"), hh + 1)
                act.activation(ys_hi[:, hh], yT[:, :], ACT.Copy).then_inc(S("h_yhi"), 1)

        splits(0, 0, 2)
        act.wait_ge(S("x_in"), 16)
        act.wait_ge(S("eps_set"), 1)
        for rt in range(RT):
            act.activation(xn[:, rt], x_sb[:, rt], ACT.Square, accum_out=stat[:, 32 + rt:33 + rt])
        exp_ln_rsqrt_in = stat[:, 32:34]
        me(act.activation(stat[:, 40:41], gbias[:, 0:1], ACT.Copy))
        exp_ln_rsqrt(exp_ln_rsqrt_in, 2, D, stat[:, 34:36]).then_inc(S("n_rs"), 1)
        act.wait_ge(S("cs_zero"), 1)
        for r in range(2):
            ins = act.activation(cs[:, :, r], pC[:, 56 + 16 * r:72 + 16 * r], ACT.Silu)
        ins.then_inc(S("cs_set"), 1)
        to_act("x")

        def plain_block(B, dst, q0, hooks=None):
            for i in range(2, 10):
                splits(q0, i, i + 1)
                if hooks:
                    hooks(i)

        for seg in range(4):
            for b in range(4):
                B = 4 * seg + b
                plain_block(B, None, 2 * B, None if seg == 0 else lambda i: head(seg - 1, b, i))
                act.wait_ge(used, BU * (B + 1))
                if seg < 3:
                    act.activation(br[seg % 2][:, :, b * BW:(b + 1) * BW], gemm_ps[:, B % 2],
                                   ACT.Silu if b == 3 else ACT.Copy).then_inc(evac_act, 1)
                else:
                    act.activation(xn[:, :, b * NBLK:(b + 1) * NBLK], gemm_ps[:, B % 2],
                                   ACT.Sigmoid).then_inc(evac_act, 1)
                if B == 3:
                    act.wait_ge(S("f_val"), 1)
                    me(act.activation(fl[:, 3:5, 0:HEADS], fl[:, 1:3, 0:HEADS], ACT.Abs))
                    me(act.activation(fl[:, 3:5, 0:HEADS], fl[:, 3:5, 0:HEADS], ACT.Exp, scale=-1.0))
                    act.activation(fl[:, 3:5, 0:HEADS], fl[:, 3:5, 0:HEADS], ACT.Ln, bias=1.0).then_inc(S("f_sp"), 1)
        splits(U_UP0 // SLOTS, 2, UPU * DC + 2)
        with act.Fori(0, DC) as c:
            q = U_PAIRS // SLOTS + 2 * PAIR // SLOTS * c
            for j in range(2):
                splits(q, PAIR * j + 2, PAIR * j + BU + 2)
                act.wait_ge(used, U_PAIRS + 2 * PAIR * c + PAIR * j + BU)
                act.wait_ge(evac_dve, DC + 2 * c + j)
                act.activation(sg[:], gemm_ps[:, 0], ACT.Sigmoid).then_inc(evac_act, 1)
                splits(q, PAIR * j + BU + 2, PAIR * j + PAIR + 2)
        to_act("merged")
        def sums(src, junk):
            for rt in range(RT):
                act.activation(junk[rt], src[:, rt], ACT.Square, accum_out=stat[:, 32 + rt:33 + rt])
            me(act.activation(stat[:, 40:41], gbias[:, 0:1], ACT.Copy))
            exp_ln_rsqrt(stat[:, 32:34], 2, D, stat[:, 34:36]).then_inc(S("n_rs"), 1)

        def log_sigmoid_part(out, src):
            me(act.activation(out, src, ACT.Abs))
            me(act.activation(out, out, ACT.Exp, scale=-1.0))
            return act.activation(out, out, ACT.Ln, bias=1.0)

        for half in range(2):
            with act.Fori(DC // 2 * half, DC // 2 * (half + 1)) as c:
                splits(U_OUT // SLOTS + 2 * c, 2, 10)
            if half == 0:
                act.wait_ge(S("ctx_in"), 16)
                act.wait_ge(evac_dve, 12)
                sums(ctx_sb, [xn[:, rt] for rt in range(RT)])
        to_act("ctx")
        for cb in range(6):
            for i in range(2, 10):
                splits(U_CTX // SLOTS + 2 * cb, i, i + 1)
                if cb == 0 and i == 3:
                    act.wait_ge(evac_dve, 16)
                    act.wait_ge(S("tr_ps"), TR("ctx"))
                    sums(xres, [xn[:, rt] for rt in range(RT)])
            act.wait_ge(used, U_CTX + BU * (cb + 1))
            act.wait_ge(S("n_xn"), 4)
            dst = cm if cb < 3 else cg
            act.activation(dst[:, :, cb % 3 * NBLK:(cb % 3 + 1) * NBLK], gemm_ps[:, (B_CTX + cb) % 2], ACT.Copy).then_inc(evac_act, 1)
        to_act("x1")

        fv8 = lambda t: t.rearrange("p a b -> p (a b)")
        pre = fv8(sx[:, 0:2]).rearrange("p (t d g h) -> p t d g h", t=4, d=2, g=2)
        sp8 = sx[:, 2].rearrange("p (t d h) -> p t d h", t=4, d=2)

        def step(s):
            if s == 11:
                act.wait_ge(S("m_pre"), 1)
                for d in range(2):
                    ins = act.activation(sp8[:, :, d], pre[:, :, d, 1], ACT.Abs)
                me(ins)
                me(act.activation(sx[:, 2], sx[:, 2], ACT.Exp, scale=-1.0))
                act.activation(sx[:, 2], sx[:, 2], ACT.Ln, bias=1.0).then_inc(S("m_sp"), 1)
            if s == 18:
                act.wait_ge(S("m_FM"), 1)
                act.activation(sx[:, 6, 0:16], sx[:, 5, 0:16], ACT.Exp, scale=-1.0).then_inc(S("m_em"), 1)
            if 20 <= s < 28:
                n = s - 20
                act.wait_ge(S("g_dec"), n + 1)
                if n >= 2:
                    act.wait_ge(S("g_la"), n - 1)
                log_sigmoid_part(spd[:, n % 2], ps[:, n % 2]).then_inc(S("g_sp"), 1)
            if 28 <= s < 32:
                m = s - 28
                act.wait_ge(S("g_w"), m + 1)
                if m >= 2:
                    act.wait_ge(S("g_kend"), m - 1)
                act.activation(kexp[m % 2][:, :], (pC, pA)[m % 2], ACT.Exp).then_inc(S("g_kexp"), 1)
            if 34 <= s < 66:
                h, i = (s - 34) // 8, (s - 34) % 8 + 2
                if i == 2:
                    act.wait_ge(S("m_T"), h + 1)
                    act.activation(mkT[:, :], pA, ACT.Copy, scale=SCALE).then_inc(S("m_kT"), 1)
                if i in (5, 7):
                    act.wait_ge(S("m_arg"), 2 * h + (i == 7) + 1)
                    act.activation(mpT[:, :], mpT[:, :], ACT.Exp, scale=-1.0).then_inc(S("m_exp"), 1)
                if i == 9:
                    act.wait_ge(S("m_num"), 2 * h + 2)
                    act.activation(sx[:, 7, 0:4], pC[:, 0:4], ACT.Abs).then_inc(S("m_den"), 1)
            if s == 66:
                act.wait_ge(S("g_S"), 1)
                act.activation(state[:, 0].rearrange("p h v -> p (h v)"), ps[:, 0:2].rearrange("p a b -> p (a b)"),
                               ACT.Copy).then_inc(S("g_state"), 1)
            if 68 <= s <= 100:
                gla_consume(s - 68)
            if s >= 77 and (s - 77) % 8 == 0:
                h = (s - 77) // 8
                act.wait_ge(S("g_o"), 4 * h + 4)
                act.activation(y[:, :, h * GDV:(h + 1) * GDV], pD.rearrange("p (r v) -> p r v", r=RT),
                               ACT.Copy).then_inc(S("g_y"), 1)

        turn = [0]

        def take():
            act.wait_ge(S("g_ps"), turn[0] + 1)
            turn[0] += 1
            return ps[:, (turn[0] - 1) % 2]

        def gla_consume(k):
            gc, j = k // 2, k % 2
            h, c = gc // 4, gc % 4
            if j == 0 and gc and c % 2 == 0:
                act.activation(sc[:, 2], take()[:, 0:P], ACT.Copy).then_inc(S("g_free"), 1)
            if k == 32:
                return
            if j == 0 and c == 0:
                bank = take()
                if h:
                    act.wait_ge(S("g_mult"), 8 * h)
                act.activation(gqT[:, 0], bank[:, 0:T], ACT.Copy, scale=SCALE)
                act.activation(gqT[:, 1], bank[:, T:2 * T], ACT.Copy).then_inc(S("g_free"), 1)
            if j == 0:
                bank = take()
                if gc >= 2:
                    act.wait_ge(S("g_o"), gc - 1)
                act.activation(cr[:, c % 2], bank[:, 0:P], ACT.Exp)
                act.activation(fq[:, gc % 2], bank[:, P:2 * P], ACT.Exp).then_inc(S("g_free"), 1)
            bank = take()
            if k >= 2:
                act.wait_ge(S("g_sc"), k - 1)
            act.activation(ek[:, k % 2].rearrange("p l t -> p (l t)"), bank, ACT.Exp).then_inc(S("g_free"), 1)

        for xb in range(12):
            for i in range(2, 10):
                splits(U_X // SLOTS + 2 * xb, i, i + 1)
                step(8 * xb + i)
            act.wait_ge(used, U_X + BU * (xb + 1))
            dst = (xm, xg, gates)[xb // 4][:, :, xb % 4 * NBLK:(xb % 4 + 1) * NBLK]
            if xb == 0:
                act.wait_ge(S("x1_out"), 16)
            act.activation(dst, gemm_ps[:, (B_X + xb) % 2],
                           ACT.Copy if xb < 8 else ACT.Silu if xb < 10 else ACT.Sigmoid).then_inc(evac_act, 1)
        for s in range(98, 103):
            step(s)
        act.wait_ge(S("m_y"), HEADS)
        me(act.activation(stat[:, 40:41], gbias[:, 0:1], ACT.Copy))
        for rt in range(RT):
            for g in range(8):
                act.activation(xg[:, rt, g * GDV:(g + 1) * GDV], y[:, rt, g * GDV:(g + 1) * GDV], ACT.Square, accum_out=sx[:, 8, 8 * rt + g:8 * rt + g + 1])
        me(act.activation(stat[:, 40:41], gbias[:, 0:1], ACT.Copy))
        exp_ln_rsqrt(sx[:, 8, 0:16], 16, GDV, sx[:, 9, 0:16]).then_inc(S("y_rs"), 1)
        to_act("y")
        act.wait_ge(S("gt_ps"), 1)
        act.activation(gtb[:, :], ps[:].rearrange("p a b -> p (a b)"), ACT.Copy, scale=-1.0).then_inc(S("gt_in"), 1)
        with act.Fori(0, DC - 1) as c:
            splits(U_OUT2 // SLOTS + 2 * c, 2, 10)
        splits(U_OUT2 // SLOTS + 2 * (DC - 1), 2, 10)
        act.wait_ge(evac_dve, 20)
        sums(xres, [xn[:, rt] for rt in range(RT)])
        to_act("x2")

        def ffn_hook(b, i, par, start, finish, nf=2):
            if i == 3 and finish:
                act.wait_ge(S("f_acc"), b - 1)
                act.activation(sil[:, 0:finish], acc[:, 0:finish], ACT.Silu).then_inc(S("f_sil"), 1)
            if i == 5 and finish:
                act.wait_ge(S("f_fv"), b - 1)
                act.activation(ft_hi[:, bass.ds((b - 2) * 2, finish)], fv[:, 0:finish], ACT.Copy).then_inc(S("f_hi"), 1)
            if i == 6 and start:
                act.wait_ge(S("f_T"), b)
                src = pA[:, 0:start * T].rearrange("p (f y x) -> p f y x", f=start, y=4)
                for f in range(start):
                    ins = act.activation(gp[:, f, 1:5, 1:65], src[:, f], ACT.Copy)
                me(ins)
                for f in range(start):
                    fc = (b - 1) * 2 + f
                    ins = act.activation(acc[:, f].rearrange("p (y x) -> p y x", y=4), gp[:, f, 0:4, 0:64], ACT.Identity,
                                         scale=cw[:, bass.ds(fc, 1)], bias=cw[:, bass.ds(9 * FCH + fc, 1)])
                ins.then_inc(S("f_tap0"), 1)

        def ffn_block(b, par, start=2, finish=2, k0=0):
            for i in range(2, 10):
                splits(U_FFN // SLOTS + 2 * b, i, i + 1)
                ffn_hook(b, i, par, start, finish)
            act.wait_ge(used, U_FFN + BU * (b + 1))
            if start:
                act.wait_ge(S("f_T"), b)
            act.activation(ub[:, par], gemm_ps[:, par], ACT.Copy).then_inc(evac_act, 1)

        act.wait_ge(S("gp_zero"), 1)
        ffn_block(0, 0, 0, 0)
        ffn_block(1, 1, 2, 0)
        first = me.n
        in_ffn[0] = True
        with act.Fori(0, 9) as n:
            me.iteration(first, 2 * n)
            for k in range(2):
                ffn_block(2 * n + 2 + k, k)
        me.iteration(first + 18, 0)
        ffn_block(20, 0)
        ffn_block(21, 1)
        for i in range(2, 10):
            splits(U_DOWN // SLOTS, i, i + 1)
            ffn_hook(22, i, 0, 1, 2)
        for i in range(2, 10):
            splits(U_DOWN // SLOTS + 2, i, i + 1)
            ffn_hook(23, i, 1, 0, 1)
        splits(U_DOWN // SLOTS, 18, DU + 2)
        act.wait_ge(S("gt_ps"), 2)
        act.activation(gt2b[:, :], ps[:].rearrange("p a b -> p (a b)"), ACT.Copy, scale=-1.0).then_inc(S("gt_in"), 1)
        splits(U_DOWN // SLOTS, DU + 2, DC * DU)
        act.wait_ge(evac_dve, 24)
        sums(x2_sb, [squares[:, rt] for rt in range(RT)])

    @block.vector
    def _(dve):
        me = Count(dve, S("dve_own"))

        def split(q, slot):
            dve.wait_ge(hi_done, 4 * q + slot + 1)
            dve.tensor_tensor(w_lo[:, slot], raw[:, slot], w_hi[:, slot].bitcast(F32), ALU.subtract).then_inc(lo_done, 1)

        def splits(q, lo, hi):
            for i in range(lo, hi):
                split(q + i // SLOTS, i % SLOTS)

        def newton(ss, r, mean_of, t):
            me(dve.tensor_scalar(t, ss, 1.0 / mean_of, EPS, ALU.mult, ALU.add))
            me(dve.tensor_tensor(t, t, r, ALU.mult))
            me(dve.tensor_tensor(t, t, r, ALU.mult))
            me(dve.tensor_scalar(t, t, -0.5, 1.5, ALU.mult, ALU.add))
            me(dve.tensor_tensor(r, r, t, ALU.mult))

        def to_act(use, scale=None, bias=None):
            for g in range(BU):
                G = BU * tr_use[use] + g
                dve.wait_ge(S("tr_ps"), G + 1)
                if g >= 2:
                    dve.wait_ge(S("tr_hi"), G - 1)
                bank = ps[:, g % 2]
                if scale is None:
                    dve.tensor_copy(tmpT[:, g % 2].rearrange("p a b -> p (a b)"), bank).then_inc(S("tr_val"), 1)
                else:
                    for k in range(UK):
                        kc = UK * g + k
                        b = bias[:, kc:kc + 1] if bias is not None else None
                        ins = dve.tensor_scalar(tmpT[:, g % 2, k], bank[:, k * T:(k + 1) * T], scale[:, kc:kc + 1], b,
                                                ALU.mult, ALU.add if bias is not None else ALU.bypass)
                    ins.then_inc(S("tr_val"), 1)
                dve.wait_ge(S("tr_hi"), G + 1)
                dve.tensor_tensor(a_lo[:, UK * g:UK * g + UK], tmpT[:, g % 2],
                                  a_hi[:, UK * g:UK * g + UK].bitcast(F32), ALU.subtract).then_inc(S("tr_lo"), 1)

        def head(r, h, i):
            hh = HEADS * r + h
            src = br[r % 2]
            qk = src[:, :, 0:2 * BW].rearrange("p r (t c) -> p r t c", t=2)[:, :, :, h * HD:(h + 1) * HD]
            if i == 2:
                if hh == 0:
                    dve.wait_ge(evac_act, 4)
                if h == 0 and r > 0:
                    dve.wait_ge(evac_act, 4 * (r + 1))
                if r < 2:
                    if hh > 0:
                        dve.wait_ge(S("h_T"), hh)
                    for rt in range(RT):
                        ins = dve.tensor_tensor(qkn[:, rt], qk[:, rt], qk[:, rt], ALU.mult)
                    me(ins)
                    dve.tensor_reduce(stat[:, 0:4], qkn[:].rearrange("p r t c -> p (r t) c"), AX_X,
                                      ALU.add).then_inc(S("h_ss"), 1)
            if i == 4:
                if r < 2:
                    dve.wait_ge(S("h_rs"), 4 * r + h + 1)
                    newton(stat[:, 0:4], stat[:, 4:8], HD, stat[:, 8:12])
                    for rt in range(RT):
                        for t in range(2):
                            c = 2 * rt + t
                            ins = dve.tensor_scalar(qkn[:, rt, t], qk[:, rt, t], stat[:, 4 + c:5 + c], None, ALU.mult)
                    ins.then_inc(S("h_pre"), 1)
            if i == 5:
                dve.wait_ge(S("h_T"), hh + 1)
                dve.tensor_copy(qkgT[:, 2], pB[:, 0:T]).then_inc(S("h_gT"), 1)
            if i == 6:
                dve.wait_ge(S("h_L"), hh + 1)
                if r < 2:
                    for rt in range(RT):
                        ins = dve.tensor_reduce(stat[:, 18 + rt:19 + rt], pC[:, rt * T:rt * T + P * (rt + 1)], AX_X, ALU.max)
                    me(ins)
                    dve.tensor_scalar(stat[:, 16:18], stat[:, 18:20], -1.0, None, ALU.mult).then_inc(S("h_mx"), 1)
            if i == 7:
                if r < 2:
                    dve.wait_ge(S("h_exp"), 4 * r + h + 1)
                    me(dve.reciprocal(stat[:, 22:24], stat[:, 20:22]))
                    for rt in range(RT):
                        n = P * (rt + 1)
                        ins = dve.tensor_scalar(probs[:, rt, 0:n], probs[:, rt, 0:n], stat[:, 22 + rt:23 + rt], None, ALU.mult)
                    ins.then_inc(S("h_p"), 1)
                else:
                    dve.wait_ge(S("h_sp"), h + 1)
                    me(dve.scalar_tensor_tensor(out=zwork[:, 1], in0=pC[:, 0:3 * P], scalar=0.0, in1=zwork[:, 0],
                                                op0=ALU.max, op1=ALU.add))
                    dve.tensor_tensor(zwork[:, 1], zwork[:, 1], C("strict"), ALU.mult).then_inc(S("h_p"), 1)
            if i == 8 and r < 2:
                dve.wait_ge(S("h_PT"), 4 * r + h + 1)
                dve.tensor_copy(probsT[:, :], pA[:, 0:3 * P]).then_inc(S("h_PTs"), 1)
            if i == 9:
                dve.wait_ge(S("h_O"), hh + 1)
                if hh > 0:
                    dve.wait_ge(S("h_yhi"), hh)
                dve.tensor_tensor(yT[:, :], pB[:, 0:T], qkgT[:, 2], ALU.mult).then_inc(S("h_y"), 1)
                dve.wait_ge(S("h_yhi"), hh + 1)
                dve.tensor_tensor(ys_lo[:, hh], yT[:, :], ys_hi[:, hh].bitcast(F32), ALU.subtract).then_inc(S("h_ylo"), 1)

        def mod_copy(m):
            dve.wait_ge(mod_used, BU * (m + 1))
            if not (isinstance(m, int) and m == 0):
                dve.wait_ge(mod_out, 64 * m)
            dve.tensor_copy(mrow[:, :], pD).then_inc(mod_evac, 1)

        dve.memset(gbias[:, :], EPS).then_inc(S("eps_set"), 1)
        dve.wait_ge(S("vec_in"), 144)
        N = 2 * MAX_REL + 1
        dve.tensor_copy(rel_ext[:, 0:N], rrows[0:HEADS, 0:N])
        dve.tensor_copy(rel_ext[:, N:384], rrows[0:HEADS, N - 1:N].to_broadcast([HEADS, 384 - N])).then_inc(S("rel_ext"), 1)
        dve.wait_ge(S("n_vecT"), 1)
        me(dve.tensor_copy(vec[:, 0:52], pC[:, 0:52]))
        dve.tensor_copy(vec[:, 56:60], pC[:, 52:56])
        dve.memset(cs[:], 0.0).then_inc(S("cs_zero"), 1)
        for r in range(2):
            dve.tensor_scalar(vec[:, 52 + 2 * r:53 + 2 * r], vec[:, 48 + 2 * r:49 + 2 * r], SCALE, None, ALU.mult)
            me(dve.tensor_copy(vec[:, 53 + 2 * r:54 + 2 * r], vec[:, 49 + 2 * r:50 + 2 * r]))
        dve.wait_ge(S("n_rs"), 1)
        newton(stat[:, 32:34], stat[:, 34:36], D, stat[:, 36:38])
        for rt in range(RT):
            dve.tensor_scalar(xn[:, rt], x_sb[:, rt], stat[:, 34 + rt:35 + rt], None, ALU.mult).then_inc(S("n_xn"), 1)
        to_act("x", vec[:, 0:16])
        splits(0, 0, 2)
        for seg in range(4):
            for b in range(4):
                B = 4 * seg + b
                for i in range(2, 10):
                    splits(2 * B, i, i + 1)
                    if seg:
                        head(seg - 1, b, i)
                if B % 2:
                    mod_copy(B // 2)
                if B == 3:
                    dve.wait_ge(S("f_ps"), 1)
                    dve.tensor_tensor(fl[:, 1:3, 0:HEADS], pC[:, 0:8].rearrange("p (r h) -> p r h", r=RT),
                                         fl[:, 0:1, 0:HEADS].to_broadcast([P, RT, HEADS]), ALU.add).then_inc(S("f_val"), 1)
                    dve.wait_ge(S("f_sp"), 1)
                    dve.scalar_tensor_tensor(out=fl[:, 5:7, 0:HEADS], in0=fl[:, 1:3, 0:HEADS], scalar=0.0,
                                             in1=fl[:, 3:5, 0:HEADS], op0=ALU.min, op1=ALU.subtract).then_inc(S("f_log"), 1)
                    dve.wait_ge(S("f_c"), 1)
                    dve.tensor_copy(cneg[0:HEADS, :], pC[0:HEADS, 256:512]).then_inc(S("f_cneg"), 1)

        for c in range(DC):
            splits(U_UP0 // SLOTS, UPU * c + 2, UPU * c + 4)
            dve.wait_ge(used, U_UP0 + UPU * (c + 1))
            cols = slice(c * NBLK, (c + 1) * NBLK)
            dve.tensor_tensor(merged[:, :, cols], gemm_ps[:, (B_UP0 + c) % 2], xn[:, :, cols], ALU.mult).then_inc(evac_dve, 1)
        first = me.n
        with dve.Fori(0, DC) as c:
            me.iteration(first, 2 * c)
            q = U_PAIRS // SLOTS + 2 * PAIR // SLOTS * c
            for j in range(2):
                splits(q, PAIR * j + 2, PAIR * j + PAIR + 2)
                dve.wait_ge(evac_act, 16 + 2 * c + j + 1)
                dve.wait_ge(used, U_PAIRS + 2 * PAIR * c + PAIR * (j + 1))
                me(dve.tensor_tensor(sg[:], gemm_ps[:, 1], sg[:], ALU.mult))
                m = merged[:, :, bass.ds(c * NBLK, NBLK)]
                dve.tensor_tensor(m, m, sg[:], ALU.add).then_inc(evac_dve, 1)
            mod_copy(8 + c)
        me.iteration(first + 2 * DC, 0)
        to_act("merged")
        def normed(dst, src):
            newton(stat[:, 32:34], stat[:, 34:36], D, stat[:, 36:38])
            for rt in range(RT):
                dve.tensor_scalar(dst[:, rt], src[:, rt], stat[:, 34 + rt:35 + rt], None, ALU.mult).then_inc(S("n_xn"), 1)

        for half in range(2):
            for k in range(2):
                c = 2 * half + k
                splits(U_OUT // SLOTS + 2 * c, 2, 10)
                dve.wait_ge(used, U_OUT + BU * (c + 1))
                if c == 0:
                    dve.wait_ge(S("xres_in"), 16)
                xs = xres[:, :, c * NBLK:(c + 1) * NBLK]
                dve.tensor_tensor(xs, gemm_ps[:, k], xs, ALU.add).then_inc(evac_dve, 1)
            if half == 0:
                dve.wait_ge(S("n_rs"), 2)
                normed(xn, ctx_sb)

        def mod_vectors(bank, cols, g):
            dve.tensor_reduce(vec[:, cols:cols + 32].rearrange("p (v j) -> p v j", v=2),
                              bank.rearrange("p (v g j) -> p v j g", v=2, g=4), AX_X, ALU.add)
            me(dve.engine_nop())
            s = vec[:, cols + 16:cols + 32]
            me(dve.scalar_tensor_tensor(out=s, in0=s, scalar=1.0, in1=g, op0=ALU.add, op1=ALU.mult))

        dve.wait_ge(S("mv_ps"), 1)
        for r in range(2):
            mod_vectors(pA[:, r * P:(r + 1) * P], 60 + 32 * r, vec[:, 16:32])
        for j in range(2):
            for kc in range(4):
                dve.tensor_copy(vec[:, 8 * j + 2 * kc:8 * j + 2 * kc + 2], vec[:, 56 + 2 * j:58 + 2 * j])
        me(dve.engine_nop())
        dve.engine_nop().then_inc(S("mv_done"), 1)
        to_act("ctx", vec[:, 108:124], vec[:, 92:108])
        for cb in range(6):
            for i in range(2, 10):
                splits(U_CTX // SLOTS + 2 * cb, i, i + 1)
                if cb == 0 and i == 2:
                    dve.wait_ge(S("s_ps"), 1)
                    dve.wait_ge(S("wsm_in"), 48)
                    dve.tensor_copy(sm[:, 0:2], pC[:, 0:64].rearrange("p (r c) -> p r c", r=RT)).then_inc(S("sm_in"), 1)
                if cb == 0 and i == 4:
                    dve.wait_ge(S("n_rs"), 3)
                    normed(xn, xres)
            mod_copy(12 + cb)
        to_act("x1", vec[:, 76:92], vec[:, 60:76])

        pre_all = sx[:, 0:2].rearrange("p a b -> p (a b)")
        pre = pre_all.rearrange("p (t d g h) -> p t d g h", t=4, d=2, g=2)
        t8 = lambda row, t=4: sx[:, row, 0:8 * t].rearrange("p (t d h) -> p t d h", t=t, d=2)
        G8, FM = t8(4), t8(5, 2)
        bc = lambda ap, n: ap.rearrange("p (o t) -> p o t", o=1).to_broadcast([P, n, P])

        def step(s):
            if s == 2:
                dve.wait_ge(S("s_ps"), 2)
                dve.tensor_copy(sm[:, 2:4], pC[:, 0:64].rearrange("p (r c) -> p r c", r=RT)).then_inc(S("sm_in"), 1)
            if s == 10:
                dve.tensor_tensor(pre_all.rearrange("p (t c) -> p t c", t=4), sm[:, :, LR:2 * LR],
                                  sx[:, 11:12, 0:LR].to_broadcast([P, 4, LR]), ALU.add).then_inc(S("m_pre"), 1)
            if s == 12:
                dve.wait_ge(S("m_sp"), 1)
                for d in range(2):
                    ins = dve.scalar_tensor_tensor(out=t8(3)[:, :, d], in0=pre[:, :, d, 1], scalar=0.0, in1=t8(2)[:, :, d],
                                                   op0=ALU.min, op1=ALU.subtract)
                ins.then_inc(S("m_lf"), 1)
            if s == 14:
                dve.wait_ge(S("m_F"), 1)
                F = pC[:, P:P + 32].rearrange("p (t d h) -> p t d h", t=4, d=2)
                for d in range(2):
                    for r, sign in ((0, NORMALIZER), (2, -NORMALIZER)):
                        dve.scalar_tensor_tensor(out=G8[:, r:r + 2, d], in0=F[:, r:r + 2, d], scalar=sign,
                                                 in1=pre[:, r:r + 2, d, 0], op0=ALU.mult, op1=ALU.add)
                me(dve.tensor_scalar(FM, F[:, 2:4], NORMALIZER, None, ALU.mult))
                dve.engine_nop().then_inc(S("m_G"), 1)
            if s == 15:
                dve.wait_ge(S("m_GT"), 1)
                me(dve.tensor_copy(grows[:, :], pA[0:8, :]))
                me(dve.tensor_reduce(stat[0:8, 44:45], grows[:, 0:T], AX_X, ALU.max))
                x = grows[:, T:2 * T]
                dve.tensor_tensor_scan(mrows[:, 0], x, x, stat[0:8, 44:45], ALU.max, ALU.max)
                me(dve.tensor_tensor_scan(mrows[:, 1, ::-1], x[:, ::-1], x[:, ::-1], stat[0:8, 44:45], ALU.max, ALU.max))
                dve.engine_nop().then_inc(S("m_rows"), 1)
            if s == 17:
                dve.wait_ge(S("m_MT"), 1)
                M = pB[:, 0:32].rearrange("p (r w d h) -> p r w d h", r=RT, w=2, d=2)
                for d in range(2):
                    ins = dve.tensor_tensor(FM[:, :, d], M[:, :, d, d], FM[:, :, d], ALU.add)
                ins.then_inc(S("m_FM"), 1)
            if s == 18:
                me(dve.memset(glrT[:, :], 1.0))
                dve.wait_ge(S("g_glr"), 1)
                dve.tensor_copy(glrT[0:LR, :], pA[0:LR, :]).then_inc(S("g_glrT"), 1)
            if 21 <= s < 29:
                n = s - 21
                t, d = n // 2, n % 2
                dve.wait_ge(S("g_sp"), n + 1)
                dst = y[:, t, 2 * BW + d * BW:2 * BW + (d + 1) * BW] if t < 2 else la[:, t - 2, d]
                dve.scalar_tensor_tensor(out=dst, in0=ps[:, n % 2], scalar=0.0, in1=spd[:, n % 2],
                                         op0=ALU.min, op1=ALU.subtract).then_inc(S("g_la"), 1)
            if 29 <= s < 33:
                m = s - 29
                t, d = m // 2, m % 2
                dve.wait_ge(S("g_kexp"), m + 1)
                dve.tensor_tensor(y[:, t, d * BW:(d + 1) * BW], kexp[m % 2][:, :], cg[:, t, 0:BW], ALU.mult).then_inc(S("g_kend"), 1)
            if 34 <= s < 66:
                h, i = (s - 34) // 8, (s - 34) % 8 + 2
                if i == 2:
                    dve.wait_ge(S("m_T"), h + 1)
                    dve.tensor_copy(mqT[:, :], pB[:, 0:T]).then_inc(S("m_qT"), 1)
                if i in (4, 7):
                    d = i == 7
                    dve.wait_ge(S("m_QK"), h + 1)
                    if h or d:
                        dve.wait_ge(S("m_num"), 2 * h + d)
                    M = pC[:, d * T:(d + 1) * T]
                    for n, (t, lo, hi) in enumerate(tiles[d]):
                        at0 = 2 * P * n
                        ins = dve.tensor_scalar(mpT[:, at0:at0 + hi - lo], M[:, lo:hi], G8[:, t, d, h:h + 1], 0.0,
                                                ALU.subtract, ALU.max)
                    ins.then_inc(S("m_arg"), 1)
                if i in (5, 8):
                    d = i == 8
                    dve.wait_ge(S("m_exp"), 2 * h + d + 1)
                    qk = ps[:, 0:2].rearrange("p a b -> p (a b)")
                    for n, (t, lo, hi) in enumerate(tiles[d]):
                        at0 = 2 * P * n
                        dst = mpT[:, at0:at0 + hi - lo]
                        ins = dve.tensor_tensor(dst, qk[:, t * T + lo:t * T + hi], dst, ALU.mult)
                    me(ins)
                    a0, a1 = ((4, 6), (5, 6))[d]
                    for q in (a0, a1):
                        dst = mpT[:, q * P:(q + 1) * P]
                        ins = dve.tensor_tensor(dst, dst, C("le" if d else "ge"), ALU.mult)
                    ins.then_inc(S("m_s"), 1)
                if i == 9:
                    dve.wait_ge(S("m_den"), h + 1)
                    dve.wait_ge(S("m_em"), 1)
                    em = t8(6, 2)
                    for d in range(2):
                        ins = dve.tensor_tensor(sx[:, 7, 4 + 2 * d:6 + 2 * d], sx[:, 7, 2 * d:2 * d + 2], em[:, :, d, h], ALU.max)
                    me(ins)
                    me(dve.reciprocal(sx[:, 10, 0:4], sx[:, 7, 4:8]))
                    for d in range(2):
                        for rt in range(RT):
                            dst = y[:, rt, D // 2 + h * GDV:D // 2 + (h + 1) * GDV]
                            src = (pD, pA)[d][:, rt * GDV:(rt + 1) * GDV]
                            r = sx[:, 10, 2 * d + rt:2 * d + rt + 1]
                            if d == 0:
                                ins = dve.tensor_scalar(dst, src, r, None, ALU.mult)
                            else:
                                ins = dve.scalar_tensor_tensor(out=dst, in0=src, scalar=r, in1=dst, op0=ALU.mult, op1=ALU.add)
                        if d == 0:
                            me(ins)
                    ins.then_inc(S("m_y"), 1)
            if s == 66:
                dve.wait_ge(S("g_S"), 1)
                dve.tensor_copy(state[:, 1].rearrange("p h v -> p (h v)"), ps[:, 2:4].rearrange("p a b -> p (a b)")).then_inc(S("g_state"), 1)
            if 69 <= s < 101:
                gla_mult(s - 69)
            if 70 <= s < 102:
                gla_mask(s - 70)

        tiles = (((0, 0, T), (1, 0, T), (2, 0, T), (3, P, T)), ((0, 0, T), (1, 0, T), (3, 0, T), (2, 0, P)))

        def gla_mult(k):
            gc, j = k // 2, k % 2
            h, c = gc // 4, gc % 4
            d, rt = c // 2, c % 2
            base_turn = 15 * h + (1, 4, 8, 11)[c]
            q, kk = gqT[:, 0, rt * P:(rt + 1) * P], gqT[:, 1, rt * P:(rt + 1) * P]
            if j == 0:
                dve.wait_ge(S("g_free"), base_turn + 1)
                dve.tensor_tensor(cr[:, rt], cr[:, rt], q if d != rt else kk, ALU.mult)
                dve.tensor_tensor(fq[:, gc % 2], fq[:, gc % 2], q, ALU.mult).then_inc(S("g_f"), 1)
            dve.wait_ge(S("g_free"), base_turn + 2 + j)
            if k:
                dve.wait_ge(S("g_sc"), k)
            dve.tensor_tensor(rk[:], ek[:, k % 2], bc(kk, 4), ALU.mult)
            dve.tensor_tensor(ek[:, k % 2], ek[:, k % 2], bc(q, 4), ALU.mult).then_inc(S("g_mult"), 1)

        def gla_mask(k):
            gc, j = k // 2, k % 2
            d = gc % 4 // 2
            if k == 0:
                dve.wait_ge(S("lsum_in"), 32)
            dve.wait_ge(S("g_sc"), k + 1)
            me(dve.tensor_tensor(masked[:], pC.rearrange("p (l t) -> p l t", l=4), lpair[:, d, 4 * j:4 * j + 4], ALU.mult))
            if gc and j == 0:
                dve.wait_ge(S("g_o"), gc)
            ins = dve.tensor_reduce(sc[:, j], masked[:].rearrange("p l t -> p t l"), AX_X, ALU.add)
            if j:
                me(ins)
                ins = dve.tensor_tensor(sc[:, 0], sc[:, 0], sc[:, 1], ALU.add)
            ins.then_inc(S("g_mask"), 1)

        for xb in range(12):
            for i in range(2, 10):
                splits(U_X // SLOTS + 2 * xb, i, i + 1)
                step(8 * xb + i)
            if xb in (1, 3):
                mod_copy(18 + xb // 2)
        for s in range(98, 103):
            step(s)
        dve.wait_ge(S("y_rs"), 1)
        newton(sx[:, 8, 0:16], sx[:, 9, 0:16], GDV, sx[:, 10, 0:16])
        dve.wait_ge(evac_act, 42)
        for rt in range(RT):
            for g in range(8):
                cols = slice(g * GDV, (g + 1) * GDV)
                ins = dve.scalar_tensor_tensor(out=y[:, rt, cols], in0=y[:, rt, cols], scalar=sx[:, 9, 8 * rt + g:8 * rt + g + 1],
                                               in1=gates[:, rt, cols], op0=ALU.mult, op1=ALU.mult)
        ins.then_inc(S("y_done"), 1)
        to_act("y", vec[:, 0:16])
        dve.wait_ge(S("mv_ps"), 2)
        mod_vectors(pC[:, 0:P], 124, vec[:, 32:48])
        dve.engine_nop().then_inc(S("mv_done"), 1)
        dve.wait_ge(S("gt_in"), 1)
        dve.wait_ge(S("xres_in2"), 16)
        for c in range(DC):
            splits(U_OUT2 // SLOTS + 2 * c, 2, 10)
            dve.wait_ge(used, U_OUT2 + BU * (c + 1))
            cols = slice(c * NBLK, (c + 1) * NBLK)
            for rt in range(RT):
                ins = dve.tensor_tensor(sg[:, rt], gemm_ps[:, c % 2, rt], gtb[:, cols], ALU.mult)
            me(ins)
            dve.tensor_tensor(xres[:, :, cols], xres[:, :, cols], sg[:], ALU.add).then_inc(evac_dve, 1)
            mod_copy(20 + c)
        dve.wait_ge(S("n_rs"), 4)
        normed(xn, xres)
        to_act("x2", vec[:, 140:156], vec[:, 124:140])
        dve.memset(gp[:], 0.0).then_inc(S("gp_zero"), 1)
        dve.wait_ge(S("cw_ps"), 1)
        dve.tensor_copy(cw[:, :], pC[:, 0:10 * FCH]).then_inc(S("gp_zero"), 1)

        def ffn_hook(b, i, par, start, finish):
            if i == 4 and finish:
                dve.wait_ge(S("f_sil"), b - 1)
                dve.tensor_tensor(fv[:, 0:finish], sil[:, 0:finish], pB[:, 0:finish * T].rearrange("p (f t) -> p f t", f=finish),
                                  ALU.mult).then_inc(S("f_fv"), 1)
            if i == 6 and finish:
                dve.wait_ge(S("f_hi"), b - 1)
                at_f = bass.ds((b - 2) * 2, finish)
                dve.tensor_tensor(ft_lo[:, at_f], fv[:, 0:finish], ft_hi[:, at_f].bitcast(F32), ALU.subtract).then_inc(S("f_lo"), 1)
            if i >= 7 and start:
                if i == 7:
                    dve.wait_ge(S("f_tap0"), b)
                for tap in {7: (1, 2, 3), 8: (4, 5, 6), 9: (7, 8)}[i]:
                    dy, dx = tap // 3, tap % 3
                    for f in range(start):
                        a_f = acc[:, f].rearrange("p (y x) -> p y x", y=4)
                        ins = dve.scalar_tensor_tensor(out=a_f, in0=gp[:, f, dy:dy + 4, dx:dx + 64],
                                                       scalar=cw[:, bass.ds(tap * FCH + (b - 1) * 2 + f, 1)], in1=a_f,
                                                       op0=ALU.mult, op1=ALU.add)
                    if tap < 8:
                        me(ins)
                    else:
                        ins.then_inc(S("f_acc"), 1)

        def ffn_block(b, par, start=2, finish=2):
            for i in range(2, 10):
                splits(U_FFN // SLOTS + 2 * b, i, i + 1)
                ffn_hook(b, i, par, start, finish)

        ffn_block(0, 0, 0, 0)
        ffn_block(1, 1, 2, 0)
        dve.wait_ge(S("x2_out"), 16)
        first = me.n
        with dve.Fori(0, 9) as n:
            me.iteration(first, 14 * n)
            for k in range(2):
                ffn_block(2 * n + 2 + k, k)
        me.iteration(first + 14 * 9, 0)
        ffn_block(20, 0)
        ffn_block(21, 1)
        for i in range(2, 10):
            splits(U_DOWN // SLOTS, i, i + 1)
            ffn_hook(22, i, 0, 1, 2)
        for i in range(2, 10):
            splits(U_DOWN // SLOTS + 2, i, i + 1)
            ffn_hook(23, i, 1, 0, 1)
        tmp = tmp_dn
        for c in range(DC):
            splits(U_DOWN // SLOTS, 18 if c == 0 else DU * c + 2, min(DU * (c + 1) + 2, DC * DU))
            if c == 0:
                dve.wait_ge(S("gt_in"), 2)
                dve.wait_ge(S("x2_in"), 32)
            dve.wait_ge(used, U_DOWN + DU * (c + 1))
            cols = slice(c * NBLK, (c + 1) * NBLK)
            for rt in range(RT):
                ins = dve.tensor_tensor(tmp[:, rt], gemm_ps[:, c % 2, rt], gt2b[:, cols], ALU.mult)
            me(ins)
            dve.tensor_tensor(x2_sb[:, :, cols], x2_sb[:, :, cols], tmp[:], ALU.add).then_inc(evac_dve, 1)
        dve.wait_ge(S("n_rs"), 5)
        newton(stat[:, 32:34], stat[:, 34:36], D, stat[:, 36:38])
        for rt in range(RT):
            dve.scalar_tensor_tensor(out=x2_sb[:, rt], in0=x2_sb[:, rt], scalar=stat[:, 34 + rt:35 + rt], in1=gfin[:, :],
                                     op0=ALU.mult, op1=ALU.mult).then_inc(S("out_done"), 1)


    @block.tensor
    def _(pe):
        def product(u0, slot0, bank, hi, lo, units, chunk0=0, opened=False, after=None, chunks=None, n=NBLK):
            chunks = chunks or units * UK
            for i in range(units):
                slot = (slot0 + i) % SLOTS
                pe.wait_ge(lo_done, u0 + i + 1)
                for kk in range(UK):
                    k = UK * i + kk
                    if k >= chunks:
                        continue
                    for rt in range(RT):
                        tok = slice(rt * P, (rt + 1) * P)
                        for part, (x, w) in enumerate(((hi, w_hi), (hi, w_lo), (lo, w_hi))):
                            mm = pe.matmul(gemm_ps[:, bank, rt, 0:n], x[:, chunk0 + k, tok], w[:, slot, kk, 0:n],
                                           start=(k == 0 and part == 0 and not opened),
                                           stop=(k == chunks - 1 and part == 2))
                mm.then_inc(used, 1)
                if after:
                    after(i)

        def add_row(bank):
            for rt in range(RT):
                pe.matmul(gemm_ps[:, bank, rt], C("sel", 1, 0, P), brow[0:1, 0], start=True, stop=False)

        def mod_unit(m, i):
            if i == 0:
                pe.wait_ge(S("bmod_in"), 16 * (m + 1))
                if not (isinstance(m, int) and m == 0):
                    pe.wait_ge(mod_evac, m)
            pe.wait_ge(mod_in[i % SLOTS], 16 * (2 * m + i // SLOTS + 1))
            for kk in range(UK):
                k = UK * i + kk
                g = k % 4
                mm = pe.matmul(pD[32 * g:32 * g + 32, :], cs[:, k], mraw[:, i % SLOTS, kk],
                               start=(k < 4), stop=(k >= KC - 4), skip_group_check=True)
                if k == 0:
                    pe.matmul(pD[0:32, :], C("two", 1), brow[0:1, 1], start=False, stop=False, skip_group_check=True)
            mm.then_inc(mod_used, 1)

        def every_other(m, half, u):
            if u % 2:
                mod_unit(m, 4 * half + u // 2)

        def to_act(use, src):
            for g in range(BU):
                G = BU * tr_use[use] + g
                if G >= 2:
                    pe.wait_ge(S("tr_val"), G - 1)
                for k in range(UK):
                    for rt in range(RT):
                        kc = UK * g + k
                        mm = pe.transpose(ps[:, g % 2, k * T + rt * P:k * T + (rt + 1) * P],
                                          src[:, rt, kc * P:(kc + 1) * P], ident)
                mm.then_inc(S("tr_ps"), 1)

        def head(r, h, u):
            hh = HEADS * r + h
            src = br[r % 2]
            qT, kT = qkgT[:, 0], qkgT[:, 1]
            if u == 2:
                if r < 2:
                    pe.wait_ge(S("h_pre"), hh + 1)
                else:
                    pe.wait_ge(evac_act, 4 * (r + 1))
                if hh > 0:
                    pe.wait_ge(S("h_y"), hh)
                for rt in range(RT):
                    for t in range(2):
                        s = qkn[:, rt, t] if r < 2 else src[:, rt, t * BW + h * HD:t * BW + (h + 1) * HD]
                        pe.transpose(pA[:, t * T + rt * P:t * T + (rt + 1) * P], s, ident)
                    mm = pe.transpose(pB[:, rt * P:(rt + 1) * P], src[:, rt, 3 * BW + h * HD:3 * BW + (h + 1) * HD], ident)
                mm.then_inc(S("h_T"), 1)
            if u == 3:
                pe.wait_ge(S("h_qkT"), hh + 1)
                if r < 2:
                    if hh == 0:
                        pe.wait_ge(S("f_cneg"), 1)
                    if hh == HEADS:
                        pe.wait_ge(S("rel_in"), 16)
                    if hh > 0:
                        pe.wait_ge(S("h_exp"), 4 * r + h)
                    for rt in range(RT):
                        n = P * (rt + 1)
                        out = pC[:, rt * T:rt * T + n]
                        pe.matmul(out, qT[:, rt * P:(rt + 1) * P], kT[:, 0:n], start=True, stop=False)
                        if r == 0:
                            pe.matmul(out, C("sel", HEADS, h * P, P), cneg[0:HEADS, 0:n], start=False, stop=False)
                        else:
                            for kt in range(rt + 1):
                                d = (rt - kt) * P
                                pe.matmul(out[:, kt * P:(kt + 1) * P], relb[:, h, d:d + P], C("anti"), start=False, stop=False)
                        mm = pe.matmul(out[:, rt * P:n], ident, C("m_causal" if r == 0 else "m_chunk"), start=False, stop=True)
                else:
                    if h == 0:
                        pe.wait_ge(S("h_exp"), 2 * HEADS)
                    else:
                        pe.wait_ge(S("h_PTs"), hh)
                    pe.matmul(pC[:, 0:T], kT[:, 0:P], qT[:, 0:T], start=True, stop=False, skip_group_check=True)
                    mm = pe.matmul(pC[:, T:3 * P], kT[:, P:T], qT[:, P:T], start=False, stop=False, skip_group_check=True)
                mm.then_inc(S("h_L"), 1)
            if u == 5:
                pe.wait_ge(S("h_p"), hh + 1)
                if r < 2:
                    for n, (rt, kt) in enumerate(((0, 0), (1, 0), (1, 1))):
                        mm = pe.transpose(pA[:, n * P:(n + 1) * P], probs[:, rt, kt * P:(kt + 1) * P], ident)
                    mm.then_inc(S("h_PT"), 1)
                else:
                    lk = zwork[:, 1]
                    kw = dict(start=False, skip_group_check=True)
                    pe.matmul(pC[:, 0:T], C("neg_suf_in"), lk[:, 0:T], stop=False, **kw)
                    pe.matmul(pC[:, P:T], C("neg_all"), lk[:, T:3 * P], stop=False, **kw)
                    pe.matmul(pC[:, T:3 * P], C("neg_suf_in"), lk[:, T:3 * P], stop=False, **kw)
                    pe.matmul(pC[:, 0:P], ident, C("m_strict"), stop=False, **kw)
                    pe.matmul(pC[:, T:3 * P], ident, C("m_strict"), stop=True, **kw).then_inc(S("h_R"), 1)
            if u == 6:
                pe.wait_ge(S("h_PTs"), hh + 1)
                pe.wait_ge(S("h_gT"), hh + 1)
                v = src[:, :, 2 * BW + h * HD:2 * BW + (h + 1) * HD]
                pe.matmul(pB[:, 0:T], v[:, 0], probsT[:, 0:T], start=True, stop=False)
                pe.matmul(pB[:, P:T], v[:, 1], probsT[:, T:3 * P], start=False, stop=True).then_inc(S("h_O"), 1)

        pe.wait_ge(S("const_in"), 16)
        pe.wait_ge(S("vec_in"), 144)
        pe.transpose(pC[:, 0:88], vrows[0:88, :], ident[0:88, 0:88]).then_inc(S("n_vecT"), 1)
        pe.wait_ge(S("n_xn"), 2)
        pe.wait_ge(S("cs_set"), 1)
        to_act("x", xn)
        for seg in range(4):
            for b in range(4):
                B = 4 * seg + b
                if B >= 2:
                    pe.wait_ge(evac_act, B - 1)
                if B == 0:
                    pe.wait_ge(S("tr_lo"), BU)
                if seg == 3:
                    pe.wait_ge(brow_in, 16 * (b + 1))
                    add_row(B % 2)
                product(BU * B, 0, B % 2, a_hi, a_lo, BU, opened=(seg == 3),
                        after=lambda u: (seg and head(seg - 1, b, u), every_other(B // 2, B % 2, u)))
                if B == 3:
                    pe.wait_ge(S("wf_in"), 32)
                    for rt in range(RT):
                        for k in range(KC):
                            for n, x in enumerate((a_hi, a_lo)):
                                mm = pe.matmul(pC[:, rt * HEADS:(rt + 1) * HEADS], x[:, k, rt * P:(rt + 1) * P].bitcast(F32),
                                               wf[:, k], start=(k == 0 and n == 0), stop=(k == KC - 1 and n == 1))
                    mm.then_inc(S("f_ps"), 1)
                    pe.wait_ge(S("f_log"), 1)
                    lf = [fl[:, 5 + rt, 0:HEADS] for rt in range(RT)]
                    crow = pC[0:HEADS, 256:512]
                    pe.matmul(crow[:, 0:P], lf[0], C("neg_pre_in"), start=True, stop=True)
                    pe.matmul(crow[:, P:T], lf[0], C("neg_all"), start=True, stop=False)
                    pe.matmul(crow[:, P:T], lf[1], C("neg_pre_in"), start=False, stop=True).then_inc(S("f_c"), 1)
        pe.wait_ge(S("h_ylo"), NBR * HEADS)
        for c in range(DC):
            B = B_UP0 + c
            if c < 2:
                pe.wait_ge(evac_act, B - 1)
            else:
                pe.wait_ge(evac_dve, c - 1)
            product(U_UP0 + UPU * c, UPU * c, B % 2, ys_hi, ys_lo, UPU)
        pe.wait_ge(evac_dve, DC)
        with pe.Fori(0, DC) as c:
            for j in range(2):
                u0 = U_PAIRS + 2 * PAIR * c + PAIR * j
                pe.wait_ge(brow_in, 16 * (DC + 2 * c + j + 1))
                pe.wait_ge(evac_act, 16 + 2 * c + j)
                add_row(0)
                product(u0, PAIR * j, 0, a_hi, a_lo, BU, opened=True, after=lambda u: every_other(8 + c, j, u))
                pe.wait_ge(evac_dve, DC + 2 * c + j)
                product(u0 + BU, PAIR * j + BU, 1, ys_hi, ys_lo, UPU, chunk0=4 * (j + 1))
        pe.wait_ge(evac_dve, 12)
        to_act("merged", merged)
        def small_product(n):
            for rt in range(RT):
                for k in range(KC):
                    for part, x in enumerate((a_hi, a_lo)):
                        mm = pe.matmul(pC[:, rt * 32:rt * 32 + 32], x[:, k, rt * P:(rt + 1) * P].bitcast(F32), wsm[:, k],
                                       start=(k == 0 and part == 0), stop=(k == KC - 1 and part == 1))
            mm.then_inc(S("s_ps"), 1)

        pe.wait_ge(S("tr_lo"), TR("merged"))
        with pe.Fori(0, DC // 2) as i:
            for k in range(2):
                c = 2 * i + k
                pe.wait_ge(evac_dve, 12 + c - 1)
                product(U_OUT + BU * c, 0, k, a_hi, a_lo, BU)
        pe.wait_ge(S("mvr_in"), 256)
        for r in range(2):
            mm = pe.transpose(pA[:, r * P:(r + 1) * P], mvr[:, r], ident)
        mm.then_inc(S("mv_ps"), 1)
        pe.wait_ge(S("n_xn"), 4)
        pe.wait_ge(S("mv_done"), 1)
        to_act("ctx", xn)
        pe.wait_ge(S("tr_lo"), TR("ctx"))
        pe.wait_ge(S("wsm_in"), 48)
        small_product(0)
        for cb in range(6):
            if cb < 2:
                pe.wait_ge(evac_dve, 15 + cb)
            else:
                pe.wait_ge(evac_act, 24 + cb - 1)
            product(U_CTX + BU * cb, 0, (B_CTX + cb) % 2, a_hi, a_lo, BU, after=lambda u: mod_unit(12 + cb, u))
        pe.wait_ge(S("n_xn"), 6)
        to_act("x1", xn)
        pe.wait_ge(S("tr_lo"), TR("x1"))
        pe.wait_ge(S("sm_in"), 1)
        small_product(1)

        LF = sx[:, 3].rearrange("p (t d h) -> p t d h", t=4, d=2)
        LAc = lambda t, d: y[:, t, 2 * BW + d * BW:2 * BW + (d + 1) * BW]

        def step(s):
            if s == 11:
                pe.wait_ge(S("m_lf"), 1)
                F = pC[:, P:P + 32].rearrange("p (t d h) -> p t d h", t=4, d=2)
                for t, d, terms in ((0, 0, (("suf_ex", 0), ("all", 1))), (1, 0, (("suf_ex", 1),)),
                                    (0, 1, (("pre_ex", 0),)), (1, 1, (("all", 0), ("pre_ex", 1))),
                                    (2, 0, (("pre_in", 2),)), (3, 0, (("all", 2), ("pre_in", 3))),
                                    (2, 1, (("suf_in", 2), ("all", 3))), (3, 1, (("suf_in", 3),))):
                    for n, (name, t2) in enumerate(terms):
                        mm = pe.matmul(F[:, t, d], MT[name], LF[:, t2, d], start=(n == 0), stop=(n == len(terms) - 1))
                mm.then_inc(S("m_F"), 1)
            if s == 13:
                pe.wait_ge(S("m_G"), 1)
                for t in range(4):
                    mm = pe.transpose(pA[0:8, t * P:(t + 1) * P], sx[:, 4, 8 * t:8 * t + 8], ident)
                mm.then_inc(S("m_GT"), 1)
            if s == 15:
                pe.wait_ge(S("m_rows"), 1)
                for rt in range(RT):
                    for w in range(2):
                        mm = pe.transpose(pB[:, 16 * rt + 8 * w:16 * rt + 8 * w + 8], mrows[:, w, rt * P:(rt + 1) * P], ident[0:8, 0:8])
                mm.then_inc(S("m_MT"), 1)
            if s == 16:
                for t in range(4):
                    mm = pe.transpose(pA[0:LR, t * P:(t + 1) * P], sm[:, t, 0:LR], ident)
                mm.then_inc(S("g_glr"), 1)
            if 18 <= s < 26:
                n = s - 18
                if n == 0:
                    pe.wait_ge(S("wlr_in"), 32)
                    pe.wait_ge(S("g_glrT"), 1)
                    pe.wait_ge(S("m_FM"), 1)
                if n >= 2:
                    pe.wait_ge(S("g_la"), n - 1)
                t, d = n // 2, n % 2
                pe.matmul(ps[:, n % 2], glrT[0:LR + 1, t * P:(t + 1) * P], wlr[0:LR + 1, d], start=True, stop=True).then_inc(S("g_dec"), 1)
            if 26 <= s < 30:
                m = s - 26
                t, d = m // 2, m % 2
                pe.wait_ge(S("g_la"), 8 if m % 2 else 6)
                if m >= 2:
                    pe.wait_ge(S("g_kexp"), m - 1)
                bank = (pC, pA)[m % 2]
                terms = {(0, 0): (("suf_ex", 0), ("all", 1)), (1, 0): (("suf_ex", 1),),
                         (0, 1): (("pre_ex", 0),), (1, 1): (("all", 0), ("pre_ex", 1))}[t, d]
                for n, (name, t2) in enumerate(terms):
                    mm = pe.matmul(bank, MT[name], LAc(t2, d), start=(n == 0), stop=(n == len(terms) - 1))
                mm.then_inc(S("g_w"), 1)
            if 32 <= s < 64:
                h, u = (s - 32) // 8, (s - 32) % 8
                if u == 0:
                    if h:
                        pe.wait_ge(S("m_y"), h)
                    else:
                        pe.wait_ge(evac_act, 30 + 4)
                        pe.wait_ge(S("g_kexp"), 4)
                    for rt in range(RT):
                        pe.transpose(pA[:, rt * P:(rt + 1) * P], cm[:, rt, h * HD:(h + 1) * HD], ident)
                        pe.transpose(pA[:, T + rt * P:T + (rt + 1) * P], xm[:, rt, BW + h * HD:BW + (h + 1) * HD], ident)
                        mm = pe.transpose(pB[:, rt * P:(rt + 1) * P], xm[:, rt, h * HD:(h + 1) * HD], ident)
                    mm.then_inc(S("m_T"), 1)
                if u == 2:
                    pe.wait_ge(S("m_kT"), h + 1)
                    pe.wait_ge(S("m_qT"), h + 1)
                    for t in range(4):
                        pe.matmul(ps[:, t // 2, t % 2 * T:(t % 2 + 1) * T], mkT[:, t * P:(t + 1) * P], mqT[:, :], start=True, stop=True)
                    for d in range(2):
                        r = 4 * d + h
                        mm = pe.matmul(pC[:, d * T:(d + 1) * T], C("sel", 8, r * P, P), mrows[:, d], start=True, stop=True)
                    mm.then_inc(S("m_QK"), 1)
                if u in (4, 7):
                    d = u == 7
                    if h == 0 and d == 0:
                        pe.wait_ge(mod_evac, 20)
                    pe.wait_ge(S("m_s"), 2 * h + d + 1)
                    num(h, int(d))
            if s == 64:
                pe.wait_ge(S("m_y"), HEADS)
                for d in range(2):
                    for h in range(HEADS):
                        out = ps[:, 2 * d + h // 2, h % 2 * GDV:(h % 2 + 1) * GDV]
                        for t in range(RT):
                            mm = pe.matmul(out, y[:, t, d * BW + h * HD:d * BW + (h + 1) * HD], cg[:, t, BW + h * GDV:BW + (h + 1) * GDV],
                                           start=(t == 0), stop=(t == 1))
                mm.then_inc(S("g_S"), 1)
            if 66 <= s <= 98:
                gla_fill(s - 66)
            if 67 <= s < 99:
                gla_score(s - 67)
            if s >= 69 and s % 2 and (s - 69) // 2 < 16:
                gla_out((s - 69) // 2)

        MT = {n: C(n) for n in ("pre_in", "suf_in", "pre_ex", "suf_ex", "all")}
        tiles = (((0, 0, T), (1, 0, T), (2, 0, T), (3, P, T)), ((0, 0, T), (1, 0, T), (3, 0, T), (2, 0, P)))
        def num(h, d):
            v = [cm[:, 0, BW:], cm[:, 1, BW:], xm[:, 0, 2 * BW:], xm[:, 1, 2 * BW:]]
            for rt in range(RT):
                seen = [(t, 2 * P * n + rt * P - lo) for n, (t, lo, hi) in enumerate(tiles[d]) if lo <= rt * P < hi]
                for n, (t, at0) in enumerate(seen):
                    pe.matmul(numb[d][:, rt * GDV:(rt + 1) * GDV], mpT[:, at0:at0 + P], v[t][:, h * GDV:(h + 1) * GDV],
                              start=(n == 0), stop=(n == len(seen) - 1))
            for rt in range(RT):
                seen = [(t, 2 * P * n + rt * P - lo) for n, (t, lo, hi) in enumerate(tiles[d]) if lo <= rt * P < hi]
                for n, (t, at0) in enumerate(seen):
                    mm = pe.matmul(denb[:, 2 * d + rt:2 * d + rt + 1], mpT[:, at0:at0 + P], C("neg_all", P, 0, 1),
                                   start=(n == 0), stop=(n == len(seen) - 1))
            mm.then_inc(S("m_num"), 1)

        pe_turn = [0]

        def give():
            if pe_turn[0] >= 2:
                pe.wait_ge(S("g_free"), pe_turn[0] - 1)
            pe_turn[0] += 1
            return ps[:, (pe_turn[0] - 1) % 2]

        def gla_fill(k):
            gc, j = k // 2, k % 2
            h, c = gc // 4, gc % 4
            d, rt = c // 2, c % 2
            if j == 0 and gc and c % 2 == 0:
                dp = (gc - 1) % 4 // 2
                pe.wait_ge(S("g_f"), gc)
                pe.matmul(give()[:, 0:P], cr[:, dp], cr[:, 1 - dp], start=True, stop=True).then_inc(S("g_ps"), 1)
            if k == 32:
                return
            if j == 0 and c == 0:
                if h == 0:
                    pe.wait_ge(S("g_state"), 2)
                    pe.wait_ge(evac_act, 30 + 8)
                bank = give()
                for t in range(RT):
                    pe.transpose(bank[:, t * P:(t + 1) * P], xg[:, t, h * HD:(h + 1) * HD], ident)
                    mm = pe.transpose(bank[:, T + t * P:T + (t + 1) * P], xg[:, t, BW + h * HD:BW + (h + 1) * HD], ident)
                mm.then_inc(S("g_ps"), 1)
            L = lambda t: la[:, t, d, h * HD:(h + 1) * HD]
            if j == 0:
                bank = give()
                edge = {(0, 0): "suf_ex", (0, 1): "pre_in", (1, 0): "suf_in", (1, 1): "pre_ex"}[d, rt]
                since = "suf_in" if d else "pre_in"
                pe.matmul(bank[:, 0:P], L(rt), MT[edge], start=True, stop=True)
                far = rt != d
                mm = pe.matmul(bank[:, P:2 * P], L(rt), MT[since], start=True, stop=not far)
                if far:
                    mm = pe.matmul(bank[:, P:2 * P], L(1 - rt), MT["all"], start=False, stop=True)
                mm.then_inc(S("g_ps"), 1)
            bank = give()
            if k == 0:
                pe.wait_ge(S("lsum_in"), 32)
            pe.matmul(bank, L(rt), lsum[:, d, 4 * j:4 * j + 4].rearrange("p l t -> p (l t)"), start=True, stop=True).then_inc(S("g_ps"), 1)

        def gla_score(k):
            pe.wait_ge(S("g_mult"), k + 1)
            if k:
                pe.wait_ge(S("g_mask"), k)
            for l in range(4):
                mm = pe.matmul(pC[:, l * P:(l + 1) * P], rk[:, l], ek[:, k % 2, l], start=True, stop=True)
            mm.then_inc(S("g_sc"), 1)

        def gla_out(gc):
            h, c = gc // 4, gc % 4
            d, rt = c // 2, c % 2
            v = lambda t: xg[:, t, 2 * BW + h * GDV:2 * BW + (h + 1) * GDV]
            out = lambda t: pD[:, t * GDV:(t + 1) * GDV]
            kw = dict(skip_group_check=True)
            pe.wait_ge(S("g_mask"), 2 * gc + 2)
            if c == 0 and h:
                pe.wait_ge(S("g_y"), h)
            pe.matmul(out(rt), fq[:, gc % 2], state[:, d, h], start=(c == 0), stop=False, **kw)
            mm = pe.matmul(out(rt), sc[:, 0], v(rt), start=False, stop=False, **kw)
            if rt == 1:
                pe.wait_ge(S("g_free"), 15 * h + (7 if d == 0 else 14) + 1)
                mm = pe.matmul(out(1 - d), sc[:, 2], v(d), start=False, stop=(d == 1), **kw)
            mm.then_inc(S("g_o"), 1)

        numb, denb = (pD, pA), pC
        for xb in range(12):
            pe.wait_ge(evac_act, 30 + xb - 1)

            def after(u):
                step(8 * xb + u)
                if xb < 4:
                    every_other(18 + xb // 2, xb % 2, u)
            product(U_X + BU * xb, 0, (B_X + xb) % 2, a_hi, a_lo, BU, after=after)
        for s in range(96, 101):
            step(s)
        pe.wait_ge(S("y_done"), 1)
        to_act("y", y)
        pe.wait_ge(S("mvr_in2"), 128)
        pe.transpose(pC[:, 0:P], mvr[:, 0], ident).then_inc(S("mv_ps"), 1)
        pe.wait_ge(S("mv_done"), 2)
        pe.wait_ge(S("tr_lo"), TR("y"))
        pe.wait_ge(S("gtr_in"), 16)
        for c in range(DC):
            mm = pe.matmul(ps[:, c], C("neg_all", 4), gtr[:, c * NBLK:(c + 1) * NBLK], start=True, stop=True)
        mm.then_inc(S("gt_ps"), 1)
        pe.wait_ge(S("gt_in"), 1)
        for c in range(DC):
            if c < 2:
                pe.wait_ge(evac_act, 41 + c)
            else:
                pe.wait_ge(evac_dve, 16 + c - 1)
            product(U_OUT2 + BU * c, 0, c % 2, a_hi, a_lo, BU, after=lambda u: mod_unit(20 + c, u))
        pe.wait_ge(S("cw_in"), 80)
        for t in range(4):
            k = (P, P, P, 10 * FCH - 3 * P)[t]
            mm = pe.transpose(pC[:, t * P:t * P + k], cwr[0:k, t], ident[0:k, 0:k])
        mm.then_inc(S("cw_ps"), 1)
        pe.wait_ge(S("n_xn"), 8)
        to_act("x2", xn)

        def turn_u(b, par, nf):
            pe.wait_ge(evac_act, 42 + b)
            if not (isinstance(b, int) and b == 1):
                pe.wait_ge(S("f_fv"), b - 1)
            for half, bank in enumerate((pA, pB)):
                for f in range(nf):
                    for rt in range(RT):
                        c0 = (half * nf + f) * P
                        mm = pe.transpose(bank[:, f * T + rt * P:f * T + (rt + 1) * P], ub[:, 1 - par, rt, c0:c0 + P], ident)
            mm.then_inc(S("f_T"), 1)

        def ffn_block(b, par, turned=2, n=NBLK):
            if isinstance(b, int) and b < 2:
                pe.wait_ge(evac_dve, 19 + b)
            else:
                pe.wait_ge(evac_act, 42 + b - 1)
            product(U_FFN + BU * b, 0, par, a_hi, a_lo, BU, n=n,
                    after=lambda u: turn_u(b, par, turned) if u == 3 and turned else None)

        pe.wait_ge(S("tr_lo"), TR("x2"))
        pe.wait_ge(S("gp_zero"), 2)
        ffn_block(0, 0, 0)
        ffn_block(1, 1)
        with pe.Fori(0, 9) as n:
            for k in range(2):
                ffn_block(2 * n + 2 + k, k)
        ffn_block(20, 0)
        ffn_block(21, 1, n=T)
        pe.wait_ge(S("f_lo"), 20)
        for c in range(DC):
            if c < 2:
                pe.wait_ge(evac_act, 63 + c)
            else:
                pe.wait_ge(evac_dve, 20 + c - 1)

            def after(u):
                if c == 0 and u == 3:
                    turn_u(22, 0, 1)
                if c == 0 and u == 19:
                    pe.wait_ge(S("f_lo"), FB)
            product(U_DOWN + DU * c, (DU * c) % SLOTS, c % 2, ft_hi, ft_lo, DU, chunks=FCH, after=after)
            if c == 0:
                pe.wait_ge(S("gtr2_in"), 16)
                for n in range(DC):
                    mm = pe.matmul(ps[:, n], C("neg_all", 4), gtr2[:, n * NBLK:(n + 1) * NBLK], start=True, stop=True)
                mm.then_inc(S("gt_ps"), 1)

    block.__exit__(None, None, None)


_INS = [
    "x", "norm_g", "w_in", "b_f", "b_gate", "qk_norm_g", "rel_bias", "w_up", "w_out", "c_2", "ctx_2", "c_ctx_2",
    "w_mod_2", "b_mod_2", "g_norm1_2", "g_norm2_2", "w_in_2", "gla_w_lr_2", "gla_b_lr_2", "mlstm_b_gate_2",
    "gla_g_norm_2", "mlstm_g_norm_2", "w_out_2", "w_up_2", "conv_w_2", "conv_b_2", "w_down_2", "g_final_2",
]
_OUTS = [((1, T, D), "float32")]


def kernel(**inputs):
    import numpy as _np
    import concourse.bacc as _bacc
    from concourse import mybir as _mybir
    from concourse.bass_utils import run_bass_kernel_spmd as _run

    nc = _bacc.Bacc("TRN2", target_bir_lowering=False, num_devices=1)
    arrays, args = {}, {}
    named = {name: _np.ascontiguousarray(inputs[name]) for name in _INS}
    named["const"], named["lsum"] = CONST, LSUM
    named["lpair"] = LPAIR.astype(_np.dtype("bfloat16"))
    for name, a in named.items():
        arrays[f"in_{name}_dram"] = a
        args[name] = nc.dram_tensor(f"in_{name}_dram", a.shape, _mybir.dt.from_np(a.dtype), kind="ExternalInput").ap()
    for i, (shape, dtype) in enumerate(_OUTS):
        dt = _mybir.dt.from_np(_np.dtype(dtype))
        args["out"] = nc.dram_tensor(f"out_{i}_dram", shape, dt, kind="ExternalOutput").ap()
    build(nc, args)
    r = _run(nc, [arrays], core_ids=[0])
    got = tuple(r.results[0][f"out_{i}_dram"] for i in range(len(_OUTS)))
    return got[0]
```

```python
import concourse.bass as bass
from concourse import mybir
import numpy as np

F32 = mybir.dt.float32
F32R = mybir.dt.float32r
ALU = mybir.AluOpType
ACT = mybir.ActivationFunctionType
AX_X = mybir.AxisListType.X

P = 128
T = 256
RT = T // P
D = 2048
KC = D // P
NBLK = 512
UK = 2
SLOTS = 4
BU = KC // UK
HD = 128
HEADS = 4
BW = HEADS * HD
NBR = 3
MAX_REL = 128
CHUNK = 64
EPS = 1e-6
NEG = -1e30
SCALE = float(HD) ** -0.5
FF = 5504
FCH = FF // P
GDV = 256
NORMALIZER = 16.0
DC = D // NBLK

U_QKVG = 0
UPU = BW // P // UK
PAIR = BU + UPU
U_GATE0 = U_QKVG + 12 * BU
U_UP0 = U_GATE0 + DC * BU
U_PAIRS = U_UP0 + DC * UPU
U_OUT = U_PAIRS + 2 * DC * PAIR
U_CTX = U_OUT + DC * BU
U_X = U_CTX + 6 * BU
U_OUT2 = U_X + 12 * BU
U_FFN = U_OUT2 + DC * BU
FB = 22
U_DOWN = U_FFN + FB * BU
DU = (FCH + 1) // UK
U_END = U_DOWN + DC * DU

B_GATE0, B_UP0, B_PAIRS, B_OUT, B_CTX, B_X, B_OUT2, B_FFN, B_DOWN = 12, 16, 20, 36, 40, 46, 58, 62, 84


def constants():
    t = np.arange(P)
    row, col = t[:, None], t[None, :]
    one = np.ones((P, P), np.float32)
    c = {}
    c["ident"] = (row == col)
    c["anti"] = (row + col == P - 1)
    c["pre_in"] = (row <= col) / NORMALIZER
    c["suf_in"] = (row >= col) / NORMALIZER
    c["pre_ex"] = (row < col) / NORMALIZER
    c["suf_ex"] = (row > col) / NORMALIZER
    c["all"] = one / NORMALIZER
    c["neg_pre_in"] = -1.0 * (row <= col)
    c["neg_suf_in"] = -1.0 * (row >= col)
    c["neg_all"] = -one
    c["m_causal"] = NEG * (col > row)
    c["m_chunk"] = NEG * (col // CHUNK > row // CHUNK)
    c["m_strict"] = NEG * (row >= col)
    c["strict"] = np.concatenate([row < col, one, row < col], 1)
    sel = np.zeros((P, 8 * P))
    for r in range(8):
        sel[r, r * P:(r + 1) * P] = 1.0
    c["sel"] = sel
    c["ge"] = (row <= col)
    c["le"] = (row >= col)
    c["stack"] = (row % 32 == col)[:, 0:32]
    order, at, parts = {}, 0, []
    for k, v in c.items():
        v = np.asarray(v, np.float32)
        order[k] = (at, v.shape[1])
        at += v.shape[1]
        parts.append(v)
    return order, np.concatenate(parts, 1)


def level_constants():
    t = np.arange(P)
    row, col = t[:, None], t[None, :]
    sums, pairs = [], []
    for d in range(2):
        for size in (128, 64, 32, 16, 8, 4, 2):
            mid = col // size * size + size // 2
            if d == 0:
                m = np.where(col >= mid, (row >= mid) & (row <= col), (row > col) & (row < mid))
                pair = (row // size == col // size) & (row % size < size // 2) & (col % size >= size // 2)
            else:
                m = np.where(col < mid, (row >= col) & (row < mid), (row >= mid) & (row < col))
                pair = (row // size == col // size) & (row % size >= size // 2) & (col % size < size // 2)
            sums.append(m / NORMALIZER)
            pairs.append(pair)
        sums.append(np.zeros((P, P)))
        pairs.append(row == col)
    return np.concatenate(sums, 1).astype(np.float32), np.concatenate(pairs, 1).astype(np.float32)


CONST_AT, CONST = constants()
LSUM, LPAIR = level_constants()
LEVELS = 8

KB = 1024

GQ, GK, GV, GG, GLR, MQ, MK, MV, MO, MG = 0, 512, 1024, 2048, 3072, 3088, 3600, 4112, 5136, 6160
CTX_COLS = (MK, MV, MV + NBLK, GK, GV, GV + NBLK)
X_COLS = (MQ, MK, MV, MV + NBLK, GQ, GK, GV, GV + NBLK, GG, GG + NBLK, MO, MO + NBLK)
LR = 16
MODS = 24
MODC = 6 * D


class Count:

    def __init__(self, eng, sem):
        self.eng, self.sem, self.n, self.off = eng, sem, 0, 0

    def __call__(self, ins):
        self.n += 1
        ins.then_inc(self.sem, 1)
        self.eng.wait_ge(self.sem, self.n + self.off)

    def iteration(self, first, i):
        self.n, self.off = first, i



def build(nc, a):
    base = (nc.sbuf_base + 31) // 32 * 32

    def at(name, shape, dtype, kb):
        return nc.alloc_sbuf_tensor_at(name, shape, dtype, offset=base + int(kb * KB))

    raw = at("w_raw", [P, SLOTS, UK, NBLK], F32, 0)
    w_hi = at("w_hi", [P, SLOTS, UK, NBLK], F32R, 16)
    w_lo = at("w_lo", [P, SLOTS, UK, NBLK], F32R, 32)
    a_hi = at("a_hi", [P, KC, T], F32R, 48)
    a_lo = at("a_lo", [P, KC, T], F32R, 64)
    cst = at("cst", [P, CONST.shape[1]], F32, 80)
    cs = at("cs", [P, KC, 32], F32, 93.5)
    mrow = at("mrow", [P, NBLK], F32, 95.5)
    mraw = at("mraw", [P, SLOTS, UK, NBLK], F32, 97.5)
    x_sb = at("x_sb", [P, RT, D], F32, 113.5)
    xn = at("xn", [P, RT, D], F32, 113.5)
    diag = at("diag", [P, RT, P], F32, 204.5)
    br = [at(f"br{i}", [P, RT, 4 * BW], F32, 129.5 + 16 * i) for i in range(2)]
    ys_hi = at("ys_hi", [P, NBR * HEADS, T], F32R, 161.5)
    ys_lo = at("ys_lo", [P, NBR * HEADS, T], F32R, 173.5)
    brow = at("brow", [1, NBLK], F32, 185.5)
    relb = at("relb", [P, HEADS, T], F32, 189.5)
    tmpT = at("tmpT", [P, 2, UK, T], F32, 193.5)
    sg = at("sg", [P, RT, NBLK], F32, 193.5)
    qkn = at("qkn", [P, RT, 2, HD], F32, 193.5)
    qkgT = at("qkgT", [P, 3, T], F32, 195.5)
    probs = at("probs", [P, RT, T], F32, 198.5)
    zwork = at("zwork", [P, 2, 3 * P], F32, 198.5)
    probsT = at("probsT", [P, 3 * P], F32, 201.5)
    yT = at("yT", [P, T], F32, 203)
    cneg = at("cneg", [P, T], F32, 205)
    wf = at("wf", [P, KC, 32], F32, 201.5)
    fparts = at("fparts", [P, T], F32, 203.5)
    fl = at("fl", [P, 8, 8], F32, 206.25)
    gbias = at("gbias", [P, 1], F32, 206.5)
    stat = at("stat", [P, 64], F32, 206.625)
    vec = at("vec", [P, 160], F32, 207)
    merged = br[0]
    vrows = sg[:, 0, 0:P]
    rel_ext = probs[0:HEADS].rearrange('p a b -> p (a b)')[:, 0:384]
    rrows = sg[:, 1, 0:512]

    BF16 = mybir.dt.bfloat16
    ctx_sb = at("ctx_sb", [P, RT, D], F32, 129.5)
    mvr = at("mvr", [P, 2, P], F32, 153.5)
    mvb = at("mvb", [32, P], F32, 154.5)
    zparts = at("zparts", [P, T], F32, 197.5)
    xres = at("xres", [P, RT, D], F32, 161.5)
    wsm = at("wsm", [P, KC, 2 * LR], F32, 185.5)
    y = xn
    cm = at("cm", [P, RT, 3 * NBLK], F32, 129.5)
    cg = at("cg", [P, RT, 3 * NBLK], F32, 141.5)
    xm = at("xm", [P, RT, 4 * NBLK], F32, 153.5)
    xg = at("xg", [P, RT, 4 * NBLK], F32, 169.5)
    la = at("la", [P, RT, 2, NBLK], F32, 189.5)
    glrT = at("glrT", [32, 2 * T], F32, 169.5)
    spd = at("spd", [P, 2, NBLK], F32, 171.5)
    kexp = [at("kexp0", [P, NBLK], F32, 175.5), at("kexp1", [P, NBLK], F32, 181.5)]
    wlr = at("wlr", [32, 2, NBLK], F32, 177.5)
    mrows = at("mrows", [8, 2, T], F32, 185.5)
    grows = at("grows", [8, 2 * T], F32, 198.5)
    mqT = at("mqT", [P, T], F32, 197.5)
    mkT = at("mkT", [P, 2 * T], F32, 198.5)
    mpT = at("mpT", [P, 7 * P], F32, 200.5)
    sm = at("sm", [P, 4, 2 * LR], F32, 204)
    sx = at("sx", [P, 12, 32], F32, 204.5)
    gates = at("gates", [P, RT, D], F32, 153.5)
    state = at("state", [P, 2, HEADS, GDV], F32, 129.5)
    gqT = at("gqT", [P, 2, T], F32, 137.5)
    cr = at("cr", [P, RT, P], F32, 139.5)
    fq = at("fq", [P, 2, P], F32, 140.5)
    lsum = at("lsum", [P, 2, LEVELS, P], F32, 141.5)
    lpair = at("lpair", [P, 2, LEVELS, P], BF16, 149.5)
    masked = at("masked", [P, 4, P], F32, 185.5)
    ek = at("ek", [P, 2, 4, P], F32, 197.5)
    rk = at("rk", [P, 4, P], F32, 201.5)
    sc = at("sc", [P, 3, P], F32, 203.5)
    gtb = at("gtb", [P, D], F32, 129.5)
    gtr = at("gtr", [5, D], F32, 137.5)
    tmp_dn = at("tmp_dn", [P, RT, NBLK], F32, 191.5)
    ft_hi = at("ft_hi", [P, FCH, T], F32R, 97.5)
    ft_lo = at("ft_lo", [P, FCH, T], F32R, 140.5)
    ub = at("ub", [P, 2, RT, NBLK], F32, 183.5)
    gp = at("gp", [P, 2, 6, 66], F32, 191.5)
    acc = at("acc", [P, 2, T], F32, 194.75)
    sil = at("sil", [P, 2, T], F32, 196.75)
    fv = at("fv", [P, 2, T], F32, 198.75)
    cw = at("cw", [P, 10 * FCH], F32, 200.75)
    cwr = at("cwr", [P, 4, P], F32, 202.5)
    x2_sb = at("x2_sb", [P, RT, D], F32, 48)
    squares = at("squares", [P, RT, D], F32, 97.5)
    gt2b = at("gt2b", [P, D], F32, 64)
    gfin = at("gfin", [P, D], F32, 72)
    gtr2 = at("gtr2", [5, D], F32, 183.5)

    def C(name, rows=P, lo=0, n=None):
        s, width = CONST_AT[name]
        return cst[0:rows, s + lo:s + lo + (width if n is None else n)]

    gemm_ps = nc.alloc_psum_tensor("gemm_ps", [P, 2, RT, NBLK], F32)
    ps = nc.alloc_psum_tensor("ps", [P, 4, NBLK], F32)
    pA, pB, pC, pD = (ps[:, i] for i in range(4))
    ident = C("ident")

    x1_d = nc.dram_tensor("x1_d", [T, D], F32, kind="Internal").ap().rearrange("(r p) d -> p r d", p=P)
    x2_d = nc.dram_tensor("x2_d", [T, D], F32, kind="Internal").ap().rearrange("(r p) d -> p r d", p=P)
    mod_d = nc.dram_tensor("mod_d", [4, 2, MODC], F32, kind="Internal").ap()
    out_v = a["out"].rearrange("o (r p) d -> p (o r) d", p=P)
    ext_d = nc.dram_tensor("ext_d", [HEADS, 384], F32, kind="Internal").ap()

    sems = {}

    def S(name):
        if name not in sems:
            sems[name] = nc.alloc_semaphore(name)
        return sems[name]

    raw_in = [S(f"raw_in{i}") for i in range(SLOTS)]
    brow_in = S("brow_in")
    mod_in = [S(f"mod_in{i}") for i in range(SLOTS)]
    mod_used, mod_evac, mod_out = S("mod_used"), S("mod_evac"), S("mod_out")
    tr_use = {"x": 0, "merged": 1, "ctx": 2, "x1": 3, "y": 4, "x2": 5}
    TR = lambda use: BU * (tr_use[use] + 1)
    hi_done, lo_done, used = S("hi_done"), S("lo_done"), S("used")
    evac_act, evac_dve = S("evac_act"), S("evac_dve")

    w_in = a["w_in"].rearrange("o (j p) c -> p (o j) c", p=P)
    w_up = a["w_up"].rearrange("o n (j p) c -> p (o n j) c", p=P)
    w_out = a["w_out"].rearrange("o (j p) c -> p (o j) c", p=P)
    w_mod = a["w_mod_2"].rearrange("o (j p) c -> p (o j) c", p=P)
    w_in2 = a["w_in_2"].rearrange("o (j p) c -> p (o j) c", p=P)
    w_out2 = a["w_out_2"].rearrange("o (j p) c -> p (o j) c", p=P)
    w_up2 = a["w_up_2"].rearrange("o (j p) (s c) -> p (o j) s c", p=P, s=2)
    w_dn = a["w_down_2"].rearrange("o (j p) c -> p (o j) c", p=P)
    xv = a["x"].rearrange("o (r p) d -> p (o r) d", p=P)
    QKVG_COLS = NBR * 4 * BW
    GATE0 = QKVG_COLS + HEADS

    block = nc.Block()
    block.__enter__()

    @block.sync
    def _(sp):
        def unit(q, slot, src):
            if not (isinstance(q, int) and q == 0):
                sp.wait_ge(lo_done, 4 * q + slot + 1 - SLOTS)
            sp.dma_start(raw[:, slot, 0:src.shape[1], 0:src.shape[2]], src).then_inc(raw_in[slot], 16)

        def mod_unit(m, i):
            if not (isinstance(m, int) and 2 * m + i // SLOTS == 0):
                sp.wait_ge(mod_used, BU * m + i + 1 - SLOTS)
            sp.dma_start(mraw[:, i % SLOTS], w_mod[:, UK * i:UK * i + UK, bass.ds(m * NBLK, NBLK)]).then_inc(mod_in[i % SLOTS], 16)

        def units(w, q, col, first=0, count=BU, row=0, mod=None):
            for i in range(count):
                s = first + i
                unit(q + s // SLOTS, s % SLOTS, w[:, row + UK * i:row + UK * i + UK, bass.ds(col, NBLK)])
                if mod:
                    mod(i)

        def every_other(m, half):
            return lambda i: mod_unit(m, 4 * half + i // 2) if i % 2 else None

        sp.dma_start(x_sb[:], xv).then_inc(S("x_in"), 16)
        sp.dma_start(cst[:, :], a["const"]).then_inc(S("const_in"), 16)
        for i, name in enumerate(("norm_g", "g_norm1_2", "g_norm2_2")):
            sp.dma_start(vrows[16 * i:16 * i + 16, :], a[name].rearrange("o (j p) -> (o j) p", p=P)).then_inc(S("vec_in"), 16)
        sp.dma_start(vrows[48:52, :], a["qk_norm_g"].rearrange("o g p -> (o g) p")).then_inc(S("vec_in"), 16)
        sp.dma_start(vrows[52:54, :], a["gla_g_norm_2"].rearrange("o (j p) -> (o j) p", p=P)).then_inc(S("vec_in"), 16)
        sp.dma_start(vrows[54:56, :], a["mlstm_g_norm_2"].rearrange("o (j p) -> (o j) p", p=P)).then_inc(S("vec_in"), 16)
        sp.dma_start(vrows[56:72, :], a["c_2"].rearrange("o (j p) -> (o j) p", p=P)).then_inc(S("vec_in"), 16)
        sp.dma_start(vrows[72:88, :], a["c_ctx_2"].rearrange("(j p) -> j p", p=P)).then_inc(S("vec_in"), 16)
        sp.dma_start(rrows[0:HEADS, 0:2 * MAX_REL + 1], a["rel_bias"].rearrange("o h m -> (o h) m")).then_inc(S("vec_in"), 16)
        units(w_in, 0, 0)
        sp.dma_start(fl[:, 0, 0:HEADS], a["b_f"][0].partition_broadcast(P)).then_inc(S("wf_in"), 16)
        sp.wait_ge(S("wf_zero"), 1)
        sp.dma_start(wf[:, :, 0:HEADS], w_in[:, :, QKVG_COLS:GATE0]).then_inc(S("wf_in"), 16)
        sp.wait_ge(S("rel_ext"), 1)
        sp.dma_start(ext_d, rel_ext).then_inc(S("rel_out"), 16)
        for i in range(4):
            mod_unit(0, i)
        units(w_in, 2, NBLK, mod=every_other(0, 1))
        sp.wait_ge(S("rel_out"), 16)
        diagonals = bass.AP(tensor=ext_d.tensor, offset=1, ap=[[1, P], [384, HEADS], [1, T]])
        sp.dma_start(relb[:], diagonals).then_inc(S("rel_in"), 16)
        for b in range(2, 12):
            units(w_in, 2 * b, b * NBLK, mod=every_other(b // 2, b % 2))
        bg = a["b_gate"]
        for g in range(DC):
            if g:
                sp.wait_ge(used, U_GATE0 + BU * (g - 1) + 1)
            sp.dma_start(brow[:, :], bg[:, g * NBLK:(g + 1) * NBLK]).then_inc(brow_in, 16)
            b = 12 + g
            units(w_in, 2 * b, GATE0 + g * NBLK, mod=every_other(b // 2, b % 2))
        for c in range(DC):
            s = UPU * c
            units(w_up, U_UP0 // SLOTS + s // SLOTS, c * NBLK, s % SLOTS, UPU)
        with sp.Fori(0, DC) as c:
            for j in range(2):
                sp.wait_ge(used, U_PAIRS + 2 * PAIR * c + (1 if j else 1 - PAIR))
                sp.dma_start(brow[:, :], bg[:, bass.ds((j + 1) * D + c * NBLK, NBLK)]).then_inc(brow_in, 16)
                q = U_PAIRS // SLOTS + 2 * PAIR // SLOTS * c
                units(w_in, q, GATE0 + (j + 1) * D + c * NBLK, PAIR * j, mod=every_other(8 + c, j))
                units(w_up, q, c * NBLK, PAIR * j + BU, UPU, row=4 * (j + 1))
        with sp.Fori(0, DC) as c:
            units(w_out, U_OUT // SLOTS + 2 * c, c * NBLK)
        for i, col in enumerate(CTX_COLS):
            units(w_in2, U_CTX // SLOTS + 2 * i, col, mod=lambda u: mod_unit(12 + i, u))
        for i, col in enumerate(X_COLS):
            units(w_in2, U_X // SLOTS + 2 * i, col, mod=every_other(18 + i // 2, i % 2) if i < 4 else None)
        with sp.Fori(0, DC) as c:
            units(w_out2, U_OUT2 // SLOTS + 2 * c, c * NBLK, mod=lambda u: mod_unit(20 + c, u))

        def ffn_units(q, f, n):
            for i in range(BU):
                slot = i % SLOTS
                sp.wait_ge(lo_done, 4 * q + i + 1 - SLOTS)
                dst = raw[:, slot, :, 0:2 * n].rearrange("p k (s c) -> p k s c", s=2)
                for s in range(2):
                    sp.dma_start(dst[:, :, s], w_up2[:, UK * i:UK * i + UK, s, bass.ds(f, n)]).then_inc(raw_in[slot], 16)

        with sp.Fori(0, FB - 1) as i:
            ffn_units(U_FFN // SLOTS + 2 * i, T * i, T)
        ffn_units(U_FFN // SLOTS + 2 * (FB - 1), T * (FB - 1), P)
        with sp.Fori(0, DC // 2) as i:
            for k in range(2):
                for u in range(DU):
                    s = DU * k + u
                    q = U_DOWN // SLOTS + 2 * DU // SLOTS * i + s // SLOTS
                    rows = w_dn[:, UK * u:min(UK * u + UK, FCH), bass.ds((2 * i + k) * NBLK, NBLK)]
                    unit(q, s % SLOTS, rows)
        sp.wait_ge(S("out_done"), 2)
        sp.dma_start(out_v, x2_sb[:]).then_inc(S("out_in"), 16)
        sp.wait_ge(S("out_in"), 16)

    @block.gpsimd
    def _(pool):
        def mod_store(lo, hi):
            with pool.Fori(lo, hi) as m:
                pool.wait_ge(mod_evac, m + 1)
                for g in range(4):
                    pool.dma_start(mod_d[g, :, bass.ds(m * NBLK, NBLK)], mrow[32 * g:32 * g + 2, :]).then_inc(mod_out, 16)
                pool.wait_ge(mod_out, 64 * (m + 1))

        mod_store(0, 12)
        pool.wait_ge(evac_dve, 12)
        pool.dma_start(xres[:], xv).then_inc(S("xres_in"), 16)
        for r in range(2):
            for v in range(2):
                for g in range(4):
                    at_row = 64 * v + 16 * g
                    pool.dma_start(mvr[at_row:at_row + 16, r], mod_d[g, r, v * D:(v + 1) * D].rearrange("(j p) -> j p", p=P)).then_inc(S("mvr_in"), 16)
        pool.dma_start(mvb[:, :], a["b_mod_2"][0, 0:2 * D].rearrange("(j p) -> j p", p=P)).then_inc(S("mvr_in"), 16)
        pool.wait_ge(S("tr_ps"), TR("merged"))
        pool.dma_start(ctx_sb[:], a["ctx_2"].rearrange("o (r p) d -> p (o r) d", p=P)).then_inc(S("ctx_in"), 16)
        pool.dma_start(wsm[:, :, 0:LR], w_in2[:, :, GLR:GLR + LR]).then_inc(S("wsm_in"), 16)
        pool.dma_start(wsm[:, :, LR:2 * LR], w_in2[:, :, MG:MG + LR]).then_inc(S("wsm_in"), 16)
        pool.dma_start(sx[:, 11, 0:LR], a["mlstm_b_gate_2"].rearrange("o d g h -> o (d g h)")[0].partition_broadcast(P)).then_inc(S("wsm_in"), 16)
        pool.dma_start(wlr[0:LR], a["gla_w_lr_2"].rearrange("o d r k -> r (o d) k")).then_inc(S("wlr_in"), 16)
        pool.dma_start(wlr[LR:LR + 1], a["gla_b_lr_2"]).then_inc(S("wlr_in"), 16)
        pool.wait_ge(evac_dve, 16)
        pool.dma_start(x1_d, xres[:]).then_inc(S("x1_out"), 16)
        mod_store(12, 20)
        pool.wait_ge(S("g_state"), 2)
        pool.dma_start(lsum[:], a["lsum"].rearrange("p (d l t) -> p d l t", d=2, l=LEVELS)).then_inc(S("lsum_in"), 16)
        pool.dma_start(lpair[:], a["lpair"].rearrange("p (d l t) -> p d l t", d=2, l=LEVELS)).then_inc(S("lsum_in"), 16)
        pool.wait_ge(S("y_done"), 1)
        pool.wait_ge(S("x1_out"), 16)
        pool.dma_start(gtr[0:4], mod_d[:, 0, 2 * D:3 * D]).then_inc(S("gtr_in"), 16)
        pool.dma_start(gtr[4:5], a["b_mod_2"][:, 2 * D:3 * D]).then_inc(S("gtr_in"), 16)
        pool.dma_start(xres[:], x1_d).then_inc(S("xres_in2"), 16)
        for v in range(2):
            for g in range(4):
                at_row = 64 * v + 16 * g
                pool.dma_start(mvr[at_row:at_row + 16, 0], mod_d[g, 0, (3 + v) * D:(4 + v) * D].rearrange("(j p) -> j p", p=P)).then_inc(S("mvr_in2"), 16)
        pool.dma_start(mvb[:, :], a["b_mod_2"][0, 3 * D:5 * D].rearrange("(j p) -> j p", p=P)).then_inc(S("mvr_in2"), 16)
        wrows = a["conv_w_2"].rearrange("o y x (f p) -> (o y x f) p", p=P)
        n = 9 * FCH
        for t in range(4):
            k = min(P, n - P * t)
            pool.dma_start(cwr[0:k, t], wrows[P * t:P * t + k, :]).then_inc(S("cw_in"), 16)
        pool.dma_start(cwr[n - 3 * P:n - 3 * P + FCH, 3], a["conv_b_2"].rearrange("o (f p) -> (o f) p", p=P)).then_inc(S("cw_in"), 16)
        mod_store(20, 24)
        pool.wait_ge(evac_dve, 20)
        pool.dma_start(x2_d, xres[:]).then_inc(S("x2_out"), 16)
        pool.wait_ge(S("x2_out"), 16)
        pool.wait_ge(used, U_DOWN)
        pool.dma_start(x2_sb[:], x2_d).then_inc(S("x2_in"), 16)
        pool.dma_start(gfin[:], a["g_final_2"].partition_broadcast(P)).then_inc(S("x2_in"), 16)
        pool.wait_ge(S("f_fv"), FB)
        pool.dma_start(gtr2[0:4], mod_d[:, 0, 5 * D:6 * D]).then_inc(S("gtr2_in"), 16)
        pool.dma_start(gtr2[4:5], a["b_mod_2"][:, 5 * D:6 * D]).then_inc(S("gtr2_in"), 16)

    @block.scalar
    def _(act):
        me = Count(act, S("act_own"))

        def arrived(q):
            if isinstance(q, int) and q < U_FFN // SLOTS:
                return 16 * (q + 1)
            if isinstance(q, int) and q >= U_DOWN // SLOTS:
                return 16 * (q + 1) + 4 * (U_DOWN - U_FFN)
            return 16 * (q + 1) + 16 * (q + 1 - U_FFN // SLOTS) if isinstance(q, int) or in_ffn[0] else 16 * (q + 1)

        in_ffn = [False]

        def split(q, slot):
            act.wait_ge(raw_in[slot], arrived(q))
            if not (isinstance(q, int) and q == 0):
                act.wait_ge(used, 4 * q + slot + 1 - SLOTS)
            act.activation(w_hi[:, slot], raw[:, slot], ACT.Copy).then_inc(hi_done, 1)

        def splits(q, lo, hi):
            for i in range(lo, hi):
                split(q + i // SLOTS, i % SLOTS)

        def exp_ln_rsqrt(ss, n, mean_of, out):
            me(act.activation(out, ss, ACT.Ln, scale=1.0 / mean_of, bias=gbias[:, 0:1]))
            return act.activation(out, out, ACT.Exp, scale=-0.5)

        def turned(use, g):
            G = BU * tr_use[use] + g
            act.wait_ge(S("tr_val"), G + 1)
            act.activation(a_hi[:, UK * g:UK * g + UK], tmpT[:, g % 2], ACT.Copy).then_inc(S("tr_hi"), 1)

        def head(r, h, i):
            hh = HEADS * r + h
            src = br[r % 2]
            if i == 3:
                if r < 2:
                    act.wait_ge(S("h_ss"), 4 * r + h + 1)
                    exp_ln_rsqrt(stat[:, 0:4], 4, HD, stat[:, 4:8]).then_inc(S("h_rs"), 1)
            if i == 5:
                act.wait_ge(S("h_T"), hh + 1)
                qs = vec[:, 52 + 2 * r:53 + 2 * r] if r < 2 else SCALE
                ks = vec[:, 53 + 2 * r:54 + 2 * r] if r < 2 else 1.0
                act.activation(qkgT[:, 0], pA[:, 0:T], ACT.Copy if r == 2 else ACT.Identity, scale=qs)
                act.activation(qkgT[:, 1], pA[:, T:2 * T], ACT.Copy if r == 2 else ACT.Identity,
                               scale=ks).then_inc(S("h_qkT"), 1)
            if i == 6:
                if r < 2:
                    act.wait_ge(S("h_mx"), 4 * r + h + 1)
                    for rt in range(RT):
                        n = P * (rt + 1)
                        ins = act.activation(probs[:, rt, 0:n], pC[:, rt * T:rt * T + n], ACT.Exp,
                                             bias=stat[:, 16 + rt:17 + rt], accum_out=stat[:, 20 + rt:21 + rt])
                    ins.then_inc(S("h_exp"), 1)
                else:
                    act.wait_ge(S("h_L"), hh + 1)
                    me(act.activation(zwork[:, 0], pC[:, 0:3 * P], ACT.Abs))
                    me(act.activation(zwork[:, 0], zwork[:, 0], ACT.Exp, scale=-1.0))
                    act.activation(zwork[:, 0], zwork[:, 0], ACT.Ln, bias=1.0).then_inc(S("h_sp"), 1)
            if i == 8 and r == 2:
                act.wait_ge(S("h_R"), h + 1)
                act.activation(probsT[:, :], pC[:, 0:3 * P], ACT.Exp).then_inc(S("h_PTs"), 1)
            if i == 9:
                act.wait_ge(S("h_y"), hh + 1)
                act.activation(ys_hi[:, hh], yT[:, :], ACT.Copy).then_inc(S("h_yhi"), 1)

        splits(0, 0, 2)
        act.wait_ge(S("x_in"), 16)
        act.wait_ge(S("eps_set"), 1)
        for rt in range(RT):
            act.activation(br[0][:, rt], x_sb[:, rt], ACT.Square, accum_out=stat[:, 32 + rt:33 + rt])
        exp_ln_rsqrt_in = stat[:, 32:34]
        me(act.activation(stat[:, 40:41], gbias[:, 0:1], ACT.Copy))
        exp_ln_rsqrt(exp_ln_rsqrt_in, 2, D, stat[:, 34:36]).then_inc(S("n_rs"), 1)
        act.wait_ge(S("cs_zero"), 1)
        for r in range(2):
            ins = act.activation(cs[:, :, r], pC[:, 56 + 16 * r:72 + 16 * r], ACT.Silu)
        ins.then_inc(S("cs_set"), 1)

        def plain_block(B, dst, q0, hooks=None):
            for i in range(2, 10):
                if B == 0:
                    turned("x", i - 2)
                splits(q0, i, i + 1)
                if hooks:
                    hooks(i)

        def forget_gates(B, i):
            if (B, i) == (2, 6):
                act.wait_ge(S("f_val"), 1)
                me(act.activation(fl[:, 3:5, 0:HEADS], fl[:, 1:3, 0:HEADS], ACT.Abs))
                me(act.activation(fl[:, 3:5, 0:HEADS], fl[:, 3:5, 0:HEADS], ACT.Exp, scale=-1.0))
                act.activation(fl[:, 3:5, 0:HEADS], fl[:, 3:5, 0:HEADS], ACT.Ln, bias=1.0).then_inc(S("f_sp"), 1)

        for seg in range(4):
            for b in range(4):
                B = 4 * seg + b
                plain_block(B, None, 2 * B, lambda i: head(seg - 1, b, i) if seg else forget_gates(B, i))
                act.wait_ge(used, BU * (B + 1))
                if seg < 3:
                    act.activation(br[seg % 2][:, :, b * BW:(b + 1) * BW], gemm_ps[:, B % 2],
                                   ACT.Silu if b == 3 else ACT.Copy).then_inc(evac_act, 1)
                else:
                    act.activation(xn[:, :, b * NBLK:(b + 1) * NBLK], gemm_ps[:, B % 2],
                                   ACT.Sigmoid).then_inc(evac_act, 1)
        splits(U_UP0 // SLOTS, 2, UPU * DC + 2)
        with act.Fori(0, DC) as c:
            q = U_PAIRS // SLOTS + 2 * PAIR // SLOTS * c
            for j in range(2):
                splits(q, PAIR * j + 2, PAIR * j + BU + 2)
                act.wait_ge(used, U_PAIRS + 2 * PAIR * c + PAIR * j + BU)
                act.wait_ge(evac_dve, DC + 2 * c + j)
                act.activation(sg[:], gemm_ps[:, 0], ACT.Sigmoid).then_inc(evac_act, 1)
                splits(q, PAIR * j + BU + 2, PAIR * j + PAIR + 2)

        def sums(src, junk):
            for rt in range(RT):
                act.activation(junk[rt], src[:, rt], ACT.Square, accum_out=stat[:, 32 + rt:33 + rt])
            me(act.activation(stat[:, 40:41], gbias[:, 0:1], ACT.Copy))
            exp_ln_rsqrt(stat[:, 32:34], 2, D, stat[:, 34:36]).then_inc(S("n_rs"), 1)

        def log_sigmoid_part(out, src):
            me(act.activation(out, src, ACT.Abs))
            me(act.activation(out, out, ACT.Exp, scale=-1.0))
            return act.activation(out, out, ACT.Ln, bias=1.0)

        for c in range(DC):
            for i in range(2, 10):
                if c == 0:
                    turned("merged", i - 2)
                splits(U_OUT // SLOTS + 2 * c, i, i + 1)
            if c == 1:
                act.wait_ge(S("ctx_in"), 16)
                act.wait_ge(evac_dve, 12)
                sums(ctx_sb, [xn[:, rt] for rt in range(RT)])
        for cb in range(6):
            for i in range(2, 10):
                if cb == 0:
                    turned("ctx", i - 2)
                splits(U_CTX // SLOTS + 2 * cb, i, i + 1)
                if cb == 1 and i == 3:
                    act.wait_ge(evac_dve, 16)
                    sums(xres, [xn[:, rt] for rt in range(RT)])
            act.wait_ge(used, U_CTX + BU * (cb + 1))
            dst = cm if cb < 3 else cg
            act.activation(dst[:, :, cb % 3 * NBLK:(cb % 3 + 1) * NBLK], gemm_ps[:, (B_CTX + cb) % 2], ACT.Copy).then_inc(evac_act, 1)

        fv8 = lambda t: t.rearrange("p a b -> p (a b)")
        pre = fv8(sx[:, 0:2]).rearrange("p (t d g h) -> p t d g h", t=4, d=2, g=2)
        sp8 = sx[:, 2].rearrange("p (t d h) -> p t d h", t=4, d=2)

        def step(s):
            if s == 13:
                act.wait_ge(S("m_pre"), 1)
                for d in range(2):
                    ins = act.activation(sp8[:, :, d], pre[:, :, d, 1], ACT.Abs)
                me(ins)
                me(act.activation(sx[:, 2], sx[:, 2], ACT.Exp, scale=-1.0))
                act.activation(sx[:, 2], sx[:, 2], ACT.Ln, bias=1.0).then_inc(S("m_sp"), 1)
            if s == 20:
                act.wait_ge(S("m_FM"), 1)
                act.activation(sx[:, 6, 0:16], sx[:, 5, 0:16], ACT.Exp, scale=-1.0).then_inc(S("m_em"), 1)
            if 22 <= s < 30:
                n = s - 22
                act.wait_ge(S("g_dec"), n + 1)
                if n >= 2:
                    act.wait_ge(S("g_la"), n - 1)
                log_sigmoid_part(spd[:, n % 2], ps[:, n % 2]).then_inc(S("g_sp"), 1)
            if 30 <= s < 34:
                m = s - 30
                act.wait_ge(S("g_w"), m + 1)
                if m >= 2:
                    act.wait_ge(S("g_kend"), m - 1)
                act.activation(kexp[m % 2][:, :], (pC, pA)[m % 2], ACT.Exp).then_inc(S("g_kexp"), 1)
            if 34 <= s < 66:
                h, i = (s - 34) // 8, (s - 34) % 8 + 2
                if i == 2:
                    act.wait_ge(S("m_T"), h + 1)
                    act.activation(mkT[:, :], pA, ACT.Copy, scale=SCALE).then_inc(S("m_kT"), 1)
                if i in (5, 7):
                    act.wait_ge(S("m_arg"), 2 * h + (i == 7) + 1)
                    act.activation(mpT[:, :], mpT[:, :], ACT.Exp, scale=-1.0).then_inc(S("m_exp"), 1)
                if i == 9:
                    act.wait_ge(S("m_num"), 2 * h + 2)
                    act.activation(sx[:, 7, 0:4], pC[:, 0:4], ACT.Abs).then_inc(S("m_den"), 1)
            if s == 66:
                act.wait_ge(S("g_S"), 1)
                act.activation(state[:, 0].rearrange("p h v -> p (h v)"), ps[:, 0:2].rearrange("p a b -> p (a b)"),
                               ACT.Copy).then_inc(S("g_state"), 1)
            if 68 <= s <= 100:
                gla_consume(s - 68)
            if s >= 77 and (s - 77) % 8 == 0:
                h = (s - 77) // 8
                act.wait_ge(S("g_o"), 4 * h + 4)
                act.activation(y[:, :, h * GDV:(h + 1) * GDV], pD.rearrange("p (r v) -> p r v", r=RT),
                               ACT.Copy).then_inc(S("g_y"), 1)

        turn = [0]

        def take():
            act.wait_ge(S("g_ps"), turn[0] + 1)
            turn[0] += 1
            return ps[:, (turn[0] - 1) % 2]

        def gla_consume(k):
            gc, j = k // 2, k % 2
            h, c = gc // 4, gc % 4
            if j == 0 and gc and c % 2 == 0:
                act.activation(sc[:, 2], take()[:, 0:P], ACT.Copy).then_inc(S("g_free"), 1)
            if k == 32:
                return
            if j == 0 and c == 0:
                bank = take()
                if h:
                    act.wait_ge(S("g_mult"), 8 * h)
                act.activation(gqT[:, 0], bank[:, 0:T], ACT.Copy, scale=SCALE)
                act.activation(gqT[:, 1], bank[:, T:2 * T], ACT.Copy).then_inc(S("g_free"), 1)
            if j == 0:
                bank = take()
                if gc >= 2:
                    act.wait_ge(S("g_o"), gc - 1)
                act.activation(cr[:, c % 2], bank[:, 0:P], ACT.Exp)
                act.activation(fq[:, gc % 2], bank[:, P:2 * P], ACT.Exp).then_inc(S("g_free"), 1)
            bank = take()
            if k >= 2:
                act.wait_ge(S("g_sc"), k - 1)
            act.activation(ek[:, k % 2].rearrange("p l t -> p (l t)"), bank, ACT.Exp).then_inc(S("g_free"), 1)

        for xb in range(12):
            for i in range(2, 10):
                if xb == 0:
                    turned("x1", i - 2)
                splits(U_X // SLOTS + 2 * xb, i, i + 1)
                step(8 * xb + i)
            act.wait_ge(used, U_X + BU * (xb + 1))
            dst = (xm, xg, gates)[xb // 4][:, :, xb % 4 * NBLK:(xb % 4 + 1) * NBLK]
            if xb == 0:
                act.wait_ge(S("x1_out"), 16)
            act.activation(dst, gemm_ps[:, (B_X + xb) % 2],
                           ACT.Copy if xb < 8 else ACT.Silu if xb < 10 else ACT.Sigmoid).then_inc(evac_act, 1)
        for s in range(98, 103):
            step(s)
        act.wait_ge(S("m_y"), HEADS)
        me(act.activation(stat[:, 40:41], gbias[:, 0:1], ACT.Copy))
        for rt in range(RT):
            for g in range(8):
                act.activation(xg[:, rt, g * GDV:(g + 1) * GDV], y[:, rt, g * GDV:(g + 1) * GDV], ACT.Square, accum_out=sx[:, 8, 8 * rt + g:8 * rt + g + 1])
        me(act.activation(stat[:, 40:41], gbias[:, 0:1], ACT.Copy))
        exp_ln_rsqrt(sx[:, 8, 0:16], 16, GDV, sx[:, 9, 0:16]).then_inc(S("y_rs"), 1)
        for c in range(DC):
            for i in range(2, 10):
                if c == 0:
                    turned("y", i - 2)
                splits(U_OUT2 // SLOTS + 2 * c, i, i + 1)
                n = 8 * c + i - 8
                if 0 <= n < DC:
                    act.wait_ge(S("gt_ps"), n + 1)
                    act.activation(gtb[:, n * NBLK:(n + 1) * NBLK], pC, ACT.Copy, scale=-1.0).then_inc(S("gt_in"), 1)
        act.wait_ge(evac_dve, 20)
        sums(xres, [xn[:, rt] for rt in range(RT)])

        def ffn_hook(b, i, par, start, finish, nf=2):
            if i == 3 and finish:
                act.wait_ge(S("f_acc"), b - 1)
                act.activation(sil[:, 0:finish], acc[:, 0:finish], ACT.Silu).then_inc(S("f_sil"), 1)
            if i == 5 and finish:
                act.wait_ge(S("f_fv"), b - 1)
                act.activation(ft_hi[:, bass.ds((b - 2) * 2, finish)], fv[:, 0:finish], ACT.Copy).then_inc(S("f_hi"), 1)
            if i == 6 and start:
                act.wait_ge(S("f_T"), b)
                src = pA[:, 0:start * T].rearrange("p (f y x) -> p f y x", f=start, y=4)
                for f in range(start):
                    ins = act.activation(gp[:, f, 1:5, 1:65], src[:, f], ACT.Copy)
                me(ins)
                for f in range(start):
                    fc = (b - 1) * 2 + f
                    ins = act.activation(acc[:, f].rearrange("p (y x) -> p y x", y=4), gp[:, f, 0:4, 0:64], ACT.Identity,
                                         scale=cw[:, bass.ds(fc, 1)], bias=cw[:, bass.ds(9 * FCH + fc, 1)])
                ins.then_inc(S("f_tap0"), 1)

        def ffn_block(b, par, start=2, finish=2, k0=0):
            for i in range(2, 10):
                if isinstance(b, int) and b == 0:
                    turned("x2", i - 2)
                splits(U_FFN // SLOTS + 2 * b, i, i + 1)
                ffn_hook(b, i, par, start, finish)
            act.wait_ge(used, U_FFN + BU * (b + 1))
            if start:
                act.wait_ge(S("f_T"), b)
            act.activation(ub[:, par], gemm_ps[:, par], ACT.Copy).then_inc(evac_act, 1)

        ffn_block(0, 0, 0, 0)
        act.wait_ge(S("gp_zero"), 2)
        ffn_block(1, 1, 2, 0)
        first = me.n
        in_ffn[0] = True
        with act.Fori(0, 9) as n:
            me.iteration(first, 2 * n)
            for k in range(2):
                ffn_block(2 * n + 2 + k, k)
        me.iteration(first + 18, 0)
        ffn_block(20, 0)
        ffn_block(21, 1)
        for i in range(2, 10):
            splits(U_DOWN // SLOTS, i, i + 1)
            ffn_hook(22, i, 0, 1, 2)
        for i in range(2, 10):
            splits(U_DOWN // SLOTS + 2, i, i + 1)
            ffn_hook(23, i, 1, 0, 1)
        splits(U_DOWN // SLOTS, 18, DU + 2)
        act.wait_ge(S("gt_ps"), DC + 1)
        act.activation(gt2b[:, :], ps[:].rearrange("p a b -> p (a b)"), ACT.Copy, scale=-1.0).then_inc(S("gt_in"), 1)
        splits(U_DOWN // SLOTS, DU + 2, DC * DU)
        act.wait_ge(evac_dve, 24)
        sums(x2_sb, [squares[:, rt] for rt in range(RT)])

    @block.vector
    def _(dve):
        me = Count(dve, S("dve_own"))

        def split(q, slot):
            dve.wait_ge(hi_done, 4 * q + slot + 1)
            dve.tensor_tensor(w_lo[:, slot], raw[:, slot], w_hi[:, slot].bitcast(F32), ALU.subtract).then_inc(lo_done, 1)

        def splits(q, lo, hi):
            for i in range(lo, hi):
                split(q + i // SLOTS, i % SLOTS)

        def newton(ss, r, mean_of, t):
            me(dve.tensor_scalar(t, ss, 1.0 / mean_of, EPS, ALU.mult, ALU.add))
            me(dve.tensor_tensor(t, t, r, ALU.mult))
            me(dve.tensor_tensor(t, t, r, ALU.mult))
            me(dve.tensor_scalar(t, t, -0.5, 1.5, ALU.mult, ALU.add))
            me(dve.tensor_tensor(r, r, t, ALU.mult))

        def turned(use, g, scale=None, bias=None):
            G = BU * tr_use[use] + g
            dve.wait_ge(S("tr_ps"), G + 1)
            if g >= 2:
                dve.wait_ge(S("tr_hi"), G - 1)
            bank = ps[:, g % 2]
            if scale is None:
                dve.tensor_copy(tmpT[:, g % 2].rearrange("p a b -> p (a b)"), bank).then_inc(S("tr_val"), 1)
            else:
                for k in range(UK):
                    kc = UK * g + k
                    b = bias[:, kc:kc + 1] if bias is not None else None
                    ins = dve.tensor_scalar(tmpT[:, g % 2, k], bank[:, k * T:(k + 1) * T], scale[:, kc:kc + 1], b,
                                            ALU.mult, ALU.add if bias is not None else ALU.bypass)
                ins.then_inc(S("tr_val"), 1)

        def turned_rest(use, g):
            dve.wait_ge(S("tr_hi"), BU * tr_use[use] + g + 1)
            dve.tensor_tensor(a_lo[:, UK * g:UK * g + UK], tmpT[:, g % 2],
                              a_hi[:, UK * g:UK * g + UK].bitcast(F32), ALU.subtract).then_inc(S("tr_lo"), 1)

        def diagonals():
            newton(stat[:, 32:34], stat[:, 34:36], D, stat[:, 36:38])
            for rt in range(RT):
                ins = dve.tensor_scalar(diag[:, rt], ident, stat[:, 34 + rt:35 + rt], None, ALU.mult)
            ins.then_inc(S("diag_set"), 1)

        def head(r, h, i):
            hh = HEADS * r + h
            src = br[r % 2]
            qk = src[:, :, 0:2 * BW].rearrange("p r (t c) -> p r t c", t=2)[:, :, :, h * HD:(h + 1) * HD]
            if i == 2:
                if hh == 0:
                    dve.wait_ge(evac_act, 4)
                if h == 0 and r > 0:
                    dve.wait_ge(evac_act, 4 * (r + 1))
                if r < 2:
                    if hh > 0:
                        dve.wait_ge(S("h_T"), hh)
                    for rt in range(RT):
                        ins = dve.tensor_tensor(qkn[:, rt], qk[:, rt], qk[:, rt], ALU.mult)
                    me(ins)
                    dve.tensor_reduce(stat[:, 0:4], qkn[:].rearrange("p r t c -> p (r t) c"), AX_X,
                                      ALU.add).then_inc(S("h_ss"), 1)
            if i == 4:
                if r < 2:
                    dve.wait_ge(S("h_rs"), 4 * r + h + 1)
                    newton(stat[:, 0:4], stat[:, 4:8], HD, stat[:, 8:12])
                    for rt in range(RT):
                        for t in range(2):
                            c = 2 * rt + t
                            ins = dve.tensor_scalar(qkn[:, rt, t], qk[:, rt, t], stat[:, 4 + c:5 + c], None, ALU.mult)
                    ins.then_inc(S("h_pre"), 1)
            if i == 5:
                dve.wait_ge(S("h_T"), hh + 1)
                dve.tensor_copy(qkgT[:, 2], pB[:, 0:T]).then_inc(S("h_gT"), 1)
            if i == 6:
                dve.wait_ge(S("h_L"), hh + 1)
                if r < 2:
                    for rt in range(RT):
                        ins = dve.tensor_reduce(stat[:, 18 + rt:19 + rt], pC[:, rt * T:rt * T + P * (rt + 1)], AX_X, ALU.max)
                    me(ins)
                    dve.tensor_scalar(stat[:, 16:18], stat[:, 18:20], -1.0, None, ALU.mult).then_inc(S("h_mx"), 1)
            if i == 7:
                if r < 2:
                    dve.wait_ge(S("h_exp"), 4 * r + h + 1)
                    me(dve.reciprocal(stat[:, 22:24], stat[:, 20:22]))
                    for rt in range(RT):
                        n = P * (rt + 1)
                        ins = dve.tensor_scalar(probs[:, rt, 0:n], probs[:, rt, 0:n], stat[:, 22 + rt:23 + rt], None, ALU.mult)
                    ins.then_inc(S("h_p"), 1)
                else:
                    dve.wait_ge(S("h_sp"), h + 1)
                    me(dve.scalar_tensor_tensor(out=zwork[:, 1], in0=pC[:, 0:3 * P], scalar=0.0, in1=zwork[:, 0],
                                                op0=ALU.max, op1=ALU.add))
                    dve.tensor_tensor(zwork[:, 1], zwork[:, 1], C("strict"), ALU.mult).then_inc(S("h_p"), 1)
            if i == 8 and r < 2:
                dve.wait_ge(S("h_PT"), 4 * r + h + 1)
                dve.tensor_copy(probsT[:, :], pA[:, 0:3 * P]).then_inc(S("h_PTs"), 1)
            if i == 9:
                dve.wait_ge(S("h_O"), hh + 1)
                if hh > 0:
                    dve.wait_ge(S("h_yhi"), hh)
                dve.tensor_tensor(yT[:, :], pB[:, 0:T], qkgT[:, 2], ALU.mult).then_inc(S("h_y"), 1)
                dve.wait_ge(S("h_yhi"), hh + 1)
                dve.tensor_tensor(ys_lo[:, hh], yT[:, :], ys_hi[:, hh].bitcast(F32), ALU.subtract).then_inc(S("h_ylo"), 1)

        def mod_copy(m):
            dve.wait_ge(mod_used, BU * (m + 1))
            if not (isinstance(m, int) and m == 0):
                dve.wait_ge(mod_out, 64 * m)
            dve.tensor_copy(mrow[:, :], pD).then_inc(mod_evac, 1)

        dve.memset(gbias[:, :], EPS).then_inc(S("eps_set"), 1)
        dve.memset(wf[:], 0.0).then_inc(S("wf_zero"), 1)
        dve.wait_ge(S("vec_in"), 144)
        N = 2 * MAX_REL + 1
        dve.tensor_copy(rel_ext[:, 0:N], rrows[0:HEADS, 0:N])
        dve.tensor_copy(rel_ext[:, N:384], rrows[0:HEADS, N - 1:N].to_broadcast([HEADS, 384 - N])).then_inc(S("rel_ext"), 1)
        dve.wait_ge(S("n_vecT"), 1)
        me(dve.tensor_copy(vec[:, 0:52], pC[:, 0:52]))
        dve.tensor_copy(vec[:, 56:60], pC[:, 52:56])
        dve.memset(cs[:], 0.0).then_inc(S("cs_zero"), 1)
        for r in range(2):
            dve.tensor_scalar(vec[:, 52 + 2 * r:53 + 2 * r], vec[:, 48 + 2 * r:49 + 2 * r], SCALE, None, ALU.mult)
            me(dve.tensor_copy(vec[:, 53 + 2 * r:54 + 2 * r], vec[:, 49 + 2 * r:50 + 2 * r]))
        dve.wait_ge(S("n_rs"), 1)
        diagonals()
        splits(0, 0, 2)

        def forget_gates(B, i):
            if (B, i) == (2, 3):
                dve.wait_ge(S("f_parts"), 1)
                dve.tensor_copy(fparts[:, :], pC[:, 0:T]).then_inc(S("f_copied"), 1)
            if (B, i) == (2, 5):
                dve.wait_ge(S("f_ps"), 1)
                dve.tensor_tensor(fl[:, 1:3, 0:HEADS], pC[:, T:T + 64].rearrange("p (r h) -> p r h", r=RT)[:, :, 0:HEADS],
                                  fl[:, 0:1, 0:HEADS].to_broadcast([P, RT, HEADS]), ALU.add).then_inc(S("f_val"), 1)
            if (B, i) == (2, 8):
                dve.wait_ge(S("f_sp"), 1)
                dve.scalar_tensor_tensor(out=fl[:, 5:7, 0:HEADS], in0=fl[:, 1:3, 0:HEADS], scalar=0.0,
                                         in1=fl[:, 3:5, 0:HEADS], op0=ALU.min, op1=ALU.subtract).then_inc(S("f_log"), 1)
            if (B, i) == (3, 5):
                dve.wait_ge(S("f_c"), 1)
                dve.tensor_copy(cneg[0:HEADS, :], pC[0:HEADS, 0:T]).then_inc(S("f_cneg"), 1)

        for seg in range(4):
            for b in range(4):
                B = 4 * seg + b
                for i in range(2, 10):
                    if B == 0:
                        turned("x", i - 2, vec[:, 0:16])
                    splits(2 * B, i, i + 1)
                    if B == 0:
                        turned_rest("x", i - 2)
                    if seg:
                        head(seg - 1, b, i)
                    else:
                        forget_gates(B, i)
                if B % 2:
                    mod_copy(B // 2)

        for c in range(DC):
            splits(U_UP0 // SLOTS, UPU * c + 2, UPU * c + 4)
            dve.wait_ge(used, U_UP0 + UPU * (c + 1))
            cols = slice(c * NBLK, (c + 1) * NBLK)
            dve.tensor_tensor(merged[:, :, cols], gemm_ps[:, (B_UP0 + c) % 2], xn[:, :, cols], ALU.mult).then_inc(evac_dve, 1)
        first = me.n
        with dve.Fori(0, DC) as c:
            me.iteration(first, 2 * c)
            q = U_PAIRS // SLOTS + 2 * PAIR // SLOTS * c
            for j in range(2):
                splits(q, PAIR * j + 2, PAIR * j + PAIR + 2)
                dve.wait_ge(evac_act, 16 + 2 * c + j + 1)
                dve.wait_ge(used, U_PAIRS + 2 * PAIR * c + PAIR * (j + 1))
                me(dve.tensor_tensor(sg[:], gemm_ps[:, 1], sg[:], ALU.mult))
                m = merged[:, :, bass.ds(c * NBLK, NBLK)]
                dve.tensor_tensor(m, m, sg[:], ALU.add).then_inc(evac_dve, 1)
            mod_copy(8 + c)
        me.iteration(first + 2 * DC, 0)
        for c in range(DC):
            for i in range(2, 10):
                if c == 0:
                    turned("merged", i - 2)
                splits(U_OUT // SLOTS + 2 * c, i, i + 1)
                if c == 0:
                    turned_rest("merged", i - 2)
            dve.wait_ge(used, U_OUT + BU * (c + 1))
            if c == 0:
                dve.wait_ge(S("xres_in"), 16)
            xs = xres[:, :, c * NBLK:(c + 1) * NBLK]
            dve.tensor_tensor(xs, gemm_ps[:, c % 2], xs, ALU.add).then_inc(evac_dve, 1)
            if c == 1:
                dve.wait_ge(S("n_rs"), 2)
                diagonals()

        def mod_vectors(bank, cols, g, bias):
            both = vec[:, cols:cols + 32]
            dve.tensor_reduce(both.rearrange("p (v j) -> p v j", v=2),
                              bank.rearrange("p (v g j) -> p v j g", v=2, g=4), AX_X, ALU.add)
            me(dve.engine_nop())
            me(dve.tensor_tensor(both, bias, both, ALU.add))
            s = vec[:, cols + 16:cols + 32]
            me(dve.scalar_tensor_tensor(out=s, in0=s, scalar=1.0, in1=g, op0=ALU.add, op1=ALU.mult))

        dve.wait_ge(S("mv_ps"), 1)
        for r in range(2):
            mod_vectors(pA[:, r * P:(r + 1) * P], 60 + 32 * r, vec[:, 16:32], pA[:, 2 * P:2 * P + 32])
        for j in range(2):
            for kc in range(4):
                dve.tensor_copy(vec[:, 8 * j + 2 * kc:8 * j + 2 * kc + 2], vec[:, 56 + 2 * j:58 + 2 * j])
        me(dve.engine_nop())
        dve.engine_nop().then_inc(S("mv_done"), 1)

        def small_parts(n):
            dve.wait_ge(S("s_ps"), n + 1)
            dve.tensor_copy(zparts[:, :], pC[:, 0:T]).then_inc(S("s_parts"), 1)

        def small_sums(n):
            dve.wait_ge(S("s_tok"), n + 1)
            dve.tensor_copy(sm[:, 2 * n:2 * n + 2], pC[:, T:T + 64].rearrange("p (r c) -> p r c", r=RT)).then_inc(S("sm_in"), 1)
            dve.wait_ge(S("sm_in"), n + 1)

        for cb in range(6):
            for i in range(2, 10):
                if cb == 0:
                    turned("ctx", i - 2, vec[:, 108:124], vec[:, 92:108])
                splits(U_CTX // SLOTS + 2 * cb, i, i + 1)
                if cb == 0:
                    turned_rest("ctx", i - 2)
                if cb == 1 and i == 3:
                    small_parts(0)
                if cb == 1 and i == 5:
                    small_sums(0)
                if cb == 2 and i == 4:
                    dve.wait_ge(S("n_rs"), 3)
                    diagonals()
            mod_copy(12 + cb)

        pre_all = sx[:, 0:2].rearrange("p a b -> p (a b)")
        pre = pre_all.rearrange("p (t d g h) -> p t d g h", t=4, d=2, g=2)
        t8 = lambda row, t=4: sx[:, row, 0:8 * t].rearrange("p (t d h) -> p t d h", t=t, d=2)
        G8, FM = t8(4), t8(5, 2)
        bc = lambda ap, n: ap.rearrange("p (o t) -> p o t", o=1).to_broadcast([P, n, P])

        def step(s):
            if s == 10:
                small_parts(1)
            if s == 12:
                small_sums(1)
                dve.wait_ge(S("wsm_in"), 48)
                dve.tensor_tensor(pre_all.rearrange("p (t c) -> p t c", t=4), sm[:, :, LR:2 * LR],
                                  sx[:, 11:12, 0:LR].to_broadcast([P, 4, LR]), ALU.add).then_inc(S("m_pre"), 1)
            if s == 14:
                dve.wait_ge(S("m_sp"), 1)
                for d in range(2):
                    ins = dve.scalar_tensor_tensor(out=t8(3)[:, :, d], in0=pre[:, :, d, 1], scalar=0.0, in1=t8(2)[:, :, d],
                                                   op0=ALU.min, op1=ALU.subtract)
                ins.then_inc(S("m_lf"), 1)
            if s == 16:
                dve.wait_ge(S("m_F"), 1)
                F = pC[:, P:P + 32].rearrange("p (t d h) -> p t d h", t=4, d=2)
                for d in range(2):
                    for r, sign in ((0, NORMALIZER), (2, -NORMALIZER)):
                        dve.scalar_tensor_tensor(out=G8[:, r:r + 2, d], in0=F[:, r:r + 2, d], scalar=sign,
                                                 in1=pre[:, r:r + 2, d, 0], op0=ALU.mult, op1=ALU.add)
                me(dve.tensor_scalar(FM, F[:, 2:4], NORMALIZER, None, ALU.mult))
                dve.engine_nop().then_inc(S("m_G"), 1)
            if s == 17:
                dve.wait_ge(S("m_GT"), 1)
                me(dve.tensor_copy(grows[:, :], pA[0:8, :]))
                me(dve.tensor_reduce(stat[0:8, 44:45], grows[:, 0:T], AX_X, ALU.max))
                x = grows[:, T:2 * T]
                dve.tensor_tensor_scan(mrows[:, 0], x, x, stat[0:8, 44:45], ALU.max, ALU.max)
                me(dve.tensor_tensor_scan(mrows[:, 1, ::-1], x[:, ::-1], x[:, ::-1], stat[0:8, 44:45], ALU.max, ALU.max))
                dve.engine_nop().then_inc(S("m_rows"), 1)
            if s == 19:
                dve.wait_ge(S("m_MT"), 1)
                M = pB[:, 0:32].rearrange("p (r w d h) -> p r w d h", r=RT, w=2, d=2)
                for d in range(2):
                    ins = dve.tensor_tensor(FM[:, :, d], M[:, :, d, d], FM[:, :, d], ALU.add)
                ins.then_inc(S("m_FM"), 1)
            if s == 20:
                me(dve.memset(glrT[:, :], 1.0))
                dve.wait_ge(S("g_glr"), 1)
                dve.tensor_copy(glrT[0:LR, :], pA[0:LR, :]).then_inc(S("g_glrT"), 1)
            if 23 <= s < 31:
                n = s - 23
                t, d = n // 2, n % 2
                dve.wait_ge(S("g_sp"), n + 1)
                dst = y[:, t, 2 * BW + d * BW:2 * BW + (d + 1) * BW] if t < 2 else la[:, t - 2, d]
                dve.scalar_tensor_tensor(out=dst, in0=ps[:, n % 2], scalar=0.0, in1=spd[:, n % 2],
                                         op0=ALU.min, op1=ALU.subtract).then_inc(S("g_la"), 1)
            if 31 <= s < 35:
                m = s - 31
                t, d = m // 2, m % 2
                dve.wait_ge(S("g_kexp"), m + 1)
                dve.tensor_tensor(y[:, t, d * BW:(d + 1) * BW], kexp[m % 2][:, :], cg[:, t, 0:BW], ALU.mult).then_inc(S("g_kend"), 1)
            if 34 <= s < 66:
                h, i = (s - 34) // 8, (s - 34) % 8 + 2
                if i == 2:
                    dve.wait_ge(S("m_T"), h + 1)
                    dve.tensor_copy(mqT[:, :], pB[:, 0:T]).then_inc(S("m_qT"), 1)
                if i in (4, 7):
                    d = i == 7
                    dve.wait_ge(S("m_QK"), h + 1)
                    if h or d:
                        dve.wait_ge(S("m_num"), 2 * h + d)
                    M = pC[:, d * T:(d + 1) * T]
                    for n, (t, lo, hi) in enumerate(tiles[d]):
                        at0 = 2 * P * n
                        ins = dve.tensor_scalar(mpT[:, at0:at0 + hi - lo], M[:, lo:hi], G8[:, t, d, h:h + 1], 0.0,
                                                ALU.subtract, ALU.max)
                    ins.then_inc(S("m_arg"), 1)
                if i in (5, 8):
                    d = i == 8
                    dve.wait_ge(S("m_exp"), 2 * h + d + 1)
                    qk = ps[:, 0:2].rearrange("p a b -> p (a b)")
                    for n, (t, lo, hi) in enumerate(tiles[d]):
                        at0 = 2 * P * n
                        dst = mpT[:, at0:at0 + hi - lo]
                        ins = dve.tensor_tensor(dst, qk[:, t * T + lo:t * T + hi], dst, ALU.mult)
                    me(ins)
                    a0, a1 = ((4, 6), (5, 6))[d]
                    for q in (a0, a1):
                        dst = mpT[:, q * P:(q + 1) * P]
                        ins = dve.tensor_tensor(dst, dst, C("le" if d else "ge"), ALU.mult)
                    ins.then_inc(S("m_s"), 1)
                if i == 9:
                    dve.wait_ge(S("m_den"), h + 1)
                    dve.wait_ge(S("m_em"), 1)
                    em = t8(6, 2)
                    for d in range(2):
                        ins = dve.tensor_tensor(sx[:, 7, 4 + 2 * d:6 + 2 * d], sx[:, 7, 2 * d:2 * d + 2], em[:, :, d, h], ALU.max)
                    me(ins)
                    me(dve.reciprocal(sx[:, 10, 0:4], sx[:, 7, 4:8]))
                    for d in range(2):
                        for rt in range(RT):
                            dst = y[:, rt, D // 2 + h * GDV:D // 2 + (h + 1) * GDV]
                            src = (pD, pA)[d][:, rt * GDV:(rt + 1) * GDV]
                            r = sx[:, 10, 2 * d + rt:2 * d + rt + 1]
                            if d == 0:
                                ins = dve.tensor_scalar(dst, src, r, None, ALU.mult)
                            else:
                                ins = dve.scalar_tensor_tensor(out=dst, in0=src, scalar=r, in1=dst, op0=ALU.mult, op1=ALU.add)
                        if d == 0:
                            me(ins)
                    ins.then_inc(S("m_y"), 1)
            if s == 66:
                dve.wait_ge(S("g_S"), 1)
                dve.tensor_copy(state[:, 1].rearrange("p h v -> p (h v)"), ps[:, 2:4].rearrange("p a b -> p (a b)")).then_inc(S("g_state"), 1)
            if 69 <= s < 101:
                gla_mult(s - 69)
            if 70 <= s < 102:
                gla_mask(s - 70)

        tiles = (((0, 0, T), (1, 0, T), (2, 0, T), (3, P, T)), ((0, 0, T), (1, 0, T), (3, 0, T), (2, 0, P)))

        def gla_mult(k):
            gc, j = k // 2, k % 2
            h, c = gc // 4, gc % 4
            d, rt = c // 2, c % 2
            base_turn = 15 * h + (1, 4, 8, 11)[c]
            q, kk = gqT[:, 0, rt * P:(rt + 1) * P], gqT[:, 1, rt * P:(rt + 1) * P]
            if j == 0:
                dve.wait_ge(S("g_free"), base_turn + 1)
                dve.tensor_tensor(cr[:, rt], cr[:, rt], q if d != rt else kk, ALU.mult)
                dve.tensor_tensor(fq[:, gc % 2], fq[:, gc % 2], q, ALU.mult).then_inc(S("g_f"), 1)
            dve.wait_ge(S("g_free"), base_turn + 2 + j)
            if k:
                dve.wait_ge(S("g_sc"), k)
            dve.tensor_tensor(rk[:], ek[:, k % 2], bc(kk, 4), ALU.mult)
            dve.tensor_tensor(ek[:, k % 2], ek[:, k % 2], bc(q, 4), ALU.mult).then_inc(S("g_mult"), 1)

        def gla_mask(k):
            gc, j = k // 2, k % 2
            d = gc % 4 // 2
            if k == 0:
                dve.wait_ge(S("lsum_in"), 32)
            dve.wait_ge(S("g_sc"), k + 1)
            if k:
                dve.wait_ge(S("g_mask"), k)
            dve.tensor_tensor(masked[:], pC.rearrange("p (l t) -> p l t", l=4), lpair[:, d, 4 * j:4 * j + 4],
                              ALU.mult).then_inc(S("g_masked"), 1)
            dve.wait_ge(S("g_masked"), k + 1)
            if gc and j == 0:
                dve.wait_ge(S("g_o"), gc)
            ins = dve.tensor_reduce(sc[:, j], masked[:].rearrange("p l t -> p t l"), AX_X, ALU.add)
            if j:
                me(ins)
                ins = dve.tensor_tensor(sc[:, 0], sc[:, 0], sc[:, 1], ALU.add)
            ins.then_inc(S("g_mask"), 1)

        for xb in range(12):
            for i in range(2, 10):
                if xb == 0:
                    turned("x1", i - 2, vec[:, 76:92], vec[:, 60:76])
                splits(U_X // SLOTS + 2 * xb, i, i + 1)
                if xb == 0:
                    turned_rest("x1", i - 2)
                step(8 * xb + i)
            if xb in (1, 3):
                mod_copy(18 + xb // 2)
        for s in range(98, 103):
            step(s)
        dve.wait_ge(S("y_rs"), 1)
        newton(sx[:, 8, 0:16], sx[:, 9, 0:16], GDV, sx[:, 10, 0:16])
        dve.wait_ge(evac_act, 42)
        for rt in range(RT):
            for g in range(8):
                cols = slice(g * GDV, (g + 1) * GDV)
                ins = dve.scalar_tensor_tensor(out=y[:, rt, cols], in0=y[:, rt, cols], scalar=sx[:, 9, 8 * rt + g:8 * rt + g + 1],
                                               in1=gates[:, rt, cols], op0=ALU.mult, op1=ALU.mult)
        ins.then_inc(S("y_done"), 1)
        for c in range(DC):
            for i in range(2, 10):
                if c == 0:
                    turned("y", i - 2, vec[:, 0:16])
                splits(U_OUT2 // SLOTS + 2 * c, i, i + 1)
                if c == 0:
                    turned_rest("y", i - 2)
                if c == 0 and i == 6:
                    dve.wait_ge(S("mv_ps"), 2)
                    mod_vectors(pC[:, 0:P], 124, vec[:, 32:48], pC[:, P:P + 32])
                    dve.engine_nop().then_inc(S("mv_done"), 1)
            dve.wait_ge(S("gt_in"), c + 1)
            if c == 0:
                dve.wait_ge(S("xres_in2"), 16)
            dve.wait_ge(used, U_OUT2 + BU * (c + 1))
            cols = slice(c * NBLK, (c + 1) * NBLK)
            for rt in range(RT):
                ins = dve.tensor_tensor(sg[:, rt], gemm_ps[:, c % 2, rt], gtb[:, cols], ALU.mult)
            me(ins)
            dve.tensor_tensor(xres[:, :, cols], xres[:, :, cols], sg[:], ALU.add).then_inc(evac_dve, 1)
            mod_copy(20 + c)
        dve.wait_ge(S("cw_ps"), 1)
        dve.tensor_copy(cw[:, :], pC[:, 0:10 * FCH]).then_inc(S("gp_zero"), 1)
        dve.wait_ge(S("n_rs"), 4)
        diagonals()

        def ffn_hook(b, i, par, start, finish):
            if i == 4 and finish:
                dve.wait_ge(S("f_sil"), b - 1)
                dve.tensor_tensor(fv[:, 0:finish], sil[:, 0:finish], pB[:, 0:finish * T].rearrange("p (f t) -> p f t", f=finish),
                                  ALU.mult).then_inc(S("f_fv"), 1)
            if i == 6 and finish:
                dve.wait_ge(S("f_hi"), b - 1)
                at_f = bass.ds((b - 2) * 2, finish)
                dve.tensor_tensor(ft_lo[:, at_f], fv[:, 0:finish], ft_hi[:, at_f].bitcast(F32), ALU.subtract).then_inc(S("f_lo"), 1)
            if i >= 7 and start:
                if i == 7:
                    dve.wait_ge(S("f_tap0"), b)
                for tap in {7: (1, 2, 3), 8: (4, 5, 6), 9: (7, 8)}[i]:
                    dy, dx = tap // 3, tap % 3
                    for f in range(start):
                        a_f = acc[:, f].rearrange("p (y x) -> p y x", y=4)
                        ins = dve.scalar_tensor_tensor(out=a_f, in0=gp[:, f, dy:dy + 4, dx:dx + 64],
                                                       scalar=cw[:, bass.ds(tap * FCH + (b - 1) * 2 + f, 1)], in1=a_f,
                                                       op0=ALU.mult, op1=ALU.add)
                    if tap < 8:
                        me(ins)
                    else:
                        ins.then_inc(S("f_acc"), 1)

        def ffn_block(b, par, start=2, finish=2):
            for i in range(2, 10):
                first = isinstance(b, int) and b == 0
                if first:
                    turned("x2", i - 2, vec[:, 140:156], vec[:, 124:140])
                splits(U_FFN // SLOTS + 2 * b, i, i + 1)
                if first:
                    turned_rest("x2", i - 2)
                ffn_hook(b, i, par, start, finish)

        ffn_block(0, 0, 0, 0)
        dve.memset(gp[:], 0.0).then_inc(S("gp_zero"), 1)
        ffn_block(1, 1, 2, 0)
        dve.wait_ge(S("x2_out"), 16)
        first = me.n
        with dve.Fori(0, 9) as n:
            me.iteration(first, 14 * n)
            for k in range(2):
                ffn_block(2 * n + 2 + k, k)
        me.iteration(first + 14 * 9, 0)
        ffn_block(20, 0)
        ffn_block(21, 1)
        for i in range(2, 10):
            splits(U_DOWN // SLOTS, i, i + 1)
            ffn_hook(22, i, 0, 1, 2)
        for i in range(2, 10):
            splits(U_DOWN // SLOTS + 2, i, i + 1)
            ffn_hook(23, i, 1, 0, 1)
        tmp = tmp_dn
        for c in range(DC):
            splits(U_DOWN // SLOTS, 18 if c == 0 else DU * c + 2, min(DU * (c + 1) + 2, DC * DU))
            if c == 0:
                dve.wait_ge(S("gt_in"), DC + 1)
                dve.wait_ge(S("x2_in"), 32)
            dve.wait_ge(used, U_DOWN + DU * (c + 1))
            cols = slice(c * NBLK, (c + 1) * NBLK)
            for rt in range(RT):
                ins = dve.tensor_tensor(tmp[:, rt], gemm_ps[:, c % 2, rt], gt2b[:, cols], ALU.mult)
            me(ins)
            dve.tensor_tensor(x2_sb[:, :, cols], x2_sb[:, :, cols], tmp[:], ALU.add).then_inc(evac_dve, 1)
        dve.wait_ge(S("n_rs"), 5)
        newton(stat[:, 32:34], stat[:, 34:36], D, stat[:, 36:38])
        for rt in range(RT):
            dve.scalar_tensor_tensor(out=x2_sb[:, rt], in0=x2_sb[:, rt], scalar=stat[:, 34 + rt:35 + rt], in1=gfin[:, :],
                                     op0=ALU.mult, op1=ALU.mult).then_inc(S("out_done"), 1)


    @block.tensor
    def _(pe):
        def product(u0, slot0, bank, hi, lo, units, chunk0=0, opened=False, after=None, chunks=None, n=NBLK,
                    halfway=None, turning=None):
            if turning:
                turn(*turning, 0)
                turn(*turning, 1)
            chunks = chunks or units * UK
            for i in range(units):
                slot = (slot0 + i) % SLOTS
                if turning:
                    pe.wait_ge(S("tr_lo"), BU * tr_use[turning[0]] + i + 1)
                pe.wait_ge(lo_done, u0 + i + 1)
                for kk in range(UK):
                    k = UK * i + kk
                    if k >= chunks:
                        continue
                    for rt in range(RT):
                        tok = slice(rt * P, (rt + 1) * P)
                        for part, (x, w) in enumerate(((hi, w_hi), (hi, w_lo), (lo, w_hi))):
                            mm = pe.matmul(gemm_ps[:, bank, rt, 0:n], x[:, chunk0 + k, tok], w[:, slot, kk, 0:n],
                                           start=(k == 0 and part == 0 and not opened),
                                           stop=(k == chunks - 1 and part == 2))
                    if halfway and kk == 0:
                        halfway(i)
                mm.then_inc(used, 1)
                if turning and i + 2 < BU:
                    turn(*turning, i + 2)
                if after:
                    after(i)

        def add_row(bank):
            for rt in range(RT):
                pe.matmul(gemm_ps[:, bank, rt], C("sel", 1, 0, P), brow[:, :], start=True, stop=False)

        def mod_unit(m, i):
            if i == 0:
                if not (isinstance(m, int) and m == 0):
                    pe.wait_ge(mod_evac, m)
            pe.wait_ge(mod_in[i % SLOTS], 16 * (2 * m + i // SLOTS + 1))
            for kk in range(UK):
                k = UK * i + kk
                g = k % 4
                mm = pe.matmul(pD[32 * g:32 * g + 32, :], cs[:, k], mraw[:, i % SLOTS, kk],
                               start=(k < 4), stop=(k >= KC - 4), skip_group_check=True)
            mm.then_inc(mod_used, 1)

        def every_other(m, half, u):
            if u % 2:
                mod_unit(m, 4 * half + u // 2)

        def turn(use, src, scaled, g):
            G = BU * tr_use[use] + g
            if G >= 2:
                pe.wait_ge(S("tr_val"), G - 1)
            for k in range(UK):
                for rt in range(RT):
                    kc = UK * g + k
                    out = ps[:, g % 2, k * T + rt * P:k * T + (rt + 1) * P]
                    part = src[:, rt, kc * P:(kc + 1) * P]
                    if scaled:
                        mm = pe.matmul(out, part, diag[:, rt], start=True, stop=True)
                    else:
                        mm = pe.transpose(out, part, ident)
            mm.then_inc(S("tr_ps"), 1)

        def narrow_product(w):
            for k in range(KC):
                g = k % 4
                for part, x in enumerate((a_hi, a_lo)):
                    mm = pe.matmul(pC[32 * g:32 * g + 32, 0:T], w[:, k], x[:, k].bitcast(F32),
                                   start=(k < 4 and part == 0), stop=(k >= KC - 4 and part == 1), skip_group_check=True)
            return mm

        def stacked(parts):
            for rt in range(RT):
                mm = pe.matmul(pC[:, T + 32 * rt:T + 32 * rt + 32], parts[:, rt * P:(rt + 1) * P], C("stack"),
                               start=True, stop=True)
            return mm

        def head(r, h, u):
            hh = HEADS * r + h
            src = br[r % 2]
            qT, kT = qkgT[:, 0], qkgT[:, 1]
            if u == 2:
                if r < 2:
                    pe.wait_ge(S("h_pre"), hh + 1)
                else:
                    pe.wait_ge(evac_act, 4 * (r + 1))
                if hh > 0:
                    pe.wait_ge(S("h_y"), hh)
                for rt in range(RT):
                    for t in range(2):
                        s = qkn[:, rt, t] if r < 2 else src[:, rt, t * BW + h * HD:t * BW + (h + 1) * HD]
                        pe.transpose(pA[:, t * T + rt * P:t * T + (rt + 1) * P], s, ident)
                    mm = pe.transpose(pB[:, rt * P:(rt + 1) * P], src[:, rt, 3 * BW + h * HD:3 * BW + (h + 1) * HD], ident)
                mm.then_inc(S("h_T"), 1)
            if u == 3:
                pe.wait_ge(S("h_qkT"), hh + 1)
                if r < 2:
                    if hh == 0:
                        pe.wait_ge(S("f_cneg"), 1)
                    if hh == HEADS:
                        pe.wait_ge(S("rel_in"), 16)
                    if hh > 0:
                        pe.wait_ge(S("h_exp"), 4 * r + h)
                    for rt in range(RT):
                        n = P * (rt + 1)
                        out = pC[:, rt * T:rt * T + n]
                        pe.matmul(out, qT[:, rt * P:(rt + 1) * P], kT[:, 0:n], start=True, stop=False)
                        if r == 0:
                            pe.matmul(out, C("sel", HEADS, h * P, P), cneg[0:HEADS, 0:n], start=False, stop=False)
                        else:
                            for kt in range(rt + 1):
                                d = (rt - kt) * P
                                pe.matmul(out[:, kt * P:(kt + 1) * P], relb[:, h, d:d + P], C("anti"), start=False, stop=False)
                        mm = pe.matmul(out[:, rt * P:n], ident, C("m_causal" if r == 0 else "m_chunk"), start=False, stop=True)
                else:
                    if h == 0:
                        pe.wait_ge(S("h_exp"), 2 * HEADS)
                    else:
                        pe.wait_ge(S("h_PTs"), hh)
                    pe.matmul(pC[:, 0:T], kT[:, 0:P], qT[:, 0:T], start=True, stop=False, skip_group_check=True)
                    mm = pe.matmul(pC[:, T:3 * P], kT[:, P:T], qT[:, P:T], start=False, stop=False, skip_group_check=True)
                mm.then_inc(S("h_L"), 1)
            if u == 5:
                pe.wait_ge(S("h_p"), hh + 1)
                if r < 2:
                    for n, (rt, kt) in enumerate(((0, 0), (1, 0), (1, 1))):
                        mm = pe.transpose(pA[:, n * P:(n + 1) * P], probs[:, rt, kt * P:(kt + 1) * P], ident)
                    mm.then_inc(S("h_PT"), 1)
                else:
                    lk = zwork[:, 1]
                    kw = dict(start=False, skip_group_check=True)
                    pe.matmul(pC[:, 0:T], C("neg_suf_in"), lk[:, 0:T], stop=False, **kw)
                    pe.matmul(pC[:, P:T], C("neg_all"), lk[:, T:3 * P], stop=False, **kw)
                    pe.matmul(pC[:, T:3 * P], C("neg_suf_in"), lk[:, T:3 * P], stop=False, **kw)
                    pe.matmul(pC[:, 0:P], ident, C("m_strict"), stop=False, **kw)
                    pe.matmul(pC[:, T:3 * P], ident, C("m_strict"), stop=True, **kw).then_inc(S("h_R"), 1)
            if u == 6:
                pe.wait_ge(S("h_PTs"), hh + 1)
                pe.wait_ge(S("h_gT"), hh + 1)
                v = src[:, :, 2 * BW + h * HD:2 * BW + (h + 1) * HD]
                pe.matmul(pB[:, 0:T], v[:, 0], probsT[:, 0:T], start=True, stop=False)
                pe.matmul(pB[:, P:T], v[:, 1], probsT[:, T:3 * P], start=False, stop=True).then_inc(S("h_O"), 1)

        def forget_gates(B, u):
            if (B, u) == (1, 7):
                pe.wait_ge(S("wf_in"), 32)
                narrow_product(wf).then_inc(S("f_parts"), 1)
            if (B, u) == (2, 1):
                pe.wait_ge(S("f_copied"), 1)
                stacked(fparts).then_inc(S("f_ps"), 1)
            if (B, u) == (3, 1):
                pe.wait_ge(S("f_log"), 1)
                lf = [fl[:, 5 + rt, 0:HEADS] for rt in range(RT)]
                crow = pC[0:HEADS, 0:T]
                pe.matmul(crow[:, 0:P], lf[0], C("neg_pre_in"), start=True, stop=True)
                pe.matmul(crow[:, P:T], lf[0], C("neg_all"), start=True, stop=False)
                pe.matmul(crow[:, P:T], lf[1], C("neg_pre_in"), start=False, stop=True).then_inc(S("f_c"), 1)

        pe.wait_ge(S("const_in"), 16)
        pe.wait_ge(S("vec_in"), 144)
        pe.transpose(pC[:, 0:88], vrows[0:88, :], ident[0:88, 0:88]).then_inc(S("n_vecT"), 1)
        pe.wait_ge(S("cs_set"), 1)
        pe.wait_ge(S("diag_set"), 1)
        for seg in range(4):
            for b in range(4):
                B = 4 * seg + b
                if B >= 2:
                    pe.wait_ge(evac_act, B - 1)
                if seg == 3:
                    pe.wait_ge(brow_in, 16 * (b + 1))
                    add_row(B % 2)

                def after(u):
                    if seg:
                        head(seg - 1, b, u)
                    else:
                        forget_gates(B, u)
                    every_other(B // 2, B % 2, u)
                product(BU * B, 0, B % 2, a_hi, a_lo, BU, opened=(seg == 3), after=after,
                        turning=("x", x_sb, True) if B == 0 else None)
        pe.wait_ge(S("h_ylo"), NBR * HEADS)
        for c in range(DC):
            B = B_UP0 + c
            if c < 2:
                pe.wait_ge(evac_act, B - 1)
            else:
                pe.wait_ge(evac_dve, c - 1)
            product(U_UP0 + UPU * c, UPU * c, B % 2, ys_hi, ys_lo, UPU)
        pe.wait_ge(evac_dve, DC)
        with pe.Fori(0, DC) as c:
            for j in range(2):
                u0 = U_PAIRS + 2 * PAIR * c + PAIR * j
                pe.wait_ge(brow_in, 16 * (DC + 2 * c + j + 1))
                pe.wait_ge(evac_act, 16 + 2 * c + j)
                add_row(0)
                product(u0, PAIR * j, 0, a_hi, a_lo, BU, opened=True, after=lambda u: every_other(8 + c, j, u))
                pe.wait_ge(evac_dve, DC + 2 * c + j)
                product(u0 + BU, PAIR * j + BU, 1, ys_hi, ys_lo, UPU, chunk0=4 * (j + 1))
        pe.wait_ge(evac_dve, 12)
        for c in range(DC):
            pe.wait_ge(evac_dve, 12 + c - 1 if c else 12)
            product(U_OUT + BU * c, 0, c % 2, a_hi, a_lo, BU, turning=("merged", merged, False) if c == 0 else None)
        pe.wait_ge(S("mvr_in"), 272)
        for r in range(2):
            pe.transpose(pA[:, r * P:(r + 1) * P], mvr[:, r], ident)
        pe.transpose(pA[:, 2 * P:2 * P + 32], mvb[:, :], ident[0:32, 0:32]).then_inc(S("mv_ps"), 1)
        pe.wait_ge(S("diag_set"), 2)
        pe.wait_ge(S("mv_done"), 1)

        def small_product(n):
            if n == 0:
                pe.wait_ge(S("wsm_in"), 48)
            else:
                pe.wait_ge(S("sm_in"), n)
            narrow_product(wsm).then_inc(S("s_ps"), 1)

        def small_stack(n):
            pe.wait_ge(S("s_parts"), n + 1)
            stacked(zparts).then_inc(S("s_tok"), 1)

        for cb in range(6):
            if cb < 2:
                pe.wait_ge(evac_dve, 15 + cb)
            else:
                pe.wait_ge(evac_act, 24 + cb - 1)

            def after(u):
                mod_unit(12 + cb, u)
                if (cb, u) == (0, 7):
                    small_product(0)
                if (cb, u) == (1, 1):
                    small_stack(0)
            product(U_CTX + BU * cb, 0, (B_CTX + cb) % 2, a_hi, a_lo, BU, after=after,
                    turning=("ctx", ctx_sb, True) if cb == 0 else None)
        pe.wait_ge(S("diag_set"), 3)

        LF = sx[:, 3].rearrange("p (t d h) -> p t d h", t=4, d=2)
        LAc = lambda t, d: y[:, t, 2 * BW + d * BW:2 * BW + (d + 1) * BW]

        def step(s):
            if s == 7:
                small_product(1)
            if s == 9:
                small_stack(1)
            if s == 13:
                pe.wait_ge(S("m_lf"), 1)
                F = pC[:, P:P + 32].rearrange("p (t d h) -> p t d h", t=4, d=2)
                for t, d, terms in ((0, 0, (("suf_ex", 0), ("all", 1))), (1, 0, (("suf_ex", 1),)),
                                    (0, 1, (("pre_ex", 0),)), (1, 1, (("all", 0), ("pre_ex", 1))),
                                    (2, 0, (("pre_in", 2),)), (3, 0, (("all", 2), ("pre_in", 3))),
                                    (2, 1, (("suf_in", 2), ("all", 3))), (3, 1, (("suf_in", 3),))):
                    for n, (name, t2) in enumerate(terms):
                        mm = pe.matmul(F[:, t, d], MT[name], LF[:, t2, d], start=(n == 0), stop=(n == len(terms) - 1))
                mm.then_inc(S("m_F"), 1)
            if s == 15:
                pe.wait_ge(S("m_G"), 1)
                for t in range(4):
                    mm = pe.transpose(pA[0:8, t * P:(t + 1) * P], sx[:, 4, 8 * t:8 * t + 8], ident)
                mm.then_inc(S("m_GT"), 1)
            if s == 17:
                pe.wait_ge(S("m_rows"), 1)
                for rt in range(RT):
                    for w in range(2):
                        mm = pe.transpose(pB[:, 16 * rt + 8 * w:16 * rt + 8 * w + 8], mrows[:, w, rt * P:(rt + 1) * P], ident[0:8, 0:8])
                mm.then_inc(S("m_MT"), 1)
            if s == 18:
                for t in range(4):
                    mm = pe.transpose(pA[0:LR, t * P:(t + 1) * P], sm[:, t, 0:LR], ident)
                mm.then_inc(S("g_glr"), 1)
            if 20 <= s < 28:
                n = s - 20
                if n == 0:
                    pe.wait_ge(S("wlr_in"), 32)
                    pe.wait_ge(S("g_glrT"), 1)
                    pe.wait_ge(S("m_FM"), 1)
                if n >= 2:
                    pe.wait_ge(S("g_la"), n - 1)
                t, d = n // 2, n % 2
                pe.matmul(ps[:, n % 2], glrT[0:LR + 1, t * P:(t + 1) * P], wlr[0:LR + 1, d], start=True, stop=True).then_inc(S("g_dec"), 1)
            if 28 <= s < 32:
                m = s - 28
                t, d = m // 2, m % 2
                pe.wait_ge(S("g_la"), 8 if m % 2 else 6)
                if m >= 2:
                    pe.wait_ge(S("g_kexp"), m - 1)
                bank = (pC, pA)[m % 2]
                terms = {(0, 0): (("suf_ex", 0), ("all", 1)), (1, 0): (("suf_ex", 1),),
                         (0, 1): (("pre_ex", 0),), (1, 1): (("all", 0), ("pre_ex", 1))}[t, d]
                for n, (name, t2) in enumerate(terms):
                    mm = pe.matmul(bank, MT[name], LAc(t2, d), start=(n == 0), stop=(n == len(terms) - 1))
                mm.then_inc(S("g_w"), 1)
            if 32 <= s < 64:
                h, u = (s - 32) // 8, (s - 32) % 8
                if u == 0:
                    if h:
                        pe.wait_ge(S("m_y"), h)
                    else:
                        pe.wait_ge(evac_act, 30 + 4)
                        pe.wait_ge(S("g_kexp"), 4)
                    for rt in range(RT):
                        pe.transpose(pA[:, rt * P:(rt + 1) * P], cm[:, rt, h * HD:(h + 1) * HD], ident)
                        pe.transpose(pA[:, T + rt * P:T + (rt + 1) * P], xm[:, rt, BW + h * HD:BW + (h + 1) * HD], ident)
                        mm = pe.transpose(pB[:, rt * P:(rt + 1) * P], xm[:, rt, h * HD:(h + 1) * HD], ident)
                    mm.then_inc(S("m_T"), 1)
                if u == 2:
                    pe.wait_ge(S("m_kT"), h + 1)
                    pe.wait_ge(S("m_qT"), h + 1)
                    for t in range(4):
                        pe.matmul(ps[:, t // 2, t % 2 * T:(t % 2 + 1) * T], mkT[:, t * P:(t + 1) * P], mqT[:, :], start=True, stop=True)
                    for d in range(2):
                        r = 4 * d + h
                        mm = pe.matmul(pC[:, d * T:(d + 1) * T], C("sel", 8, r * P, P), mrows[:, d], start=True, stop=True)
                    mm.then_inc(S("m_QK"), 1)
                if u in (4, 7):
                    d = u == 7
                    if h == 0 and d == 0:
                        pe.wait_ge(mod_evac, 20)
                    pe.wait_ge(S("m_s"), 2 * h + d + 1)
                    num(h, int(d))
            if s == 64:
                pe.wait_ge(S("m_y"), HEADS)
                for d in range(2):
                    for h in range(HEADS):
                        out = ps[:, 2 * d + h // 2, h % 2 * GDV:(h % 2 + 1) * GDV]
                        for t in range(RT):
                            mm = pe.matmul(out, y[:, t, d * BW + h * HD:d * BW + (h + 1) * HD], cg[:, t, BW + h * GDV:BW + (h + 1) * GDV],
                                           start=(t == 0), stop=(t == 1))
                mm.then_inc(S("g_S"), 1)
            if 66 <= s <= 98:
                gla_fill(s - 66)

        def half_step(s):
            if 68 <= s < 100:
                gla_score(s - 68)
            if s >= 70 and s % 2 == 0 and (s - 70) // 2 < 16:
                gla_out((s - 70) // 2)

        MT = {n: C(n) for n in ("pre_in", "suf_in", "pre_ex", "suf_ex", "all")}
        tiles = (((0, 0, T), (1, 0, T), (2, 0, T), (3, P, T)), ((0, 0, T), (1, 0, T), (3, 0, T), (2, 0, P)))
        def num(h, d):
            v = [cm[:, 0, BW:], cm[:, 1, BW:], xm[:, 0, 2 * BW:], xm[:, 1, 2 * BW:]]
            for rt in range(RT):
                seen = [(t, 2 * P * n + rt * P - lo) for n, (t, lo, hi) in enumerate(tiles[d]) if lo <= rt * P < hi]
                for n, (t, at0) in enumerate(seen):
                    pe.matmul(numb[d][:, rt * GDV:(rt + 1) * GDV], mpT[:, at0:at0 + P], v[t][:, h * GDV:(h + 1) * GDV],
                              start=(n == 0), stop=(n == len(seen) - 1))
            for rt in range(RT):
                seen = [(t, 2 * P * n + rt * P - lo) for n, (t, lo, hi) in enumerate(tiles[d]) if lo <= rt * P < hi]
                for n, (t, at0) in enumerate(seen):
                    mm = pe.matmul(denb[:, 2 * d + rt:2 * d + rt + 1], mpT[:, at0:at0 + P], C("neg_all", P, 0, 1),
                                   start=(n == 0), stop=(n == len(seen) - 1))
            mm.then_inc(S("m_num"), 1)

        pe_turn = [0]

        def give():
            if pe_turn[0] >= 2:
                pe.wait_ge(S("g_free"), pe_turn[0] - 1)
            pe_turn[0] += 1
            return ps[:, (pe_turn[0] - 1) % 2]

        def gla_fill(k):
            gc, j = k // 2, k % 2
            h, c = gc // 4, gc % 4
            d, rt = c // 2, c % 2
            if j == 0 and gc and c % 2 == 0:
                dp = (gc - 1) % 4 // 2
                pe.wait_ge(S("g_f"), gc)
                pe.matmul(give()[:, 0:P], cr[:, dp], cr[:, 1 - dp], start=True, stop=True).then_inc(S("g_ps"), 1)
            if k == 32:
                return
            if j == 0 and c == 0:
                if h == 0:
                    pe.wait_ge(S("g_state"), 2)
                    pe.wait_ge(evac_act, 30 + 8)
                bank = give()
                for t in range(RT):
                    pe.transpose(bank[:, t * P:(t + 1) * P], xg[:, t, h * HD:(h + 1) * HD], ident)
                    mm = pe.transpose(bank[:, T + t * P:T + (t + 1) * P], xg[:, t, BW + h * HD:BW + (h + 1) * HD], ident)
                mm.then_inc(S("g_ps"), 1)
            L = lambda t: la[:, t, d, h * HD:(h + 1) * HD]
            if j == 0:
                bank = give()
                edge = {(0, 0): "suf_ex", (0, 1): "pre_in", (1, 0): "suf_in", (1, 1): "pre_ex"}[d, rt]
                since = "suf_in" if d else "pre_in"
                pe.matmul(bank[:, 0:P], L(rt), MT[edge], start=True, stop=True)
                far = rt != d
                mm = pe.matmul(bank[:, P:2 * P], L(rt), MT[since], start=True, stop=not far)
                if far:
                    mm = pe.matmul(bank[:, P:2 * P], L(1 - rt), MT["all"], start=False, stop=True)
                mm.then_inc(S("g_ps"), 1)
            bank = give()
            if k == 0:
                pe.wait_ge(S("lsum_in"), 32)
            pe.matmul(bank, L(rt), lsum[:, d, 4 * j:4 * j + 4].rearrange("p l t -> p (l t)"), start=True, stop=True).then_inc(S("g_ps"), 1)

        def gla_score(k):
            pe.wait_ge(S("g_mult"), k + 1)
            if k:
                pe.wait_ge(S("g_masked"), k)
            for l in range(4):
                mm = pe.matmul(pC[:, l * P:(l + 1) * P], rk[:, l], ek[:, k % 2, l], start=True, stop=True)
            mm.then_inc(S("g_sc"), 1)

        def gla_out(gc):
            h, c = gc // 4, gc % 4
            d, rt = c // 2, c % 2
            v = lambda t: xg[:, t, 2 * BW + h * GDV:2 * BW + (h + 1) * GDV]
            out = lambda t: pD[:, t * GDV:(t + 1) * GDV]
            kw = dict(skip_group_check=True)
            pe.wait_ge(S("g_mask"), 2 * gc + 2)
            if c == 0 and h:
                pe.wait_ge(S("g_y"), h)
            pe.matmul(out(rt), fq[:, gc % 2], state[:, d, h], start=(c == 0), stop=False, **kw)
            mm = pe.matmul(out(rt), sc[:, 0], v(rt), start=False, stop=False, **kw)
            if rt == 1:
                pe.wait_ge(S("g_free"), 15 * h + (7 if d == 0 else 14) + 1)
                mm = pe.matmul(out(1 - d), sc[:, 2], v(d), start=False, stop=(d == 1), **kw)
            mm.then_inc(S("g_o"), 1)

        numb, denb = (pD, pA), pC
        for xb in range(12):
            pe.wait_ge(evac_act, 30 + xb - 1)

            def after(u):
                step(8 * xb + u)
                if xb < 4:
                    every_other(18 + xb // 2, xb % 2, u)
            product(U_X + BU * xb, 0, (B_X + xb) % 2, a_hi, a_lo, BU, after=after,
                    turning=("x1", xres, True) if xb == 0 else None,
                    halfway=(lambda u: half_step(8 * xb + u)) if xb >= 8 else None)
        for s in range(96, 102):
            half_step(s)
            step(s)
        pe.wait_ge(S("y_done"), 1)

        def second_vectors(u):
            if u == 2:
                pe.wait_ge(S("mvr_in2"), 144)
                pe.transpose(pC[:, 0:P], mvr[:, 0], ident)
                pe.transpose(pC[:, P:P + 32], mvb[:, :], ident[0:32, 0:32]).then_inc(S("mv_ps"), 1)
            if u >= 4:
                n = u - 4
                if n == 0:
                    pe.wait_ge(S("mv_done"), 2)
                    pe.wait_ge(S("gtr_in"), 32)
                else:
                    pe.wait_ge(S("gt_in"), n)
                pe.matmul(pC, C("neg_all", 5), gtr[:, n * NBLK:(n + 1) * NBLK], start=True, stop=True).then_inc(S("gt_ps"), 1)

        for c in range(DC):
            if c < 2:
                pe.wait_ge(evac_act, 41 + c)
            else:
                pe.wait_ge(evac_dve, 16 + c - 1)

            def after(u):
                mod_unit(20 + c, u)
                if c == 0:
                    second_vectors(u)
            product(U_OUT2 + BU * c, 0, c % 2, a_hi, a_lo, BU, after=after, turning=("y", y, False) if c == 0 else None)
        pe.wait_ge(S("gt_in"), DC)
        pe.wait_ge(S("cw_in"), 80)
        for t in range(4):
            k = (P, P, P, 10 * FCH - 3 * P)[t]
            mm = pe.transpose(pC[:, t * P:t * P + k], cwr[0:k, t], ident[0:k, 0:k])
        mm.then_inc(S("cw_ps"), 1)
        pe.wait_ge(S("diag_set"), 4)

        def turn_u(b, par, nf):
            pe.wait_ge(evac_act, 42 + b)
            if not (isinstance(b, int) and b == 1):
                pe.wait_ge(S("f_fv"), b - 1)
            for half, bank in enumerate((pA, pB)):
                for f in range(nf):
                    for rt in range(RT):
                        c0 = (half * nf + f) * P
                        mm = pe.transpose(bank[:, f * T + rt * P:f * T + (rt + 1) * P], ub[:, 1 - par, rt, c0:c0 + P], ident)
            mm.then_inc(S("f_T"), 1)

        def ffn_block(b, par, turned=2, n=NBLK):
            if isinstance(b, int) and b < 2:
                pe.wait_ge(evac_dve, 19 + b)
            else:
                pe.wait_ge(evac_act, 42 + b - 1)
            product(U_FFN + BU * b, 0, par, a_hi, a_lo, BU, n=n,
                    turning=("x2", xres, True) if isinstance(b, int) and b == 0 else None,
                    after=lambda u: turn_u(b, par, turned) if u == 3 and turned else None)

        ffn_block(0, 0, 0)
        ffn_block(1, 1)
        with pe.Fori(0, 9) as n:
            for k in range(2):
                ffn_block(2 * n + 2 + k, k)
        ffn_block(20, 0)
        ffn_block(21, 1, n=T)
        pe.wait_ge(S("f_lo"), 20)
        for c in range(DC):
            if c < 2:
                pe.wait_ge(evac_act, 63 + c)
            else:
                pe.wait_ge(evac_dve, 20 + c - 1)

            def after(u):
                if c == 0 and u == 3:
                    turn_u(22, 0, 1)
                if c == 0 and u == 19:
                    pe.wait_ge(S("f_lo"), FB)
            product(U_DOWN + DU * c, (DU * c) % SLOTS, c % 2, ft_hi, ft_lo, DU, chunks=FCH, after=after)
            if c == 0:
                pe.wait_ge(S("gtr2_in"), 32)
                for n in range(DC):
                    mm = pe.matmul(ps[:, n], C("neg_all", 5), gtr2[:, n * NBLK:(n + 1) * NBLK], start=True, stop=True)
                mm.then_inc(S("gt_ps"), 1)

    block.__exit__(None, None, None)


_INS = [
    "x", "norm_g", "w_in", "b_f", "b_gate", "qk_norm_g", "rel_bias", "w_up", "w_out", "c_2", "ctx_2", "c_ctx_2",
    "w_mod_2", "b_mod_2", "g_norm1_2", "g_norm2_2", "w_in_2", "gla_w_lr_2", "gla_b_lr_2", "mlstm_b_gate_2",
    "gla_g_norm_2", "mlstm_g_norm_2", "w_out_2", "w_up_2", "conv_w_2", "conv_b_2", "w_down_2", "g_final_2",
]
_OUTS = [((1, T, D), "float32")]


def kernel(**inputs):
    import numpy as _np
    import concourse.bacc as _bacc
    from concourse import mybir as _mybir
    from concourse.bass_utils import run_bass_kernel_spmd as _run

    nc = _bacc.Bacc("TRN2", target_bir_lowering=False, num_devices=1)
    arrays, args = {}, {}
    named = {name: _np.ascontiguousarray(inputs[name]) for name in _INS}
    named["const"], named["lsum"] = CONST, LSUM
    named["lpair"] = LPAIR.astype(_np.dtype("bfloat16"))
    for name, a in named.items():
        arrays[f"in_{name}_dram"] = a
        args[name] = nc.dram_tensor(f"in_{name}_dram", a.shape, _mybir.dt.from_np(a.dtype), kind="ExternalInput").ap()
    for i, (shape, dtype) in enumerate(_OUTS):
        dt = _mybir.dt.from_np(_np.dtype(dtype))
        args["out"] = nc.dram_tensor(f"out_{i}_dram", shape, dt, kind="ExternalOutput").ap()
    build(nc, args)
    r = _run(nc, [arrays], core_ids=[0])
    got = tuple(r.results[0][f"out_{i}_dram"] for i in range(len(_OUTS)))
    return got[0]
```

```python
import concourse.bass as bass
from concourse import mybir
import numpy as np

F32 = mybir.dt.float32
F32R = mybir.dt.float32r
I32 = mybir.dt.int32
ROOT_BITS = 0x5F3759DF
ALU = mybir.AluOpType
ACT = mybir.ActivationFunctionType
AX_X = mybir.AxisListType.X

P = 128
T = 256
RT = T // P
D = 2048
KC = D // P
NBLK = 512
UK = 2
SLOTS = 4
BU = KC // UK
HD = 128
HEADS = 4
BW = HEADS * HD
NBR = 3
MAX_REL = 128
CHUNK = 64
EPS = 1e-6
NEG = -1e30
SCALE = float(HD) ** -0.5
FF = 5504
FCH = FF // P
GDV = 256
NORMALIZER = 16.0
DC = D // NBLK

U_QKVG = 0
UPU = BW // P // UK
PAIR = BU + UPU
U_GATE0 = U_QKVG + 12 * BU
U_UP0 = U_GATE0 + DC * BU
U_PAIRS = U_UP0 + DC * UPU
U_OUT = U_PAIRS + 2 * DC * PAIR
U_CTX = U_OUT + DC * BU
U_X = U_CTX + 6 * BU
U_OUT2 = U_X + 12 * BU
U_FFN = U_OUT2 + DC * BU
FB = 22
U_DOWN = U_FFN + FB * BU
DU = (FCH + 1) // UK
U_END = U_DOWN + DC * DU

B_GATE0, B_UP0, B_PAIRS, B_OUT, B_CTX, B_X, B_OUT2, B_FFN, B_DOWN = 12, 16, 20, 36, 40, 46, 58, 62, 84


def constants():
    t = np.arange(P)
    row, col = t[:, None], t[None, :]
    one = np.ones((P, P), np.float32)
    c = {}
    c["ident"] = (row == col)
    c["anti"] = (row + col == P - 1)
    c["pre_in"] = (row <= col) / NORMALIZER
    c["suf_in"] = (row >= col) / NORMALIZER
    c["pre_ex"] = (row < col) / NORMALIZER
    c["suf_ex"] = (row > col) / NORMALIZER
    c["all"] = one / NORMALIZER
    c["neg_pre_in"] = -1.0 * (row <= col)
    c["neg_suf_in"] = -1.0 * (row >= col)
    c["neg_all"] = -one
    c["m_causal"] = NEG * (col > row)
    c["m_chunk"] = NEG * (col // CHUNK > row // CHUNK)
    c["m_strict"] = NEG * (row >= col)
    c["strict"] = np.concatenate([row < col, one, row < col], 1)
    sel = np.zeros((P, 8 * P))
    for r in range(8):
        sel[r, r * P:(r + 1) * P] = 1.0
    c["sel"] = sel
    c["ge"] = (row <= col)
    c["le"] = (row >= col)
    c["stack"] = (row % 32 == col)[:, 0:32]
    order, at, parts = {}, 0, []
    for k, v in c.items():
        v = np.asarray(v, np.float32)
        order[k] = (at, v.shape[1])
        at += v.shape[1]
        parts.append(v)
    return order, np.concatenate(parts, 1)


def level_constants():
    t = np.arange(P)
    row, col = t[:, None], t[None, :]
    sums, pairs = [], []
    for d in range(2):
        for size in (128, 64, 32, 16, 8, 4, 2):
            mid = col // size * size + size // 2
            if d == 0:
                m = np.where(col >= mid, (row >= mid) & (row <= col), (row > col) & (row < mid))
                pair = (row // size == col // size) & (row % size < size // 2) & (col % size >= size // 2)
            else:
                m = np.where(col < mid, (row >= col) & (row < mid), (row >= mid) & (row < col))
                pair = (row // size == col // size) & (row % size >= size // 2) & (col % size < size // 2)
            sums.append(m / NORMALIZER)
            pairs.append(pair)
        sums.append(np.zeros((P, P)))
        pairs.append(row == col)
    return np.concatenate(sums, 1).astype(np.float32), np.concatenate(pairs, 1).astype(np.float32)


CONST_AT, CONST = constants()
LSUM, LPAIR = level_constants()
LEVELS = 8

KB = 1024

GQ, GK, GV, GG, GLR, MQ, MK, MV, MO, MG = 0, 512, 1024, 2048, 3072, 3088, 3600, 4112, 5136, 6160
CTX_COLS = (MK, MV, MV + NBLK, GK, GV, GV + NBLK)
X_COLS = (MQ, MK, MV, MV + NBLK, GQ, GK, GV, GV + NBLK, MO, MO + NBLK, GG, GG + NBLK)
LR = 16
MODS = 24
MODC = 6 * D


class Count:

    def __init__(self, eng, sem):
        self.eng, self.sem, self.n, self.off = eng, sem, 0, 0

    def __call__(self, ins):
        self.n += 1
        ins.then_inc(self.sem, 1)
        self.eng.wait_ge(self.sem, self.n + self.off)

    def iteration(self, first, i):
        self.n, self.off = first, i



def build(nc, a):
    base = (nc.sbuf_base + 31) // 32 * 32

    def at(name, shape, dtype, kb):
        return nc.alloc_sbuf_tensor_at(name, shape, dtype, offset=base + int(kb * KB))

    raw = at("w_raw", [P, SLOTS, UK, NBLK], F32, 0)
    w_hi = at("w_hi", [P, SLOTS, UK, NBLK], F32R, 16)
    w_lo = at("w_lo", [P, SLOTS, UK, NBLK], F32R, 32)
    a_hi = at("a_hi", [P, KC, T], F32R, 48)
    a_lo = at("a_lo", [P, KC, T], F32R, 64)
    cst = at("cst", [P, CONST.shape[1]], F32, 80)
    cs = at("cs", [P, KC, 32], F32, 93.5)
    mrow = at("mrow", [P, NBLK], F32, 95.5)
    mraw = at("mraw", [P, SLOTS, UK, NBLK], F32, 97.5)
    x_sb = at("x_sb", [P, RT, D], F32, 113.5)
    xn = at("xn", [P, RT, D], F32, 113.5)
    diag = at("diag", [P, RT, P], F32, 204.5)
    br = [at(f"br{i}", [P, RT, 4 * BW], F32, 129.5 + 16 * i) for i in range(2)]
    ys_hi = at("ys_hi", [P, NBR * HEADS, T], F32R, 161.5)
    ys_lo = at("ys_lo", [P, NBR * HEADS, T], F32R, 173.5)
    brow = at("brow", [1, NBLK], F32, 185.5)
    relb = at("relb", [P, HEADS, T], F32, 189.5)
    tmpT = at("tmpT", [P, 2, UK, T], F32, 193.5)
    sg = at("sg", [P, RT, NBLK], F32, 193.5)
    qkn = at("qkn", [P, RT, 2, HD], F32, 193.5)
    qkgT = at("qkgT", [P, 3, T], F32, 195.5)
    probs = at("probs", [P, RT, T], F32, 198.5)
    zwork = at("zwork", [P, 2, 3 * P], F32, 198.5)
    probsT = at("probsT", [P, 3 * P], F32, 201.5)
    yT = at("yT", [P, T], F32, 203)
    cneg = at("cneg", [P, T], F32, 205)
    wf = at("wf", [P, KC, 32], F32, 201.5)
    fparts = at("fparts", [P, T], F32, 203.5)
    fl = at("fl", [P, 8, 8], F32, 206.25)
    gbias = at("gbias", [P, 1], F32, 206.5)
    stat = at("stat", [P, 64], F32, 206.625)
    vec = at("vec", [P, 160], F32, 207)
    merged = br[0]
    vrows = sg[:, 0, 0:P]
    rel_ext = probs[0:HEADS].rearrange('p a b -> p (a b)')[:, 0:384]
    rrows = sg[:, 1, 0:512]

    BF16 = mybir.dt.bfloat16
    ctx_sb = at("ctx_sb", [P, RT, D], F32, 129.5)
    mvr = at("mvr", [P, 2, P], F32, 153.5)
    mvb = at("mvb", [32, P], F32, 154.5)
    zparts = at("zparts", [P, T], F32, 197.5)
    xres = at("xres", [P, RT, D], F32, 161.5)
    wsm = at("wsm", [P, KC, 2 * LR], F32, 185.5)
    y = xn
    cm = at("cm", [P, RT, 3 * NBLK], F32, 129.5)
    cg = at("cg", [P, RT, 3 * NBLK], F32, 141.5)
    xm = at("xm", [P, RT, 4 * NBLK], F32, 153.5)
    xg = at("xg", [P, RT, 4 * NBLK], F32, 169.5)
    la = at("la", [P, RT, 2, NBLK], F32, 189.5)
    glrT = at("glrT", [32, 2 * T], F32, 169.5)
    spd = at("spd", [P, 2, NBLK], F32, 171.5)
    kexp = [at("kexp0", [P, NBLK], F32, 175.5), at("kexp1", [P, NBLK], F32, 181.5)]
    wlr = at("wlr", [32, 2, NBLK], F32, 177.5)
    mrows = at("mrows", [8, 2, T], F32, 185.5)
    grows = at("grows", [8, 2 * T], F32, 198.5)
    mqT = at("mqT", [P, T], F32, 197.5)
    mkT = at("mkT", [P, 2 * T], F32, 198.5)
    mpT = at("mpT", [P, 7 * P], F32, 200.5)
    sm = at("sm", [P, 4, 2 * LR], F32, 204)
    sx = at("sx", [P, 12, 32], F32, 204.5)
    gates = at("gates", [P, RT, D], F32, 153.5)
    state = at("state", [P, 2, HEADS, GDV], F32, 129.5)
    gqT = at("gqT", [P, 2, T], F32, 137.5)
    cr = at("cr", [P, RT, P], F32, 139.5)
    fq = at("fq", [P, 2, P], F32, 140.5)
    lsum = at("lsum", [P, 2, LEVELS, P], F32, 141.5)
    hsq = at("hsq", [P, RT, GDV], F32, 187.5)
    lpair = at("lpair", [P, 2, LEVELS, P], BF16, 149.5)
    masked = at("masked", [P, 4, P], F32, 185.5)
    ek = at("ek", [P, 2, 4, P], F32, 197.5)
    rk = at("rk", [P, 4, P], F32, 201.5)
    sc = at("sc", [P, 3, P], F32, 203.5)
    gtb = at("gtb", [P, D], F32, 129.5)
    gtr = at("gtr", [5, D], F32, 137.5)
    tmp_dn = at("tmp_dn", [P, RT, NBLK], F32, 191.5)
    ft_hi = at("ft_hi", [P, FCH, T], F32R, 97.5)
    ft_lo = at("ft_lo", [P, FCH, T], F32R, 140.5)
    ub = at("ub", [P, 2, RT, NBLK], F32, 183.5)
    gp = at("gp", [P, 2, 6, 66], F32, 191.5)
    acc = at("acc", [P, 2, T], F32, 194.75)
    sil = at("sil", [P, 2, T], F32, 196.75)
    fv = at("fv", [P, 2, T], F32, 198.75)
    cw = at("cw", [P, 10 * FCH], F32, 200.75)
    cwr = at("cwr", [P, 4, P], F32, 202.5)
    x2_sb = at("x2_sb", [P, RT, D], F32, 48)
    squares = at("squares", [P, RT, NBLK], F32, 195.5)
    gt2b = at("gt2b", [P, D], F32, 64)
    gfin = at("gfin", [P, D], F32, 72)
    gtr2 = at("gtr2", [5, D], F32, 183.5)

    def C(name, rows=P, lo=0, n=None):
        s, width = CONST_AT[name]
        return cst[0:rows, s + lo:s + lo + (width if n is None else n)]

    gemm_ps = nc.alloc_psum_tensor("gemm_ps", [P, 2, RT, NBLK], F32)
    ps = nc.alloc_psum_tensor("ps", [P, 4, NBLK], F32)
    pA, pB, pC, pD = (ps[:, i] for i in range(4))
    ident = C("ident")

    x1_d = nc.dram_tensor("x1_d", [T, D], F32, kind="Internal").ap().rearrange("(r p) d -> p r d", p=P)
    x2_d = nc.dram_tensor("x2_d", [T, D], F32, kind="Internal").ap().rearrange("(r p) d -> p r d", p=P)
    mod_d = nc.dram_tensor("mod_d", [4, 2, MODC], F32, kind="Internal").ap()
    out_v = a["out"].rearrange("o (r p) d -> p (o r) d", p=P)
    ext_d = nc.dram_tensor("ext_d", [HEADS, 384], F32, kind="Internal").ap()

    sems = {}

    def S(name):
        if name not in sems:
            sems[name] = nc.alloc_semaphore(name)
        return sems[name]

    raw_in = [S(f"raw_in{i}") for i in range(SLOTS)]
    brow_in = S("brow_in")
    mod_in = [S(f"mod_in{i}") for i in range(SLOTS)]
    mod_used, mod_evac, mod_out = S("mod_used"), S("mod_evac"), S("mod_out")
    tr_use = {"x": 0, "merged": 1, "ctx": 2, "x1": 3, "y": 4, "x2": 5}
    TR = lambda use: BU * (tr_use[use] + 1)
    hi_done, lo_done, used = S("hi_done"), S("lo_done"), S("used")
    evac_act, evac_dve = S("evac_act"), S("evac_dve")

    w_in = a["w_in"].rearrange("o (j p) c -> p (o j) c", p=P)
    w_up = a["w_up"].rearrange("o n (j p) c -> p (o n j) c", p=P)
    w_out = a["w_out"].rearrange("o (j p) c -> p (o j) c", p=P)
    w_mod = a["w_mod_2"].rearrange("o (j p) c -> p (o j) c", p=P)
    w_in2 = a["w_in_2"].rearrange("o (j p) c -> p (o j) c", p=P)
    w_out2 = a["w_out_2"].rearrange("o (j p) c -> p (o j) c", p=P)
    w_up2 = a["w_up_2"].rearrange("o (j p) (s c) -> p (o j) s c", p=P, s=2)
    w_dn = a["w_down_2"].rearrange("o (j p) c -> p (o j) c", p=P)
    xv = a["x"].rearrange("o (r p) d -> p (o r) d", p=P)
    QKVG_COLS = NBR * 4 * BW
    GATE0 = QKVG_COLS + HEADS

    with nc.Block() as block:

        @block.sync
        def _(sp):
            def unit(q, slot, src):
                if not (isinstance(q, int) and q == 0):
                    sp.wait_ge(lo_done, 4 * q + slot + 1 - SLOTS)
                sp.dma_start(raw[:, slot, 0:src.shape[1], 0:src.shape[2]], src).then_inc(raw_in[slot], 16)

            def mod_unit(m, i):
                if not (isinstance(m, int) and 2 * m + i // SLOTS == 0):
                    sp.wait_ge(mod_used, BU * m + i + 1 - SLOTS)
                sp.dma_start(mraw[:, i % SLOTS], w_mod[:, UK * i:UK * i + UK, bass.ds(m * NBLK, NBLK)]).then_inc(mod_in[i % SLOTS], 16)

            def units(w, q, col, first=0, count=BU, row=0, mod=None):
                for i in range(count):
                    s = first + i
                    unit(q + s // SLOTS, s % SLOTS, w[:, row + UK * i:row + UK * i + UK, bass.ds(col, NBLK)])
                    if mod:
                        mod(i)

            def every_other(m, half):
                return lambda i: mod_unit(m, 4 * half + i // 2) if i % 2 else None

            sp.dma_start(cst[:, 0:P], a["const"][:, 0:P]).then_inc(S("ident_in"), 16)
            for i, name in enumerate(("norm_g", "g_norm1_2", "g_norm2_2")):
                sp.dma_start(vrows[16 * i:16 * i + 16, :], a[name].rearrange("o (j p) -> (o j) p", p=P)).then_inc(S("vec_in"), 16)
            sp.dma_start(vrows[48:52, :], a["qk_norm_g"].rearrange("o g p -> (o g) p")).then_inc(S("vec_in"), 16)
            sp.dma_start(vrows[52:54, :], a["gla_g_norm_2"].rearrange("o (j p) -> (o j) p", p=P)).then_inc(S("vec_in"), 16)
            sp.dma_start(vrows[54:56, :], a["mlstm_g_norm_2"].rearrange("o (j p) -> (o j) p", p=P)).then_inc(S("vec_in"), 16)
            sp.dma_start(vrows[56:72, :], a["c_2"].rearrange("o (j p) -> (o j) p", p=P)).then_inc(S("vec_in"), 16)
            sp.dma_start(vrows[72:88, :], a["c_ctx_2"].rearrange("(j p) -> j p", p=P)).then_inc(S("vec_in"), 16)
            sp.dma_start(rrows[0:HEADS, 0:2 * MAX_REL + 1], a["rel_bias"].rearrange("o h m -> (o h) m")).then_inc(S("vec_in"), 16)
            for rt in range(RT):
                sp.dma_start(x_sb[:, rt], xv[:, rt]).then_inc(S(f"x_in{rt}"), 16)
            units(w_in, 0, 0, count=SLOTS)
            sp.dma_start(cst[:, P:], a["const"][:, P:]).then_inc(S("const_in"), 16)
            for i in range(SLOTS, BU):
                unit(i // SLOTS, i % SLOTS, w_in[:, UK * i:UK * i + UK, 0:NBLK])
            sp.dma_start(fl[:, 0, 0:HEADS], a["b_f"][0].partition_broadcast(P)).then_inc(S("wf_in"), 16)
            sp.wait_ge(S("wf_zero"), 1)
            sp.dma_start(wf[:, :, 0:HEADS], w_in[:, :, QKVG_COLS:GATE0]).then_inc(S("wf_in"), 16)
            sp.wait_ge(S("rel_ext"), 1)
            sp.dma_start(ext_d, rel_ext).then_inc(S("rel_out"), 16)
            for i in range(4):
                mod_unit(0, i)
            units(w_in, 2, NBLK, mod=every_other(0, 1))
            sp.wait_ge(S("rel_out"), 16)
            diagonals = bass.AP(tensor=ext_d.tensor, offset=1, ap=[[1, P], [384, HEADS], [1, T]])
            sp.dma_start(relb[:], diagonals).then_inc(S("rel_in"), 16)
            for b in range(2, 12):
                units(w_in, 2 * b, b * NBLK, mod=every_other(b // 2, b % 2))
            bg = a["b_gate"]
            for g in range(DC):
                if g:
                    sp.wait_ge(used, U_GATE0 + BU * (g - 1) + 1)
                sp.dma_start(brow[:, :], bg[:, g * NBLK:(g + 1) * NBLK]).then_inc(brow_in, 16)
                b = 12 + g
                units(w_in, 2 * b, GATE0 + g * NBLK, mod=every_other(b // 2, b % 2))
            for c in range(DC):
                s = UPU * c
                units(w_up, U_UP0 // SLOTS + s // SLOTS, c * NBLK, s % SLOTS, UPU)
            with sp.Fori(0, DC) as c:
                for j in range(2):
                    sp.wait_ge(used, U_PAIRS + 2 * PAIR * c + (1 if j else 1 - PAIR))
                    sp.dma_start(brow[:, :], bg[:, bass.ds((j + 1) * D + c * NBLK, NBLK)]).then_inc(brow_in, 16)
                    q = U_PAIRS // SLOTS + 2 * PAIR // SLOTS * c
                    units(w_in, q, GATE0 + (j + 1) * D + c * NBLK, PAIR * j, mod=every_other(8 + c, j))
                    units(w_up, q, c * NBLK, PAIR * j + BU, UPU, row=4 * (j + 1))
            for c in range(DC):
                units(w_out, U_OUT // SLOTS + 2 * c, c * NBLK, mod=every_other(12 + c // 2, c % 2))
            for i, col in enumerate(CTX_COLS):
                units(w_in2, U_CTX // SLOTS + 2 * i, col, mod=lambda u: mod_unit(14 + i, u))
            for i, col in enumerate(X_COLS):
                units(w_in2, U_X // SLOTS + 2 * i, col, mod=every_other(20 + i // 2, i % 2) if i < 4 else None)
            for c in range(DC):
                for i in range(BU):
                    row = UK * ((i + BU // 2) % BU)
                    unit(U_OUT2 // SLOTS + 2 * c + i // SLOTS, i % SLOTS, w_out2[:, row:row + UK, c * NBLK:(c + 1) * NBLK])
                    if c >= 2:
                        mod_unit(20 + c, i)

            def ffn_units(q, f, n):
                for i in range(BU):
                    slot = i % SLOTS
                    sp.wait_ge(lo_done, 4 * q + i + 1 - SLOTS)
                    dst = raw[:, slot, :, 0:2 * n].rearrange("p k (s c) -> p k s c", s=2)
                    for s in range(2):
                        sp.dma_start(dst[:, :, s], w_up2[:, UK * i:UK * i + UK, s, bass.ds(f, n)]).then_inc(raw_in[slot], 16)

            with sp.Fori(0, FB - 1) as i:
                ffn_units(U_FFN // SLOTS + 2 * i, T * i, T)
            ffn_units(U_FFN // SLOTS + 2 * (FB - 1), T * (FB - 1), P)
            with sp.Fori(0, DC // 2) as i:
                for k in range(2):
                    for u in range(DU):
                        s = DU * k + u
                        q = U_DOWN // SLOTS + 2 * DU // SLOTS * i + s // SLOTS
                        rows = w_dn[:, UK * u:min(UK * u + UK, FCH), bass.ds((2 * i + k) * NBLK, NBLK)]
                        unit(q, s % SLOTS, rows)
            for n in range(4):
                sp.wait_ge(S("out_done"), n + 1)
                rt, cols = n // 2, slice(n % 2 * D // 2, (n % 2 + 1) * D // 2)
                sp.dma_start(out_v[:, rt, cols], x2_sb[:, rt, cols]).then_inc(S("out_in"), 16)
            sp.wait_ge(S("out_in"), 64)

        @block.gpsimd
        def _(pool):
            def mod_store(lo, hi):
                with pool.Fori(lo, hi) as m:
                    pool.wait_ge(mod_evac, m + 1)
                    for g in range(4):
                        pool.dma_start(mod_d[g, :, bass.ds(m * NBLK, NBLK)], mrow[32 * g:32 * g + 2, :]).then_inc(mod_out, 16)
                    pool.wait_ge(mod_out, 64 * (m + 1))

            mod_store(0, 12)
            pool.wait_ge(evac_dve, 12)
            pool.dma_start(xres[:], xv).then_inc(S("xres_in"), 16)
            for r in range(2):
                for v in range(2):
                    for g in range(4):
                        at_row = 64 * v + 16 * g
                        pool.dma_start(mvr[at_row:at_row + 16, r], mod_d[g, r, v * D:(v + 1) * D].rearrange("(j p) -> j p", p=P)).then_inc(S("mvr_in"), 16)
            pool.dma_start(mvb[:, :], a["b_mod_2"][0, 0:2 * D].rearrange("(j p) -> j p", p=P)).then_inc(S("mvr_in"), 16)
            pool.wait_ge(S("tr_ps"), TR("merged"))
            pool.dma_start(ctx_sb[:], a["ctx_2"].rearrange("o (r p) d -> p (o r) d", p=P)).then_inc(S("ctx_in"), 16)
            pool.dma_start(wsm[:, :, 0:LR], w_in2[:, :, GLR:GLR + LR]).then_inc(S("wsm_in"), 16)
            pool.dma_start(wsm[:, :, LR:2 * LR], w_in2[:, :, MG:MG + LR]).then_inc(S("wsm_in"), 16)
            pool.dma_start(sx[:, 11, 0:LR], a["mlstm_b_gate_2"].rearrange("o d g h -> o (d g h)")[0].partition_broadcast(P)).then_inc(S("wsm_in"), 16)
            pool.dma_start(wlr[0:LR], a["gla_w_lr_2"].rearrange("o d r k -> r (o d) k")).then_inc(S("wlr_in"), 16)
            pool.dma_start(wlr[LR:LR + 1], a["gla_b_lr_2"]).then_inc(S("wlr_in"), 16)
            mod_store(12, 14)
            pool.wait_ge(evac_dve, 16)
            pool.dma_start(x1_d, xres[:]).then_inc(S("x1_out"), 16)
            mod_store(14, 22)
            pool.wait_ge(S("g_state"), 2)
            pool.dma_start(lsum[:], a["lsum"].rearrange("p (d l t) -> p d l t", d=2, l=LEVELS)).then_inc(S("lsum_in"), 16)
            pool.dma_start(lpair[:], a["lpair"].rearrange("p (d l t) -> p d l t", d=2, l=LEVELS)).then_inc(S("lsum_in"), 16)
            pool.wait_ge(S("y_ready"), 2 * HEADS)
            pool.wait_ge(S("x1_out"), 16)
            pool.dma_start(gtr[0:4], mod_d[:, 0, 2 * D:3 * D]).then_inc(S("gtr_in"), 16)
            pool.dma_start(gtr[4:5], a["b_mod_2"][:, 2 * D:3 * D]).then_inc(S("gtr_in"), 16)
            pool.dma_start(xres[:], x1_d).then_inc(S("xres_in2"), 16)
            for v in range(2):
                for g in range(4):
                    at_row = 64 * v + 16 * g
                    pool.dma_start(mvr[at_row:at_row + 16, 0], mod_d[g, 0, (3 + v) * D:(4 + v) * D].rearrange("(j p) -> j p", p=P)).then_inc(S("mvr_in2"), 16)
            pool.dma_start(mvb[:, :], a["b_mod_2"][0, 3 * D:5 * D].rearrange("(j p) -> j p", p=P)).then_inc(S("mvr_in2"), 16)
            wrows = a["conv_w_2"].rearrange("o y x (f p) -> (o y x f) p", p=P)
            n = 9 * FCH
            for t in range(4):
                k = min(P, n - P * t)
                pool.dma_start(cwr[0:k, t], wrows[P * t:P * t + k, :]).then_inc(S("cw_in"), 16)
            pool.dma_start(cwr[n - 3 * P:n - 3 * P + FCH, 3], a["conv_b_2"].rearrange("o (f p) -> (o f) p", p=P)).then_inc(S("cw_in"), 16)
            mod_store(22, 24)
            pool.wait_ge(evac_dve, 20)
            pool.dma_start(x2_d, xres[:]).then_inc(S("x2_out"), 16)
            pool.wait_ge(S("x2_out"), 16)
            pool.wait_ge(used, U_DOWN)
            pool.dma_start(x2_sb[:], x2_d).then_inc(S("x2_in"), 16)
            pool.dma_start(gfin[:], a["g_final_2"].partition_broadcast(P)).then_inc(S("x2_in"), 16)
            pool.wait_ge(S("f_fv"), FB)
            pool.dma_start(gtr2[0:4], mod_d[:, 0, 5 * D:6 * D]).then_inc(S("gtr2_in"), 16)
            pool.dma_start(gtr2[4:5], a["b_mod_2"][:, 5 * D:6 * D]).then_inc(S("gtr2_in"), 16)

        @block.scalar
        def _(act):
            me = Count(act, S("act_own"))

            def arrived(q, ffn):
                if isinstance(q, int):
                    return 16 * (q + 1 + min(max(q + 1 - U_FFN // SLOTS, 0), (U_DOWN - U_FFN) // SLOTS))
                return 16 * (q + 1 + q + 1 - U_FFN // SLOTS) if ffn else 16 * (q + 1)

            def split(q, slot, ffn=False):
                act.wait_ge(raw_in[slot], arrived(q, ffn))
                if not (isinstance(q, int) and q == 0):
                    act.wait_ge(used, 4 * q + slot + 1 - SLOTS)
                act.activation(w_hi[:, slot], raw[:, slot], ACT.Copy).then_inc(hi_done, 1)

            def splits(q, lo, hi, ffn=False):
                for i in range(lo, hi):
                    split(q + i // SLOTS, i % SLOTS, ffn)

            def turned(use, g):
                G = BU * tr_use[use] + g
                act.wait_ge(S("tr_val"), G + 1)
                act.activation(a_hi[:, UK * g:UK * g + UK], tmpT[:, g % 2], ACT.Copy).then_inc(S("tr_hi"), 1)

            def head(r, h, i):
                hh = HEADS * r + h
                src = br[r % 2]
                if i == (5 if hh == 0 else 4):
                    act.wait_ge(S("h_T"), hh + 1)
                    qs = vec[:, 52 + 2 * r:53 + 2 * r] if r < 2 else SCALE
                    ks = vec[:, 53 + 2 * r:54 + 2 * r] if r < 2 else 1.0
                    act.activation(qkgT[:, 0], pA[:, 0:T], ACT.Copy if r == 2 else ACT.Identity, scale=qs)
                    act.activation(qkgT[:, 1], pA[:, T:2 * T], ACT.Copy if r == 2 else ACT.Identity,
                                   scale=ks).then_inc(S("h_qkT"), 1)
                if i == (6 if r < 2 else 5):
                    if r < 2:
                        act.wait_ge(S("h_mx"), 4 * r + h + 1)
                        for rt in range(RT):
                            n = P * (rt + 1)
                            ins = act.activation(probs[:, rt, 0:n], pC[:, rt * T:rt * T + n], ACT.Exp,
                                                 bias=stat[:, 16 + rt:17 + rt], accum_out=stat[:, 20 + rt:21 + rt])
                        ins.then_inc(S("h_exp"), 1)
                    else:
                        act.wait_ge(S("h_L"), hh + 1)
                        me(act.activation(zwork[:, 0], pC[:, 0:3 * P], ACT.Abs))
                        me(act.activation(zwork[:, 0], zwork[:, 0], ACT.Exp, scale=-1.0))
                        act.activation(zwork[:, 0], zwork[:, 0], ACT.Ln, bias=1.0).then_inc(S("h_sp"), 1)
                if i == 8 and r == 2:
                    act.wait_ge(S("h_R"), h + 1)
                    act.activation(probsT[:, :], pC[:, 0:3 * P], ACT.Exp).then_inc(S("h_PTs"), 1)
                if i == 9:
                    act.wait_ge(S("h_y"), hh + 1)
                    act.activation(ys_hi[:, hh], yT[:, :], ACT.Copy).then_inc(S("h_yhi"), 1)

            act.wait_ge(S("eps_set"), 1)
            for rt in range(RT):
                act.wait_ge(S(f"x_in{rt}"), 16)
                act.activation(br[0][:, rt], x_sb[:, rt], ACT.Square, accum_out=stat[:, 32 + rt:33 + rt])
            act.activation(stat[:, 40:41], gbias[:, 0:1], ACT.Copy).then_inc(S("n_ss"), 1)
            act.wait_ge(S("cs_zero"), 1)
            for r in range(2):
                ins = act.activation(cs[:, :, r], pC[:, 56 + 16 * r:72 + 16 * r], ACT.Silu)
            ins.then_inc(S("cs_set"), 1)
            splits(0, 0, 2)

            def forget_gates(B, i):
                if (B, i) == (2, 6):
                    act.wait_ge(S("f_val"), 1)
                    me(act.activation(fl[:, 3:5, 0:HEADS], fl[:, 1:3, 0:HEADS], ACT.Abs))
                    me(act.activation(fl[:, 3:5, 0:HEADS], fl[:, 3:5, 0:HEADS], ACT.Exp, scale=-1.0))
                    act.activation(fl[:, 3:5, 0:HEADS], fl[:, 3:5, 0:HEADS], ACT.Ln, bias=1.0).then_inc(S("f_sp"), 1)

            for seg in range(4):
                for b in range(4):
                    B = 4 * seg + b
                    for i in range(2, 10):
                        if B == 0:
                            turned("x", i - 2)
                        splits(2 * B, i, i + 1)
                        if seg:
                            head(seg - 1, b, i)
                        else:
                            forget_gates(B, i)
                    act.wait_ge(used, BU * (B + 1))
                    if seg < 3:
                        act.activation(br[seg % 2][:, :, b * BW:(b + 1) * BW], gemm_ps[:, B % 2],
                                       ACT.Silu if b == 3 else ACT.Copy).then_inc(evac_act, 1)
                    else:
                        act.activation(xn[:, :, b * NBLK:(b + 1) * NBLK], gemm_ps[:, B % 2],
                                       ACT.Sigmoid).then_inc(evac_act, 1)
            splits(U_UP0 // SLOTS, 2, UPU * DC + 2)
            with act.Fori(0, DC) as c:
                q = U_PAIRS // SLOTS + 2 * PAIR // SLOTS * c
                for j in range(2):
                    splits(q, PAIR * j + 2, PAIR * j + BU + 2)
                    act.wait_ge(used, U_PAIRS + 2 * PAIR * c + PAIR * j + BU)
                    act.wait_ge(evac_dve, DC + 2 * c + j)
                    act.activation(sg[:], gemm_ps[:, 0], ACT.Sigmoid).then_inc(evac_act, 1)
                    splits(q, PAIR * j + BU + 2, PAIR * j + PAIR + 2)

            def sums(src, rt):
                act.activation(xn[:, rt], src[:, rt], ACT.Square, accum_out=stat[:, 32 + rt:33 + rt])
                if rt == RT - 1:
                    act.activation(stat[:, 40:41], gbias[:, 0:1], ACT.Copy).then_inc(S("n_ss"), 1)

            def squares_of(c, src, junk):
                for rt in range(RT):
                    at_col = 48 + DC * rt + c
                    ins = act.activation(junk(rt), src[:, rt, c * NBLK:(c + 1) * NBLK], ACT.Square, accum_out=stat[:, at_col:at_col + 1])
                me(ins)

            def sum_of_parts():
                for rt in range(RT):
                    ins = act.activation(stat[:, 56 + DC * rt:56 + DC * (rt + 1)], stat[:, 48 + DC * rt:48 + DC * (rt + 1)], ACT.Copy,
                                         accum_out=stat[:, 32 + rt:33 + rt])
                ins.then_inc(S("n_ss"), 1)

            def log_sigmoid_part(out, src):
                me(act.activation(out, src, ACT.Abs))
                me(act.activation(out, out, ACT.Exp, scale=-1.0))
                return act.activation(out, out, ACT.Ln, bias=1.0)

            for c in range(DC):
                for i in range(2, 10):
                    if c == 0:
                        turned("merged", i - 2)
                    splits(U_OUT // SLOTS + 2 * c, i, i + 1)
                    if c == 1 and i in (4, 7):
                        if i == 4:
                            act.wait_ge(S("ctx_in"), 16)
                            act.wait_ge(evac_dve, 12)
                        sums(ctx_sb, (i - 4) // 3)
                    if c == DC - 1:
                        turned("ctx", i - 2)
            for cb in range(6):
                for i in range(2, 10):
                    splits(U_CTX // SLOTS + 2 * cb, i, i + 1)
                    if cb == 5:
                        turned("x1", i - 2)
                    if cb == 1 and i in (3, 6):
                        act.wait_ge(evac_dve, 16)
                        sums(xres, (i - 3) // 3)
                act.wait_ge(used, U_CTX + BU * (cb + 1))
                dst = cm if cb < 3 else cg
                act.activation(dst[:, :, cb % 3 * NBLK:(cb % 3 + 1) * NBLK], gemm_ps[:, (B_CTX + cb) % 2], ACT.Copy).then_inc(evac_act, 1)

            pre = sx[:, 0:2].rearrange("p a b -> p (a b)").rearrange("p (t d g h) -> p t d g h", t=4, d=2, g=2)
            sp8 = sx[:, 2].rearrange("p (t d h) -> p t d h", t=4, d=2)

            def step(s):
                if s == 13:
                    act.wait_ge(S("m_pre"), 1)
                    for d in range(2):
                        ins = act.activation(sp8[:, :, d], pre[:, :, d, 1], ACT.Abs)
                    me(ins)
                    me(act.activation(sx[:, 2], sx[:, 2], ACT.Exp, scale=-1.0))
                    act.activation(sx[:, 2], sx[:, 2], ACT.Ln, bias=1.0).then_inc(S("m_sp"), 1)
                if s == 20:
                    act.wait_ge(S("m_FM"), 1)
                    act.activation(sx[:, 6, 0:16], sx[:, 5, 0:16], ACT.Exp, scale=-1.0).then_inc(S("m_em"), 1)
                if 22 <= s < 30:
                    n = s - 22
                    act.wait_ge(S("g_dec"), n + 1)
                    if n >= 2:
                        act.wait_ge(S("g_la"), n - 1)
                    log_sigmoid_part(spd[:, n % 2], ps[:, n % 2]).then_inc(S("g_sp"), 1)
                if 30 <= s < 34:
                    m = s - 30
                    act.wait_ge(S("g_w"), m + 1)
                    if m >= 2:
                        act.wait_ge(S("g_kend"), m - 1)
                    act.activation(kexp[m % 2][:, :], (pC, pA)[m % 2], ACT.Exp).then_inc(S("g_kexp"), 1)
                if 34 <= s < 62:
                    h, i = (s - 34) // 7, (s - 34) % 7 + 2
                    if i == 2:
                        act.wait_ge(S("m_T"), h + 1)
                        act.activation(mkT[:, :], pA, ACT.Copy, scale=SCALE).then_inc(S("m_kT"), 1)
                    if i in (5, 7):
                        act.wait_ge(S("m_arg"), 2 * h + (i == 7) + 1)
                        act.activation(mpT[:, :], mpT[:, :], ACT.Exp, scale=-1.0).then_inc(S("m_exp"), 1)
                    if i == 8:
                        act.wait_ge(S("m_num"), 2 * h + 2)
                        act.activation(sx[:, 7, 0:4], pC[:, 0:4], ACT.Abs).then_inc(S("m_den"), 1)
                if s == 62:
                    act.wait_ge(S("g_S"), 1)
                    act.activation(state[:, 0].rearrange("p h v -> p (h v)"), ps[:, 0:2].rearrange("p a b -> p (a b)"),
                                   ACT.Copy).then_inc(S("g_state"), 1)
                if 64 <= s <= 96:
                    gla_consume(s - 64)
                if 66 <= s < 70:
                    act.wait_ge(S("m_y"), HEADS)
                    head_squares(HEADS + s - 66, S("y_ss_m"))
                if s in (74, 82, 90, 99):
                    h = (74, 82, 90, 99).index(s)
                    act.wait_ge(S("g_y"), h + 1)
                    head_squares(h, S("y_ss"))
                if s in (73, 81, 89, 98):
                    h = (73, 81, 89, 98).index(s)
                    act.wait_ge(S("g_o"), 4 * h + 4)
                    act.activation(y[:, :, h * GDV:(h + 1) * GDV], pD.rearrange("p (r v) -> p r v", r=RT),
                                   ACT.Copy).then_inc(S("g_y"), 1)

            def head_squares(g, summed):
                for rt in range(RT):
                    me(act.activation(hsq[:, rt], y[:, rt, g * GDV:(g + 1) * GDV], ACT.Square,
                                      accum_out=sx[:, 8, 8 * rt + g:8 * rt + g + 1]))
                act.activation(stat[:, 40:41], gbias[:, 0:1], ACT.Copy).then_inc(summed, 1)

            turn = [0]

            def take():
                act.wait_ge(S("g_ps"), turn[0] + 1)
                turn[0] += 1
                return ps[:, (turn[0] - 1) % 2]

            def gla_consume(k):
                gc, j = k // 2, k % 2
                h, c = gc // 4, gc % 4
                if j == 0 and gc and c % 2 == 0:
                    act.activation(sc[:, 2], take()[:, 0:P], ACT.Copy).then_inc(S("g_free"), 1)
                if k == 32:
                    return
                if j == 0 and c == 0:
                    bank = take()
                    if h:
                        act.wait_ge(S("g_mult"), 8 * h)
                    act.activation(gqT[:, 0], bank[:, 0:T], ACT.Copy, scale=SCALE)
                    act.activation(gqT[:, 1], bank[:, T:2 * T], ACT.Copy).then_inc(S("g_free"), 1)
                if j == 0:
                    bank = take()
                    if gc >= 2:
                        act.wait_ge(S("g_o"), gc - 1)
                    act.activation(cr[:, c % 2], bank[:, 0:P], ACT.Exp)
                    act.activation(fq[:, gc % 2], bank[:, P:2 * P], ACT.Exp).then_inc(S("g_free"), 1)
                bank = take()
                if k >= 2:
                    act.wait_ge(S("g_sc"), k - 1)
                act.activation(ek[:, k % 2].rearrange("p l t -> p (l t)"), bank, ACT.Exp).then_inc(S("g_free"), 1)

            for xb in range(12):
                for i in range(2, 10):
                    splits(U_X // SLOTS + 2 * xb, i, i + 1)
                    step(8 * xb + i)
                act.wait_ge(used, U_X + BU * (xb + 1))
                at_col = ((xb + 2) % 4 if xb >= 8 else xb % 4) * NBLK
                dst = (xm, xg, gates)[xb // 4][:, :, at_col:at_col + NBLK]
                if xb == 0:
                    act.wait_ge(S("x1_out"), 16)
                act.activation(dst, gemm_ps[:, (B_X + xb) % 2],
                               ACT.Copy if xb < 8 else ACT.Sigmoid if xb < 10 else ACT.Silu).then_inc(evac_act, 1)
            for c in range(DC):
                for i in range(2, 10):
                    if c == 0:
                        turned("y", i - 2)
                    splits(U_OUT2 // SLOTS + 2 * c, i, i + 1)
                    if c == 0:
                        step(96 + i)
                    if c and i == 5:
                        act.wait_ge(evac_dve, 16 + c)
                        squares_of(c - 1, xres, lambda rt: y[:, rt, (c - 1) * NBLK:c * NBLK])
                    n = 8 * c + i - 8
                    if 0 <= n < DC:
                        act.wait_ge(S("gt_ps"), n + 1)
                        act.activation(gtb[:, n * NBLK:(n + 1) * NBLK], pC, ACT.Copy, scale=-1.0).then_inc(S("gt_in"), 1)
            act.wait_ge(evac_dve, 20)
            squares_of(DC - 1, xres, lambda rt: y[:, rt, (DC - 1) * NBLK:DC * NBLK])
            sum_of_parts()

            def ffn_hook(b, i, par, start, finish):
                if i == 3 and finish:
                    act.wait_ge(S("f_acc"), b - 1)
                    act.activation(sil[:, 0:finish], acc[:, 0:finish], ACT.Silu).then_inc(S("f_sil"), 1)
                if i == 5 and finish:
                    act.wait_ge(S("f_fv"), b - 1)
                    act.activation(ft_hi[:, bass.ds((b - 2) * 2, finish)], fv[:, 0:finish], ACT.Copy).then_inc(S("f_hi"), 1)
                if i == 6 and start:
                    act.wait_ge(S("f_T"), b)
                    src = pA[:, 0:start * T].rearrange("p (f y x) -> p f y x", f=start, y=4)
                    for f in range(start):
                        ins = act.activation(gp[:, f, 1:5, 1:65], src[:, f], ACT.Copy)
                    me(ins)
                    for f in range(start):
                        fc = (b - 1) * 2 + f
                        ins = act.activation(acc[:, f].rearrange("p (y x) -> p y x", y=4), gp[:, f, 0:4, 0:64], ACT.Identity,
                                             scale=cw[:, bass.ds(fc, 1)], bias=cw[:, bass.ds(9 * FCH + fc, 1)])
                    ins.then_inc(S("f_tap0"), 1)

            def ffn_block(b, par, start=2, finish=2):
                for i in range(2, 10):
                    if isinstance(b, int) and b == 0:
                        turned("x2", i - 2)
                    splits(U_FFN // SLOTS + 2 * b, i, i + 1, ffn=True)
                    ffn_hook(b, i, par, start, finish)
                act.wait_ge(used, U_FFN + BU * (b + 1))
                if start:
                    act.wait_ge(S("f_T"), b)
                act.activation(ub[:, par], gemm_ps[:, par], ACT.Copy).then_inc(evac_act, 1)

            ffn_block(0, 0, 0, 0)
            act.wait_ge(S("gp_zero"), 2)
            ffn_block(1, 1, 2, 0)
            first = me.n
            with act.Fori(0, 9) as n:
                me.iteration(first, 2 * n)
                for k in range(2):
                    ffn_block(2 * n + 2 + k, k)
            me.iteration(first + 18, 0)
            ffn_block(20, 0)
            ffn_block(21, 1)
            for i in range(2, 10):
                splits(U_DOWN // SLOTS, i, i + 1)
                ffn_hook(22, i, 0, 1, 2)
            for i in range(2, 10):
                splits(U_DOWN // SLOTS + 2, i, i + 1)
                ffn_hook(23, i, 1, 0, 1)
            splits(U_DOWN // SLOTS, 18, DU + 2)
            act.wait_ge(S("gt_ps"), DC + 1)
            act.activation(gt2b[:, :], ps[:].rearrange("p a b -> p (a b)"), ACT.Copy, scale=-1.0).then_inc(S("gt_in"), 1)
            splits(U_DOWN // SLOTS, DU + 2, DU + 4)
            for c in range(DC):
                if 0 < c < DC - 1:
                    splits(U_DOWN // SLOTS, DU * c + 4, DU * (c + 1) + 4)
                if c == DC - 2:
                    splits(U_DOWN // SLOTS, DU * (c + 1) + 4, DC * DU)
                act.wait_ge(evac_dve, 21 + c)
                squares_of(c, x2_sb, lambda rt: squares[:, rt])
            sum_of_parts()

        @block.vector
        def _(dve):
            me = Count(dve, S("dve_own"))

            def split(q, slot):
                dve.wait_ge(hi_done, 4 * q + slot + 1)
                dve.tensor_tensor(w_lo[:, slot], raw[:, slot], w_hi[:, slot].bitcast(F32), ALU.subtract).then_inc(lo_done, 1)

            def splits(q, lo, hi):
                for i in range(lo, hi):
                    split(q + i // SLOTS, i % SLOTS)

            def inverse_root(ss, r, mean_of, t, u):
                me(dve.tensor_scalar(t, ss, 1.0 / mean_of, EPS, ALU.mult, ALU.add))
                me(dve.tensor_scalar(r.bitcast(I32), t.bitcast(I32), 1, None, ALU.logical_shift_right))
                me(dve.tensor_scalar(r.bitcast(I32), r.bitcast(I32), -1.0, float(ROOT_BITS), ALU.mult, ALU.add))
                me(dve.tensor_scalar(t, t, -0.5, None, ALU.mult))
                for _ in range(3):
                    me(dve.tensor_tensor(u, r, r, ALU.mult))
                    me(dve.tensor_tensor(u, u, t, ALU.mult))
                    me(dve.scalar_tensor_tensor(out=r, in0=u, scalar=1.5, in1=r, op0=ALU.add, op1=ALU.mult))

            def turned(use, g, scale=None, bias=None):
                G = BU * tr_use[use] + g
                dve.wait_ge(S("tr_ps"), G + 1)
                if g >= 2:
                    dve.wait_ge(S("tr_hi"), G - 1)
                bank = ps[:, g % 2]
                if scale is None:
                    dve.tensor_copy(tmpT[:, g % 2].rearrange("p a b -> p (a b)"), bank).then_inc(S("tr_val"), 1)
                else:
                    for k in range(UK):
                        kc = UK * g + k
                        b = bias[:, kc:kc + 1] if bias is not None else None
                        ins = dve.tensor_scalar(tmpT[:, g % 2, k], bank[:, k * T:(k + 1) * T], scale[:, kc:kc + 1], b,
                                                ALU.mult, ALU.add if bias is not None else ALU.bypass)
                    ins.then_inc(S("tr_val"), 1)

            def turned_rest(use, g):
                dve.wait_ge(S("tr_hi"), BU * tr_use[use] + g + 1)
                dve.tensor_tensor(a_lo[:, UK * g:UK * g + UK], tmpT[:, g % 2],
                                  a_hi[:, UK * g:UK * g + UK].bitcast(F32), ALU.subtract).then_inc(S("tr_lo"), 1)

            def diagonals():
                inverse_root(stat[:, 32:34], stat[:, 34:36], D, stat[:, 36:38], stat[:, 38:40])
                for rt in range(RT):
                    ins = dve.tensor_scalar(diag[:, rt], ident, stat[:, 34 + rt:35 + rt], None, ALU.mult)
                ins.then_inc(S("diag_set"), 1)

            def q_and_k(hh):
                h = hh % HEADS
                return br[hh // HEADS % 2][:, :, 0:2 * BW].rearrange("p r (t c) -> p r t c", t=2)[:, :, :, h * HD:(h + 1) * HD]

            def normed(n):
                inverse_root(stat[:, 0:4], stat[:, 4:8], HD, stat[:, 8:12], stat[:, 12:16])
                for rt in range(RT):
                    for t in range(2):
                        c = 2 * rt + t
                        ins = dve.tensor_scalar(qkn[:, rt, t], q_and_k(n)[:, rt, t], stat[:, 4 + c:5 + c], None, ALU.mult)
                ins.then_inc(S("h_pre"), 1)

            def head(r, h, i):
                hh = HEADS * r + h
                if (hh == 0 and i == 2) or (hh < 2 * HEADS - 1 and i == 8):
                    n = 0 if i == 2 else hh + 1
                    if n % HEADS == 0:
                        dve.wait_ge(evac_act, 4 * (n // HEADS) + 2)
                    if n:
                        dve.wait_ge(S("h_T"), n)
                    qkn_of = q_and_k(n)
                    for rt in range(RT):
                        ins = dve.tensor_tensor(qkn[:, rt], qkn_of[:, rt], qkn_of[:, rt], ALU.mult)
                    me(ins)
                    me(dve.tensor_reduce(stat[:, 0:4], qkn[:].rearrange("p r t c -> p (r t) c"), AX_X, ALU.add))
                if hh == 0 and i == 4:
                    normed(0)
                if i == (5 if hh == 0 else 4):
                    dve.wait_ge(S("h_T"), hh + 1)
                    dve.tensor_copy(qkgT[:, 2], pB[:, 0:T]).then_inc(S("h_gT"), 1)
                if i == 6 and r < 2:
                    dve.wait_ge(S("h_L"), hh + 1)
                    if r < 2:
                        for rt in range(RT):
                            ins = dve.tensor_reduce(stat[:, 18 + rt:19 + rt], pC[:, rt * T:rt * T + P * (rt + 1)], AX_X, ALU.max)
                        me(ins)
                        dve.tensor_scalar(stat[:, 16:18], stat[:, 18:20], -1.0, None, ALU.mult).then_inc(S("h_mx"), 1)
                if i == (7 if r < 2 else 6):
                    if r < 2:
                        dve.wait_ge(S("h_exp"), 4 * r + h + 1)
                        me(dve.reciprocal(stat[:, 22:24], stat[:, 20:22]))
                        for rt in range(RT):
                            n = P * (rt + 1)
                            ins = dve.tensor_scalar(probs[:, rt, 0:n], probs[:, rt, 0:n], stat[:, 22 + rt:23 + rt], None, ALU.mult)
                        ins.then_inc(S("h_p"), 1)
                    else:
                        dve.wait_ge(S("h_sp"), h + 1)
                        me(dve.scalar_tensor_tensor(out=zwork[:, 1], in0=pC[:, 0:3 * P], scalar=0.0, in1=zwork[:, 0],
                                                    op0=ALU.max, op1=ALU.add))
                        dve.tensor_tensor(zwork[:, 1], zwork[:, 1], C("strict"), ALU.mult).then_inc(S("h_p"), 1)
                if i == 8 and r < 2:
                    dve.wait_ge(S("h_PT"), 4 * r + h + 1)
                    dve.tensor_copy(probsT[:, :], pA[:, 0:3 * P]).then_inc(S("h_PTs"), 1)
                if i == 9:
                    dve.wait_ge(S("h_O"), hh + 1)
                    if hh > 0:
                        dve.wait_ge(S("h_yhi"), hh)
                    dve.tensor_tensor(yT[:, :], pB[:, 0:T], qkgT[:, 2], ALU.mult).then_inc(S("h_y"), 1)
                    dve.wait_ge(S("h_yhi"), hh + 1)
                    dve.tensor_tensor(ys_lo[:, hh], yT[:, :], ys_hi[:, hh].bitcast(F32), ALU.subtract).then_inc(S("h_ylo"), 1)
                    if hh < 2 * HEADS - 1:
                        normed(hh + 1)

            def mod_copy(m):
                dve.wait_ge(mod_used, BU * (m + 1))
                if not (isinstance(m, int) and m == 0):
                    dve.wait_ge(mod_out, 64 * m)
                dve.tensor_copy(mrow[:, :], pD).then_inc(mod_evac, 1)

            dve.memset(gbias[:, :], EPS).then_inc(S("eps_set"), 1)
            dve.memset(wf[:], 0.0).then_inc(S("wf_zero"), 1)
            dve.wait_ge(S("vec_in"), 144)
            N = 2 * MAX_REL + 1
            dve.tensor_copy(rel_ext[:, 0:N], rrows[0:HEADS, 0:N])
            dve.tensor_copy(rel_ext[:, N:384], rrows[0:HEADS, N - 1:N].to_broadcast([HEADS, 384 - N])).then_inc(S("rel_ext"), 1)
            dve.wait_ge(S("n_vecT"), 1)
            me(dve.tensor_copy(vec[:, 0:52], pC[:, 0:52]))
            dve.tensor_copy(vec[:, 56:60], pC[:, 52:56])
            dve.memset(cs[:], 0.0).then_inc(S("cs_zero"), 1)
            for r in range(2):
                dve.tensor_scalar(vec[:, 52 + 2 * r:53 + 2 * r], vec[:, 48 + 2 * r:49 + 2 * r], SCALE, None, ALU.mult)
                me(dve.tensor_copy(vec[:, 53 + 2 * r:54 + 2 * r], vec[:, 49 + 2 * r:50 + 2 * r]))
            dve.wait_ge(S("n_ss"), 1)
            diagonals()
            splits(0, 0, 2)

            def forget_gates(B, i):
                if (B, i) == (2, 3):
                    dve.wait_ge(S("f_parts"), 1)
                    dve.tensor_copy(fparts[:, :], pC[:, 0:T]).then_inc(S("f_copied"), 1)
                if (B, i) == (2, 5):
                    dve.wait_ge(S("f_ps"), 1)
                    dve.tensor_tensor(fl[:, 1:3, 0:HEADS], pC[:, T:T + 64].rearrange("p (r h) -> p r h", r=RT)[:, :, 0:HEADS],
                                      fl[:, 0:1, 0:HEADS].to_broadcast([P, RT, HEADS]), ALU.add).then_inc(S("f_val"), 1)
                if (B, i) == (2, 8):
                    dve.wait_ge(S("f_sp"), 1)
                    dve.scalar_tensor_tensor(out=fl[:, 5:7, 0:HEADS], in0=fl[:, 1:3, 0:HEADS], scalar=0.0,
                                             in1=fl[:, 3:5, 0:HEADS], op0=ALU.min, op1=ALU.subtract).then_inc(S("f_log"), 1)
                if (B, i) == (3, 5):
                    dve.wait_ge(S("f_c"), 1)
                    dve.tensor_copy(cneg[0:HEADS, :], pC[0:HEADS, 0:T]).then_inc(S("f_cneg"), 1)

            for seg in range(4):
                for b in range(4):
                    B = 4 * seg + b
                    for i in range(2, 10):
                        if B == 0:
                            turned("x", i - 2, vec[:, 0:16])
                            turned_rest("x", i - 2)
                        splits(2 * B, i, i + 1)
                        if seg:
                            head(seg - 1, b, i)
                        else:
                            forget_gates(B, i)
                    if B % 2:
                        mod_copy(B // 2)

            for c in range(DC):
                splits(U_UP0 // SLOTS, UPU * c + 2, UPU * c + 4)
                dve.wait_ge(used, U_UP0 + UPU * (c + 1))
                cols = slice(c * NBLK, (c + 1) * NBLK)
                dve.tensor_tensor(merged[:, :, cols], gemm_ps[:, (B_UP0 + c) % 2], xn[:, :, cols], ALU.mult).then_inc(evac_dve, 1)
            first = me.n
            with dve.Fori(0, DC) as c:
                me.iteration(first, 2 * c)
                q = U_PAIRS // SLOTS + 2 * PAIR // SLOTS * c
                for j in range(2):
                    splits(q, PAIR * j + 2, PAIR * j + PAIR + 2)
                    dve.wait_ge(evac_act, 16 + 2 * c + j + 1)
                    dve.wait_ge(used, U_PAIRS + 2 * PAIR * c + PAIR * (j + 1))
                    me(dve.tensor_tensor(sg[:], gemm_ps[:, 1], sg[:], ALU.mult))
                    m = merged[:, :, bass.ds(c * NBLK, NBLK)]
                    dve.tensor_tensor(m, m, sg[:], ALU.add).then_inc(evac_dve, 1)
                mod_copy(8 + c)
            me.iteration(first + 2 * DC, 0)
            def mod_vectors(bank, cols, g, bias):
                both = vec[:, cols:cols + 32]
                dve.tensor_reduce(both.rearrange("p (v j) -> p v j", v=2),
                                  bank.rearrange("p (v g j) -> p v j g", v=2, g=4), AX_X, ALU.add)
                me(dve.engine_nop())
                me(dve.tensor_tensor(both, bias, both, ALU.add))
                s = vec[:, cols + 16:cols + 32]
                me(dve.scalar_tensor_tensor(out=s, in0=s, scalar=1.0, in1=g, op0=ALU.add, op1=ALU.mult))

            def modulation_vectors():
                dve.wait_ge(S("mv_ps"), 1)
                for r in range(2):
                    mod_vectors(pC[:, r * P:(r + 1) * P], 60 + 32 * r, vec[:, 16:32], pC[:, 2 * P:2 * P + 32])
                for j in range(2):
                    for kc in range(4):
                        at_col = 8 * (1 - j) + 2 * kc
                        dve.tensor_copy(vec[:, at_col:at_col + 2], vec[:, 56 + 2 * j:58 + 2 * j])
                me(dve.engine_nop())
                dve.engine_nop().then_inc(S("mv_done"), 1)

            for c in range(DC):
                for i in range(2, 10):
                    if c == 0:
                        turned("merged", i - 2)
                        turned_rest("merged", i - 2)
                    splits(U_OUT // SLOTS + 2 * c, i, i + 1)
                    if c == 2 and i == 3:
                        dve.wait_ge(S("n_ss"), 2)
                        diagonals()
                    if c == 2 and i == 7:
                        modulation_vectors()
                    if c == DC - 1:
                        turned("ctx", i - 2, vec[:, 108:124], vec[:, 92:108])
                        turned_rest("ctx", i - 2)
                dve.wait_ge(used, U_OUT + BU * (c + 1))
                if c == 0:
                    dve.wait_ge(S("xres_in"), 16)
                xs = xres[:, :, c * NBLK:(c + 1) * NBLK]
                dve.tensor_tensor(xs, gemm_ps[:, c % 2], xs, ALU.add).then_inc(evac_dve, 1)
                if c % 2:
                    mod_copy(12 + c // 2)

            def small_parts(n):
                dve.wait_ge(S("s_ps"), n + 1)
                dve.tensor_copy(zparts[:, :], pC[:, 0:T]).then_inc(S("s_parts"), 1)

            def small_sums(n):
                dve.wait_ge(S("s_tok"), n + 1)
                dve.tensor_copy(sm[:, 2 * n:2 * n + 2], pC[:, T:T + 64].rearrange("p (r c) -> p r c", r=RT)).then_inc(S("sm_in"), 1)
                dve.wait_ge(S("sm_in"), n + 1)

            for cb in range(6):
                for i in range(2, 10):
                    splits(U_CTX // SLOTS + 2 * cb, i, i + 1)
                    if cb == 5:
                        turned("x1", i - 2, vec[:, 76:92], vec[:, 60:76])
                        turned_rest("x1", i - 2)
                    if cb == 1 and i == 3:
                        small_parts(0)
                    if cb == 1 and i == 5:
                        small_sums(0)
                    if cb == 2 and i == 4:
                        dve.wait_ge(S("n_ss"), 3)
                        diagonals()
                mod_copy(14 + cb)

            pre_all = sx[:, 0:2].rearrange("p a b -> p (a b)")
            pre = pre_all.rearrange("p (t d g h) -> p t d g h", t=4, d=2, g=2)
            t8 = lambda row, t=4: sx[:, row, 0:8 * t].rearrange("p (t d h) -> p t d h", t=t, d=2)
            G8, FM = t8(4), t8(5, 2)
            bc = lambda ap, n: ap.rearrange("p (o t) -> p o t", o=1).to_broadcast([P, n, P])

            def step(s):
                if s == 10:
                    small_parts(1)
                if s == 12:
                    small_sums(1)
                    dve.wait_ge(S("wsm_in"), 48)
                    dve.tensor_tensor(pre_all.rearrange("p (t c) -> p t c", t=4), sm[:, :, LR:2 * LR],
                                      sx[:, 11:12, 0:LR].to_broadcast([P, 4, LR]), ALU.add).then_inc(S("m_pre"), 1)
                if s == 14:
                    dve.wait_ge(S("m_sp"), 1)
                    for d in range(2):
                        ins = dve.scalar_tensor_tensor(out=t8(3)[:, :, d], in0=pre[:, :, d, 1], scalar=0.0, in1=t8(2)[:, :, d],
                                                       op0=ALU.min, op1=ALU.subtract)
                    ins.then_inc(S("m_lf"), 1)
                if s == 16:
                    dve.wait_ge(S("m_F"), 1)
                    F = pC[:, P:P + 32].rearrange("p (t d h) -> p t d h", t=4, d=2)
                    for d in range(2):
                        for r, sign in ((0, NORMALIZER), (2, -NORMALIZER)):
                            dve.scalar_tensor_tensor(out=G8[:, r:r + 2, d], in0=F[:, r:r + 2, d], scalar=sign,
                                                     in1=pre[:, r:r + 2, d, 0], op0=ALU.mult, op1=ALU.add)
                    me(dve.tensor_scalar(FM, F[:, 2:4], NORMALIZER, None, ALU.mult))
                    dve.engine_nop().then_inc(S("m_G"), 1)
                if s == 17:
                    dve.wait_ge(S("m_GT"), 1)
                    me(dve.tensor_copy(grows[:, :], pA[0:8, :]))
                    me(dve.tensor_reduce(stat[0:8, 44:45], grows[:, 0:T], AX_X, ALU.max))
                    x = grows[:, T:2 * T]
                    dve.tensor_tensor_scan(mrows[:, 0], x, x, stat[0:8, 44:45], ALU.max, ALU.max)
                    me(dve.tensor_tensor_scan(mrows[:, 1, ::-1], x[:, ::-1], x[:, ::-1], stat[0:8, 44:45], ALU.max, ALU.max))
                    dve.engine_nop().then_inc(S("m_rows"), 1)
                if s == 19:
                    dve.wait_ge(S("m_MT"), 1)
                    M = pB[:, 0:32].rearrange("p (r w d h) -> p r w d h", r=RT, w=2, d=2)
                    for d in range(2):
                        ins = dve.tensor_tensor(FM[:, :, d], M[:, :, d, d], FM[:, :, d], ALU.add)
                    ins.then_inc(S("m_FM"), 1)
                if s == 20:
                    me(dve.memset(glrT[:, :], 1.0))
                    dve.wait_ge(S("g_glr"), 1)
                    dve.tensor_copy(glrT[0:LR, :], pA[0:LR, :]).then_inc(S("g_glrT"), 1)
                if 23 <= s < 31:
                    n = s - 23
                    t, d = n // 2, n % 2
                    dve.wait_ge(S("g_sp"), n + 1)
                    dst = y[:, t, 2 * BW + d * BW:2 * BW + (d + 1) * BW] if t < 2 else la[:, t - 2, d]
                    dve.scalar_tensor_tensor(out=dst, in0=ps[:, n % 2], scalar=0.0, in1=spd[:, n % 2],
                                             op0=ALU.min, op1=ALU.subtract).then_inc(S("g_la"), 1)
                if 31 <= s < 35:
                    m = s - 31
                    t, d = m // 2, m % 2
                    dve.wait_ge(S("g_kexp"), m + 1)
                    dve.tensor_tensor(y[:, t, d * BW:(d + 1) * BW], kexp[m % 2][:, :], cg[:, t, 0:BW], ALU.mult).then_inc(S("g_kend"), 1)
                if 34 <= s < 62:
                    h, i = (s - 34) // 7, (s - 34) % 7 + 2
                    if i == 2:
                        dve.wait_ge(S("m_T"), h + 1)
                        dve.tensor_copy(mqT[:, :], pB[:, 0:T]).then_inc(S("m_qT"), 1)
                    if i in (4, 6):
                        d = i == 6
                        dve.wait_ge(S("m_QK"), h + 1)
                        if h or d:
                            dve.wait_ge(S("m_num"), 2 * h + d)
                        M = pC[:, d * T:(d + 1) * T]
                        for n, (t, lo, hi) in enumerate(tiles[d]):
                            at0 = 2 * P * n
                            ins = dve.tensor_scalar(mpT[:, at0:at0 + hi - lo], M[:, lo:hi], G8[:, t, d, h:h + 1], 0.0,
                                                    ALU.subtract, ALU.max)
                        ins.then_inc(S("m_arg"), 1)
                    if i in (5, 7):
                        d = i == 7
                        dve.wait_ge(S("m_exp"), 2 * h + d + 1)
                        qk = ps[:, 0:2].rearrange("p a b -> p (a b)")
                        for n, (t, lo, hi) in enumerate(tiles[d]):
                            at0 = 2 * P * n
                            dst = mpT[:, at0:at0 + hi - lo]
                            ins = dve.tensor_tensor(dst, qk[:, t * T + lo:t * T + hi], dst, ALU.mult)
                        me(ins)
                        a0, a1 = ((4, 6), (5, 6))[d]
                        for q in (a0, a1):
                            dst = mpT[:, q * P:(q + 1) * P]
                            ins = dve.tensor_tensor(dst, dst, C("le" if d else "ge"), ALU.mult)
                        ins.then_inc(S("m_s"), 1)
                    if i == 8:
                        dve.wait_ge(S("m_den"), h + 1)
                        dve.wait_ge(S("m_em"), 1)
                        em = t8(6, 2)
                        for d in range(2):
                            ins = dve.tensor_tensor(sx[:, 7, 4 + 2 * d:6 + 2 * d], sx[:, 7, 2 * d:2 * d + 2], em[:, :, d, h], ALU.max)
                        me(ins)
                        me(dve.reciprocal(sx[:, 10, 0:4], sx[:, 7, 4:8]))
                        for d in range(2):
                            for rt in range(RT):
                                dst = y[:, rt, D // 2 + h * GDV:D // 2 + (h + 1) * GDV]
                                src = (pD, pA)[d][:, rt * GDV:(rt + 1) * GDV]
                                r = sx[:, 10, 2 * d + rt:2 * d + rt + 1]
                                if d == 0:
                                    ins = dve.tensor_scalar(dst, src, r, None, ALU.mult)
                                else:
                                    ins = dve.scalar_tensor_tensor(out=dst, in0=src, scalar=r, in1=dst, op0=ALU.mult, op1=ALU.add)
                            if d == 0:
                                me(ins)
                        ins.then_inc(S("m_y"), 1)
                if s == 62:
                    dve.wait_ge(S("g_S"), 1)
                    dve.tensor_copy(state[:, 1].rearrange("p h v -> p (h v)"), ps[:, 2:4].rearrange("p a b -> p (a b)")).then_inc(S("g_state"), 1)
                if 65 <= s < 97:
                    gla_mult(s - 65)
                if 66 <= s < 98:
                    gla_mask(s - 66)
                if s == 72:
                    dve.wait_ge(S("y_ss_m"), HEADS)
                    head_norms(slice(HEADS, 2 * HEADS))
                if 84 <= s < 88:
                    if s == 84:
                        dve.wait_ge(evac_act, 40)
                    gated(HEADS + s - 84)
                if s in (92, 93, 98, 101):
                    h = (92, 93, 98, 101).index(s)
                    dve.wait_ge(S("y_ss"), h + 1)
                    head_norms(slice(h, h + 1))
                    dve.wait_ge(evac_act, 41 + h // 2)
                    gated(h)

            def head_norms(g):
                m = lambda row: sx[:, row, 0:16].rearrange("p (r g) -> p r g", r=RT)[:, :, g]
                inverse_root(m(8), m(9), GDV, m(10), m(7))

            def gated(g):
                cols = slice(g * GDV, (g + 1) * GDV)
                for rt in range(RT):
                    ins = dve.scalar_tensor_tensor(out=y[:, rt, cols], in0=y[:, rt, cols], scalar=sx[:, 9, 8 * rt + g:8 * rt + g + 1],
                                                   in1=gates[:, rt, cols], op0=ALU.mult, op1=ALU.mult)
                ins.then_inc(S("y_ready"), 1)

            tiles = (((0, 0, T), (1, 0, T), (2, 0, T), (3, P, T)), ((0, 0, T), (1, 0, T), (3, 0, T), (2, 0, P)))

            def gla_mult(k):
                gc, j = k // 2, k % 2
                h, c = gc // 4, gc % 4
                d, rt = c // 2, c % 2
                base_turn = 15 * h + (1, 4, 8, 11)[c]
                q, kk = gqT[:, 0, rt * P:(rt + 1) * P], gqT[:, 1, rt * P:(rt + 1) * P]
                if j == 0:
                    dve.wait_ge(S("g_free"), base_turn + 1)
                    dve.tensor_tensor(cr[:, rt], cr[:, rt], q if d != rt else kk, ALU.mult)
                    dve.tensor_tensor(fq[:, gc % 2], fq[:, gc % 2], q, ALU.mult).then_inc(S("g_f"), 1)
                dve.wait_ge(S("g_free"), base_turn + 2 + j)
                if k:
                    dve.wait_ge(S("g_sc"), k)
                dve.tensor_tensor(rk[:], ek[:, k % 2], bc(kk, 4), ALU.mult)
                dve.tensor_tensor(ek[:, k % 2], ek[:, k % 2], bc(q, 4), ALU.mult).then_inc(S("g_mult"), 1)

            def gla_mask(k):
                gc, j = k // 2, k % 2
                d = gc % 4 // 2
                if k == 0:
                    dve.wait_ge(S("lsum_in"), 32)
                dve.wait_ge(S("g_sc"), k + 1)
                if k:
                    dve.wait_ge(S("g_mask"), k)
                dve.tensor_tensor(masked[:], pC.rearrange("p (l t) -> p l t", l=4), lpair[:, d, 4 * j:4 * j + 4],
                                  ALU.mult).then_inc(S("g_masked"), 1)
                dve.wait_ge(S("g_masked"), k + 1)
                if gc and j == 0:
                    dve.wait_ge(S("g_o"), gc)
                ins = dve.tensor_reduce(sc[:, j], masked[:].rearrange("p l t -> p t l"), AX_X, ALU.add)
                if j:
                    me(ins)
                    ins = dve.tensor_tensor(sc[:, 0], sc[:, 0], sc[:, 1], ALU.add)
                ins.then_inc(S("g_mask"), 1)

            for xb in range(12):
                for i in range(2, 10):
                    splits(U_X // SLOTS + 2 * xb, i, i + 1)
                    step(8 * xb + i)
                if xb in (1, 3):
                    mod_copy(20 + xb // 2)
            for c in range(DC):
                for i in range(2, 10):
                    if c == 0:
                        turned("y", i - 2, vec[:, 0:16])
                        turned_rest("y", i - 2)
                    splits(U_OUT2 // SLOTS + 2 * c, i, i + 1)
                    if c == 0:
                        step(96 + i)
                    if c == 1 and i == 7:
                        dve.wait_ge(S("mv_ps"), 2)
                        mod_vectors(pC[:, 0:P], 124, vec[:, 32:48], pC[:, P:P + 32])
                        dve.engine_nop().then_inc(S("mv_done"), 1)
                dve.wait_ge(S("gt_in"), c + 1)
                if c == 0:
                    dve.wait_ge(S("xres_in2"), 16)
                dve.wait_ge(used, U_OUT2 + BU * (c + 1))
                cols = slice(c * NBLK, (c + 1) * NBLK)
                for rt in range(RT):
                    ins = dve.tensor_tensor(sg[:, rt], gemm_ps[:, c % 2, rt], gtb[:, cols], ALU.mult)
                me(ins)
                dve.tensor_tensor(xres[:, :, cols], xres[:, :, cols], sg[:], ALU.add).then_inc(evac_dve, 1)
                if c >= 2:
                    mod_copy(20 + c)
            dve.wait_ge(S("cw_ps"), 1)
            dve.tensor_copy(cw[:, :], pC[:, 0:10 * FCH]).then_inc(S("gp_zero"), 1)
            dve.wait_ge(S("n_ss"), 4)
            diagonals()

            def ffn_hook(b, i, par, start, finish):
                if i == 4 and finish:
                    dve.wait_ge(S("f_sil"), b - 1)
                    dve.tensor_tensor(fv[:, 0:finish], sil[:, 0:finish], pB[:, 0:finish * T].rearrange("p (f t) -> p f t", f=finish),
                                      ALU.mult).then_inc(S("f_fv"), 1)
                if i == 6 and finish:
                    dve.wait_ge(S("f_hi"), b - 1)
                    at_f = bass.ds((b - 2) * 2, finish)
                    dve.tensor_tensor(ft_lo[:, at_f], fv[:, 0:finish], ft_hi[:, at_f].bitcast(F32), ALU.subtract).then_inc(S("f_lo"), 1)
                if i >= 7 and start:
                    if i == 7:
                        dve.wait_ge(S("f_tap0"), b)
                    for tap in {7: (1, 2, 3), 8: (4, 5, 6), 9: (7, 8)}[i]:
                        dy, dx = tap // 3, tap % 3
                        for f in range(start):
                            a_f = acc[:, f].rearrange("p (y x) -> p y x", y=4)
                            ins = dve.scalar_tensor_tensor(out=a_f, in0=gp[:, f, dy:dy + 4, dx:dx + 64],
                                                           scalar=cw[:, bass.ds(tap * FCH + (b - 1) * 2 + f, 1)], in1=a_f,
                                                           op0=ALU.mult, op1=ALU.add)
                        if tap < 8:
                            me(ins)
                        else:
                            ins.then_inc(S("f_acc"), 1)

            def ffn_block(b, par, start=2, finish=2):
                for i in range(2, 10):
                    first = isinstance(b, int) and b == 0
                    if first:
                        turned("x2", i - 2, vec[:, 140:156], vec[:, 124:140])
                        turned_rest("x2", i - 2)
                    splits(U_FFN // SLOTS + 2 * b, i, i + 1)
                    ffn_hook(b, i, par, start, finish)

            ffn_block(0, 0, 0, 0)
            dve.memset(gp[:], 0.0).then_inc(S("gp_zero"), 1)
            ffn_block(1, 1, 2, 0)
            dve.wait_ge(S("x2_out"), 16)
            first = me.n
            with dve.Fori(0, 9) as n:
                me.iteration(first, 14 * n)
                for k in range(2):
                    ffn_block(2 * n + 2 + k, k)
            me.iteration(first + 14 * 9, 0)
            ffn_block(20, 0)
            ffn_block(21, 1)
            for i in range(2, 10):
                splits(U_DOWN // SLOTS, i, i + 1)
                ffn_hook(22, i, 0, 1, 2)
            for i in range(2, 10):
                splits(U_DOWN // SLOTS + 2, i, i + 1)
                ffn_hook(23, i, 1, 0, 1)
            for c in range(DC):
                splits(U_DOWN // SLOTS, 18 if c == 0 else DU * c + 2, min(DU * (c + 1) + 2, DC * DU))
                if c == 0:
                    dve.wait_ge(S("gt_in"), DC + 1)
                    dve.wait_ge(S("x2_in"), 32)
                dve.wait_ge(used, U_DOWN + DU * (c + 1))
                cols = slice(c * NBLK, (c + 1) * NBLK)
                for rt in range(RT):
                    ins = dve.tensor_tensor(tmp_dn[:, rt], gemm_ps[:, c % 2, rt], gt2b[:, cols], ALU.mult)
                me(ins)
                dve.tensor_tensor(x2_sb[:, :, cols], x2_sb[:, :, cols], tmp_dn[:], ALU.add).then_inc(evac_dve, 1)
            dve.wait_ge(S("n_ss"), 5)
            inverse_root(stat[:, 32:34], stat[:, 34:36], D, stat[:, 36:38], stat[:, 38:40])
            for rt in range(RT):
                for half in range(2):
                    cols = slice(half * D // 2, (half + 1) * D // 2)
                    dve.scalar_tensor_tensor(out=x2_sb[:, rt, cols], in0=x2_sb[:, rt, cols], scalar=stat[:, 34 + rt:35 + rt],
                                             in1=gfin[:, cols], op0=ALU.mult, op1=ALU.mult).then_inc(S("out_done"), 1)


        @block.tensor
        def _(pe):
            def product(u0, slot0, bank, hi, lo, units, chunk0=0, opened=False, after=None, chunks=None, n=NBLK,
                        halfway=None, turning=None, turned=None,
                        turning_next=None):
                if turning:
                    turned = turning[0]
                    turn(*turning, 0)
                    turn(*turning, 1)
                chunks = chunks or units * UK
                for i in range(units):
                    slot = (slot0 + i) % SLOTS
                    if turned:
                        pe.wait_ge(S("tr_lo"), BU * tr_use[turned] + i + 1)
                    pe.wait_ge(lo_done, u0 + i + 1)
                    for kk in range(UK):
                        k = UK * i + kk
                        if k >= chunks:
                            continue
                        for rt in range(RT):
                            tok = slice(rt * P, (rt + 1) * P)
                            for part, (x, w) in enumerate(((hi, w_hi), (hi, w_lo), (lo, w_hi))):
                                mm = pe.matmul(gemm_ps[:, bank, rt, 0:n], x[:, chunk0 + k, tok], w[:, slot, kk, 0:n],
                                               start=(k == 0 and part == 0 and not opened),
                                               stop=(k == chunks - 1 and part == 2))
                        if halfway and kk == 0:
                            halfway(i)
                    mm.then_inc(used, 1)
                    if turning and i + 2 < BU:
                        turn(*turning, i + 2)
                    if turning_next:
                        turn(*turning_next, i)
                    if after:
                        after(i)

            def add_row(bank):
                for rt in range(RT):
                    pe.matmul(gemm_ps[:, bank, rt], C("sel", 1, 0, P), brow[:, :], start=True, stop=False)

            def mod_unit(m, i):
                if i == 0:
                    if not (isinstance(m, int) and m == 0):
                        pe.wait_ge(mod_evac, m)
                pe.wait_ge(mod_in[i % SLOTS], 16 * (2 * m + i // SLOTS + 1))
                for kk in range(UK):
                    k = UK * i + kk
                    g = k % 4
                    mm = pe.matmul(pD[32 * g:32 * g + 32, :], cs[:, k], mraw[:, i % SLOTS, kk],
                                   start=(k < 4), stop=(k >= KC - 4), skip_group_check=True)
                mm.then_inc(mod_used, 1)

            def every_other(m, half, u):
                if u % 2:
                    mod_unit(m, 4 * half + u // 2)

            def turn(use, src, scaled, first, g):
                G = BU * tr_use[use] + g
                if G >= 2:
                    pe.wait_ge(S("tr_val"), G - 1)
                if use == "y":
                    pe.wait_ge(S("y_ready"), g + 1)
                    if g < 2:
                        pe.wait_ge(S("g_free"), pe_turn[0])
                for k in range(UK):
                    for rt in range(RT):
                        kc = UK * g + k
                        out = ps[:, g % 2, k * T + rt * P:k * T + (rt + 1) * P]
                        from_col = (kc + first) % KC * P
                        part = src[:, rt, from_col:from_col + P]
                        if scaled:
                            mm = pe.matmul(out, part, diag[:, rt], start=True, stop=True)
                        else:
                            mm = pe.transpose(out, part, ident)
                mm.then_inc(S("tr_ps"), 1)

            def narrow_product(w):
                for k in range(KC):
                    g = k % 4
                    for part, x in enumerate((a_hi, a_lo)):
                        mm = pe.matmul(pC[32 * g:32 * g + 32, 0:T], w[:, k], x[:, k].bitcast(F32),
                                       start=(k < 4 and part == 0), stop=(k >= KC - 4 and part == 1), skip_group_check=True)
                return mm

            def stacked(parts):
                for rt in range(RT):
                    mm = pe.matmul(pC[:, T + 32 * rt:T + 32 * rt + 32], parts[:, rt * P:(rt + 1) * P], C("stack"),
                                   start=True, stop=True)
                return mm

            def head(r, h, u):
                hh = HEADS * r + h
                src = br[r % 2]
                qT, kT = qkgT[:, 0], qkgT[:, 1]
                if u == (2 if hh == 0 else 1):
                    if r < 2:
                        pe.wait_ge(S("h_pre"), hh + 1)
                    if h == 0:
                        pe.wait_ge(evac_act, 4 * (r + 1))
                    if hh > 0:
                        pe.wait_ge(S("h_y"), hh)
                    for rt in range(RT):
                        for t in range(2):
                            s = qkn[:, rt, t] if r < 2 else src[:, rt, t * BW + h * HD:t * BW + (h + 1) * HD]
                            pe.transpose(pA[:, t * T + rt * P:t * T + (rt + 1) * P], s, ident)
                        mm = pe.transpose(pB[:, rt * P:(rt + 1) * P], src[:, rt, 3 * BW + h * HD:3 * BW + (h + 1) * HD], ident)
                    mm.then_inc(S("h_T"), 1)
                if u == (3 if r < 2 else 2):
                    pe.wait_ge(S("h_qkT"), hh + 1)
                    if r < 2:
                        if hh == 0:
                            pe.wait_ge(S("f_cneg"), 1)
                        if hh == HEADS:
                            pe.wait_ge(S("rel_in"), 16)
                        if hh > 0:
                            pe.wait_ge(S("h_exp"), 4 * r + h)
                        for rt in range(RT):
                            n = P * (rt + 1)
                            out = pC[:, rt * T:rt * T + n]
                            pe.matmul(out, qT[:, rt * P:(rt + 1) * P], kT[:, 0:n], start=True, stop=False)
                            if r == 0:
                                pe.matmul(out, C("sel", HEADS, h * P, P), cneg[0:HEADS, 0:n], start=False, stop=False)
                            else:
                                for kt in range(rt + 1):
                                    d = (rt - kt) * P
                                    pe.matmul(out[:, kt * P:(kt + 1) * P], relb[:, h, d:d + P], C("anti"), start=False, stop=False)
                            mm = pe.matmul(out[:, rt * P:n], ident, C("m_causal" if r == 0 else "m_chunk"), start=False, stop=True)
                    else:
                        if h == 0:
                            pe.wait_ge(S("h_exp"), 2 * HEADS)
                        else:
                            pe.wait_ge(S("h_PTs"), hh)
                        pe.matmul(pC[:, 0:T], kT[:, 0:P], qT[:, 0:T], start=True, stop=False, skip_group_check=True)
                        mm = pe.matmul(pC[:, T:3 * P], kT[:, P:T], qT[:, P:T], start=False, stop=False, skip_group_check=True)
                    mm.then_inc(S("h_L"), 1)
                if u == 5:
                    pe.wait_ge(S("h_p"), hh + 1)
                    if r < 2:
                        for n, (rt, kt) in enumerate(((0, 0), (1, 0), (1, 1))):
                            mm = pe.transpose(pA[:, n * P:(n + 1) * P], probs[:, rt, kt * P:(kt + 1) * P], ident)
                        mm.then_inc(S("h_PT"), 1)
                    else:
                        lk = zwork[:, 1]
                        kw = dict(start=False, skip_group_check=True)
                        pe.matmul(pC[:, 0:T], C("neg_suf_in"), lk[:, 0:T], stop=False, **kw)
                        pe.matmul(pC[:, P:T], C("neg_all"), lk[:, T:3 * P], stop=False, **kw)
                        pe.matmul(pC[:, T:3 * P], C("neg_suf_in"), lk[:, T:3 * P], stop=False, **kw)
                        pe.matmul(pC[:, 0:P], ident, C("m_strict"), stop=False, **kw)
                        pe.matmul(pC[:, T:3 * P], ident, C("m_strict"), stop=True, **kw).then_inc(S("h_R"), 1)
                if u == 6:
                    pe.wait_ge(S("h_PTs"), hh + 1)
                    pe.wait_ge(S("h_gT"), hh + 1)
                    v = src[:, :, 2 * BW + h * HD:2 * BW + (h + 1) * HD]
                    pe.matmul(pB[:, 0:T], v[:, 0], probsT[:, 0:T], start=True, stop=False)
                    pe.matmul(pB[:, P:T], v[:, 1], probsT[:, T:3 * P], start=False, stop=True).then_inc(S("h_O"), 1)

            def forget_gates(B, u):
                if (B, u) == (0, 7):
                    pe.wait_ge(S("const_in"), 16)
                if (B, u) == (1, 7):
                    pe.wait_ge(S("wf_in"), 32)
                    narrow_product(wf).then_inc(S("f_parts"), 1)
                if (B, u) == (2, 1):
                    pe.wait_ge(S("f_copied"), 1)
                    stacked(fparts).then_inc(S("f_ps"), 1)
                if (B, u) == (3, 1):
                    pe.wait_ge(S("f_log"), 1)
                    lf = [fl[:, 5 + rt, 0:HEADS] for rt in range(RT)]
                    crow = pC[0:HEADS, 0:T]
                    pe.matmul(crow[:, 0:P], lf[0], C("neg_pre_in"), start=True, stop=True)
                    pe.matmul(crow[:, P:T], lf[0], C("neg_all"), start=True, stop=False)
                    pe.matmul(crow[:, P:T], lf[1], C("neg_pre_in"), start=False, stop=True).then_inc(S("f_c"), 1)

            pe.wait_ge(S("ident_in"), 16)
            pe.wait_ge(S("vec_in"), 144)
            pe.transpose(pC[:, 0:88], vrows[0:88, :], ident[0:88, 0:88]).then_inc(S("n_vecT"), 1)
            pe.wait_ge(S("cs_set"), 1)
            pe.wait_ge(S("diag_set"), 1)
            for seg in range(4):
                for b in range(4):
                    B = 4 * seg + b
                    if B >= 2:
                        pe.wait_ge(evac_act, B - 1)
                    if seg == 3:
                        pe.wait_ge(brow_in, 16 * (b + 1))
                        add_row(B % 2)

                    def after(u):
                        if seg:
                            head(seg - 1, b, u)
                        else:
                            forget_gates(B, u)
                        every_other(B // 2, B % 2, u)
                    product(BU * B, 0, B % 2, a_hi, a_lo, BU, opened=(seg == 3), after=after,
                            turning=("x", x_sb, True, 0) if B == 0 else None)
            pe.wait_ge(S("h_ylo"), NBR * HEADS)
            for c in range(DC):
                B = B_UP0 + c
                if c < 2:
                    pe.wait_ge(evac_act, B - 1)
                else:
                    pe.wait_ge(evac_dve, c - 1)
                product(U_UP0 + UPU * c, UPU * c, B % 2, ys_hi, ys_lo, UPU)
            pe.wait_ge(evac_dve, DC)
            with pe.Fori(0, DC) as c:
                for j in range(2):
                    u0 = U_PAIRS + 2 * PAIR * c + PAIR * j
                    pe.wait_ge(brow_in, 16 * (DC + 2 * c + j + 1))
                    pe.wait_ge(evac_act, 16 + 2 * c + j)
                    add_row(0)
                    product(u0, PAIR * j, 0, a_hi, a_lo, BU, opened=True, after=lambda u: every_other(8 + c, j, u))
                    pe.wait_ge(evac_dve, DC + 2 * c + j)
                    product(u0 + BU, PAIR * j + BU, 1, ys_hi, ys_lo, UPU, chunk0=4 * (j + 1))
            pe.wait_ge(evac_dve, 12)
            for c in range(DC):
                pe.wait_ge(evac_dve, 12 + c - 1 if c else 12)

                def after(u):
                    every_other(12 + c // 2, c % 2, u)
                    if (c, u) == (2, 3):
                        pe.wait_ge(S("mvr_in"), 272)
                        for r in range(2):
                            pe.transpose(pC[:, r * P:(r + 1) * P], mvr[:, r], ident)
                        pe.transpose(pC[:, 2 * P:2 * P + 32], mvb[:, :], ident[0:32, 0:32]).then_inc(S("mv_ps"), 1)
                    if (c, u) == (2, 7):
                        pe.wait_ge(S("diag_set"), 2)
                product(U_OUT + BU * c, 0, c % 2, a_hi, a_lo, BU, turning=("merged", merged, False, 0) if c == 0 else None,
                        after=after, turning_next=("ctx", ctx_sb, True, 0) if c == DC - 1 else None)

            def small_product(n):
                if n == 0:
                    pe.wait_ge(S("wsm_in"), 48)
                else:
                    pe.wait_ge(S("sm_in"), n)
                narrow_product(wsm).then_inc(S("s_ps"), 1)

            def small_stack(n):
                pe.wait_ge(S("s_parts"), n + 1)
                stacked(zparts).then_inc(S("s_tok"), 1)

            for cb in range(6):
                if cb < 2:
                    pe.wait_ge(evac_dve, 15 + cb)
                else:
                    pe.wait_ge(evac_act, 24 + cb - 1)

                def after(u):
                    mod_unit(14 + cb, u)
                    if (cb, u) == (0, 7):
                        small_product(0)
                    if (cb, u) == (1, 1):
                        small_stack(0)
                    if (cb, u) == (4, 7):
                        pe.wait_ge(S("diag_set"), 3)
                product(U_CTX + BU * cb, 0, (B_CTX + cb) % 2, a_hi, a_lo, BU, after=after,
                        turned="ctx" if cb == 0 else None, turning_next=("x1", xres, True, 0) if cb == 5 else None)

            LF = sx[:, 3].rearrange("p (t d h) -> p t d h", t=4, d=2)
            LAc = lambda t, d: y[:, t, 2 * BW + d * BW:2 * BW + (d + 1) * BW]

            def step(s):
                if s == 7:
                    small_product(1)
                if s == 9:
                    small_stack(1)
                if s == 13:
                    pe.wait_ge(S("m_lf"), 1)
                    F = pC[:, P:P + 32].rearrange("p (t d h) -> p t d h", t=4, d=2)
                    for t, d, terms in ((0, 0, (("suf_ex", 0), ("all", 1))), (1, 0, (("suf_ex", 1),)),
                                        (0, 1, (("pre_ex", 0),)), (1, 1, (("all", 0), ("pre_ex", 1))),
                                        (2, 0, (("pre_in", 2),)), (3, 0, (("all", 2), ("pre_in", 3))),
                                        (2, 1, (("suf_in", 2), ("all", 3))), (3, 1, (("suf_in", 3),))):
                        for n, (name, t2) in enumerate(terms):
                            mm = pe.matmul(F[:, t, d], MT[name], LF[:, t2, d], start=(n == 0), stop=(n == len(terms) - 1))
                    mm.then_inc(S("m_F"), 1)
                if s == 15:
                    pe.wait_ge(S("m_G"), 1)
                    for t in range(4):
                        mm = pe.transpose(pA[0:8, t * P:(t + 1) * P], sx[:, 4, 8 * t:8 * t + 8], ident)
                    mm.then_inc(S("m_GT"), 1)
                if s == 17:
                    pe.wait_ge(S("m_rows"), 1)
                    for rt in range(RT):
                        for w in range(2):
                            mm = pe.transpose(pB[:, 16 * rt + 8 * w:16 * rt + 8 * w + 8], mrows[:, w, rt * P:(rt + 1) * P], ident[0:8, 0:8])
                    mm.then_inc(S("m_MT"), 1)
                if s == 18:
                    for t in range(4):
                        mm = pe.transpose(pA[0:LR, t * P:(t + 1) * P], sm[:, t, 0:LR], ident)
                    mm.then_inc(S("g_glr"), 1)
                if 20 <= s < 28:
                    n = s - 20
                    if n == 0:
                        pe.wait_ge(S("wlr_in"), 32)
                        pe.wait_ge(S("g_glrT"), 1)
                        pe.wait_ge(S("m_FM"), 1)
                    if n >= 2:
                        pe.wait_ge(S("g_la"), n - 1)
                    t, d = n // 2, n % 2
                    pe.matmul(ps[:, n % 2], glrT[0:LR + 1, t * P:(t + 1) * P], wlr[0:LR + 1, d], start=True, stop=True).then_inc(S("g_dec"), 1)
                if 28 <= s < 32:
                    m = s - 28
                    t, d = m // 2, m % 2
                    pe.wait_ge(S("g_la"), 8 if m % 2 else 6)
                    if m >= 2:
                        pe.wait_ge(S("g_kexp"), m - 1)
                    bank = (pC, pA)[m % 2]
                    terms = {(0, 0): (("suf_ex", 0), ("all", 1)), (1, 0): (("suf_ex", 1),),
                             (0, 1): (("pre_ex", 0),), (1, 1): (("all", 0), ("pre_ex", 1))}[t, d]
                    for n, (name, t2) in enumerate(terms):
                        mm = pe.matmul(bank, MT[name], LAc(t2, d), start=(n == 0), stop=(n == len(terms) - 1))
                    mm.then_inc(S("g_w"), 1)
                if 32 <= s < 60:
                    h, u = (s - 32) // 7, (s - 32) % 7
                    if u == 0:
                        if h:
                            pe.wait_ge(S("m_y"), h)
                        else:
                            pe.wait_ge(evac_act, 30 + 4)
                            pe.wait_ge(S("g_kexp"), 4)
                        for rt in range(RT):
                            pe.transpose(pA[:, rt * P:(rt + 1) * P], cm[:, rt, h * HD:(h + 1) * HD], ident)
                            pe.transpose(pA[:, T + rt * P:T + (rt + 1) * P], xm[:, rt, BW + h * HD:BW + (h + 1) * HD], ident)
                            mm = pe.transpose(pB[:, rt * P:(rt + 1) * P], xm[:, rt, h * HD:(h + 1) * HD], ident)
                        mm.then_inc(S("m_T"), 1)
                    if u == 2:
                        pe.wait_ge(S("m_kT"), h + 1)
                        pe.wait_ge(S("m_qT"), h + 1)
                        for t in range(4):
                            pe.matmul(ps[:, t // 2, t % 2 * T:(t % 2 + 1) * T], mkT[:, t * P:(t + 1) * P], mqT[:, :], start=True, stop=True)
                        for d in range(2):
                            r = 4 * d + h
                            mm = pe.matmul(pC[:, d * T:(d + 1) * T], C("sel", 8, r * P, P), mrows[:, d], start=True, stop=True)
                        mm.then_inc(S("m_QK"), 1)
                    if u in (4, 6):
                        d = u == 6
                        if h == 0 and d == 0:
                            pe.wait_ge(mod_evac, 22)
                        pe.wait_ge(S("m_s"), 2 * h + d + 1)
                        num(h, int(d))
                if s == 60:
                    pe.wait_ge(S("m_y"), HEADS)
                    for d in range(2):
                        for h in range(HEADS):
                            out = ps[:, 2 * d + h // 2, h % 2 * GDV:(h % 2 + 1) * GDV]
                            for t in range(RT):
                                mm = pe.matmul(out, y[:, t, d * BW + h * HD:d * BW + (h + 1) * HD], cg[:, t, BW + h * GDV:BW + (h + 1) * GDV],
                                               start=(t == 0), stop=(t == 1))
                    mm.then_inc(S("g_S"), 1)
                if 62 <= s <= 94:
                    gla_fill(s - 62)

            def half_step(s):
                if 64 <= s < 96:
                    gla_score(s - 64)
                if 66 <= s < 98 and s % 2 == 0:
                    gla_out((s - 66) // 2)

            MT = {n: C(n) for n in ("pre_in", "suf_in", "pre_ex", "suf_ex", "all")}
            tiles = (((0, 0, T), (1, 0, T), (2, 0, T), (3, P, T)), ((0, 0, T), (1, 0, T), (3, 0, T), (2, 0, P)))
            def num(h, d):
                v = [cm[:, 0, BW:], cm[:, 1, BW:], xm[:, 0, 2 * BW:], xm[:, 1, 2 * BW:]]
                for rt in range(RT):
                    seen = [(t, 2 * P * n + rt * P - lo) for n, (t, lo, hi) in enumerate(tiles[d]) if lo <= rt * P < hi]
                    for n, (t, at0) in enumerate(seen):
                        pe.matmul(numb[d][:, rt * GDV:(rt + 1) * GDV], mpT[:, at0:at0 + P], v[t][:, h * GDV:(h + 1) * GDV],
                                  start=(n == 0), stop=(n == len(seen) - 1))
                for rt in range(RT):
                    seen = [(t, 2 * P * n + rt * P - lo) for n, (t, lo, hi) in enumerate(tiles[d]) if lo <= rt * P < hi]
                    for n, (t, at0) in enumerate(seen):
                        mm = pe.matmul(denb[:, 2 * d + rt:2 * d + rt + 1], mpT[:, at0:at0 + P], C("neg_all", P, 0, 1),
                                       start=(n == 0), stop=(n == len(seen) - 1))
                mm.then_inc(S("m_num"), 1)

            pe_turn = [0]

            def give():
                if pe_turn[0] >= 2:
                    pe.wait_ge(S("g_free"), pe_turn[0] - 1)
                pe_turn[0] += 1
                return ps[:, (pe_turn[0] - 1) % 2]

            def gla_fill(k):
                gc, j = k // 2, k % 2
                h, c = gc // 4, gc % 4
                d, rt = c // 2, c % 2
                if j == 0 and gc and c % 2 == 0:
                    dp = (gc - 1) % 4 // 2
                    pe.wait_ge(S("g_f"), gc)
                    pe.matmul(give()[:, 0:P], cr[:, dp], cr[:, 1 - dp], start=True, stop=True).then_inc(S("g_ps"), 1)
                if k == 32:
                    return
                if j == 0 and c == 0:
                    if h == 0:
                        pe.wait_ge(S("g_state"), 2)
                        pe.wait_ge(evac_act, 30 + 6)
                    bank = give()
                    for t in range(RT):
                        pe.transpose(bank[:, t * P:(t + 1) * P], xg[:, t, h * HD:(h + 1) * HD], ident)
                        mm = pe.transpose(bank[:, T + t * P:T + (t + 1) * P], xg[:, t, BW + h * HD:BW + (h + 1) * HD], ident)
                    mm.then_inc(S("g_ps"), 1)
                L = lambda t: la[:, t, d, h * HD:(h + 1) * HD]
                if j == 0:
                    bank = give()
                    edge = {(0, 0): "suf_ex", (0, 1): "pre_in", (1, 0): "suf_in", (1, 1): "pre_ex"}[d, rt]
                    since = "suf_in" if d else "pre_in"
                    pe.matmul(bank[:, 0:P], L(rt), MT[edge], start=True, stop=True)
                    far = rt != d
                    mm = pe.matmul(bank[:, P:2 * P], L(rt), MT[since], start=True, stop=not far)
                    if far:
                        mm = pe.matmul(bank[:, P:2 * P], L(1 - rt), MT["all"], start=False, stop=True)
                    mm.then_inc(S("g_ps"), 1)
                bank = give()
                if k == 0:
                    pe.wait_ge(S("lsum_in"), 32)
                pe.matmul(bank, L(rt), lsum[:, d, 4 * j:4 * j + 4].rearrange("p l t -> p (l t)"), start=True, stop=True).then_inc(S("g_ps"), 1)

            def gla_score(k):
                pe.wait_ge(S("g_mult"), k + 1)
                if k:
                    pe.wait_ge(S("g_masked"), k)
                for l in range(4):
                    mm = pe.matmul(pC[:, l * P:(l + 1) * P], rk[:, l], ek[:, k % 2, l], start=True, stop=True)
                mm.then_inc(S("g_sc"), 1)

            def gla_out(gc):
                h, c = gc // 4, gc % 4
                d, rt = c // 2, c % 2
                v = lambda t: xg[:, t, 2 * BW + h * GDV:2 * BW + (h + 1) * GDV]
                out = lambda t: pD[:, t * GDV:(t + 1) * GDV]
                kw = dict(skip_group_check=True)
                if gc == 0:
                    pe.wait_ge(evac_act, 30 + 8)
                pe.wait_ge(S("g_mask"), 2 * gc + 2)
                if c == 0 and h:
                    pe.wait_ge(S("g_y"), h)
                pe.matmul(out(rt), fq[:, gc % 2], state[:, d, h], start=(c == 0), stop=False, **kw)
                mm = pe.matmul(out(rt), sc[:, 0], v(rt), start=False, stop=False, **kw)
                if rt == 1:
                    pe.wait_ge(S("g_free"), 15 * h + (7 if d == 0 else 14) + 1)
                    mm = pe.matmul(out(1 - d), sc[:, 2], v(d), start=False, stop=(d == 1), **kw)
                mm.then_inc(S("g_o"), 1)

            numb, denb = (pD, pA), pC
            for xb in range(12):
                pe.wait_ge(evac_act, 30 + xb - 1)

                def after(u):
                    step(8 * xb + u)
                    if xb < 4:
                        every_other(20 + xb // 2, xb % 2, u)
                product(U_X + BU * xb, 0, (B_X + xb) % 2, a_hi, a_lo, BU, after=after,
                        turned="x1" if xb == 0 else None,
                        halfway=(lambda u: half_step(8 * xb + u)) if xb >= 8 else None)

            def second_vectors(s):
                if 6 <= s < 10:
                    n = s - 6
                    if n == 0:
                        pe.wait_ge(S("g_masked"), 32)
                        pe.wait_ge(S("gtr_in"), 32)
                    else:
                        pe.wait_ge(S("gt_in"), n)
                    pe.matmul(pC, C("neg_all", 5), gtr[:, n * NBLK:(n + 1) * NBLK], start=True, stop=True).then_inc(S("gt_ps"), 1)
                if s == 12:
                    pe.wait_ge(S("gt_in"), DC)
                    pe.wait_ge(S("mvr_in2"), 144)
                    pe.transpose(pC[:, 0:P], mvr[:, 0], ident)
                    pe.transpose(pC[:, P:P + 32], mvb[:, :], ident[0:32, 0:32]).then_inc(S("mv_ps"), 1)

            for c in range(DC):
                if c < 2:
                    pe.wait_ge(evac_act, 41 + c)
                else:
                    pe.wait_ge(evac_dve, 16 + c - 1)

                def after(u):
                    if c >= 2:
                        mod_unit(20 + c, u)
                    second_vectors(BU * c + u)
                product(U_OUT2 + BU * c, 0, c % 2, a_hi, a_lo, BU, after=after,
                        halfway=(lambda u: half_step(8 * 12 + u)) if c == 0 else None, turning=("y", y, False, KC // 2) if c == 0 else None)
            pe.wait_ge(S("mv_done"), 2)
            pe.wait_ge(S("cw_in"), 80)
            for t in range(4):
                k = (P, P, P, 10 * FCH - 3 * P)[t]
                mm = pe.transpose(pC[:, t * P:t * P + k], cwr[0:k, t], ident[0:k, 0:k])
            mm.then_inc(S("cw_ps"), 1)
            pe.wait_ge(S("diag_set"), 4)

            def turn_u(b, par, nf):
                pe.wait_ge(evac_act, 42 + b)
                if not (isinstance(b, int) and b == 1):
                    pe.wait_ge(S("f_fv"), b - 1)
                for half, bank in enumerate((pA, pB)):
                    for f in range(nf):
                        for rt in range(RT):
                            c0 = (half * nf + f) * P
                            mm = pe.transpose(bank[:, f * T + rt * P:f * T + (rt + 1) * P], ub[:, 1 - par, rt, c0:c0 + P], ident)
                mm.then_inc(S("f_T"), 1)

            def ffn_block(b, par, turned=2, n=NBLK):
                if isinstance(b, int) and b < 2:
                    pe.wait_ge(evac_dve, 19 + b)
                else:
                    pe.wait_ge(evac_act, 42 + b - 1)
                product(U_FFN + BU * b, 0, par, a_hi, a_lo, BU, n=n,
                        turning=("x2", xres, True, 0) if isinstance(b, int) and b == 0 else None,
                        after=lambda u: turn_u(b, par, turned) if u == 3 and turned else None)

            ffn_block(0, 0, 0)
            ffn_block(1, 1)
            with pe.Fori(0, 9) as n:
                for k in range(2):
                    ffn_block(2 * n + 2 + k, k)
            ffn_block(20, 0)
            ffn_block(21, 1, n=T)
            pe.wait_ge(S("f_lo"), 20)
            for c in range(DC):
                if c < 2:
                    pe.wait_ge(evac_act, 63 + c)
                else:
                    pe.wait_ge(evac_dve, 20 + c - 1)

                def after(u):
                    if c == 0 and u == 3:
                        turn_u(22, 0, 1)
                    if c == 0 and u == 19:
                        pe.wait_ge(S("f_lo"), FB)
                product(U_DOWN + DU * c, (DU * c) % SLOTS, c % 2, ft_hi, ft_lo, DU, chunks=FCH, after=after)
                if c == 0:
                    pe.wait_ge(S("gtr2_in"), 32)
                    for n in range(DC):
                        mm = pe.matmul(ps[:, n], C("neg_all", 5), gtr2[:, n * NBLK:(n + 1) * NBLK], start=True, stop=True)
                    mm.then_inc(S("gt_ps"), 1)


_INS = [
    "x", "norm_g", "w_in", "b_f", "b_gate", "qk_norm_g", "rel_bias", "w_up", "w_out", "c_2", "ctx_2", "c_ctx_2",
    "w_mod_2", "b_mod_2", "g_norm1_2", "g_norm2_2", "w_in_2", "gla_w_lr_2", "gla_b_lr_2", "mlstm_b_gate_2",
    "gla_g_norm_2", "mlstm_g_norm_2", "w_out_2", "w_up_2", "conv_w_2", "conv_b_2", "w_down_2", "g_final_2",
]
_OUTS = [((1, T, D), "float32")]


def kernel(**inputs):
    import numpy as _np
    import concourse.bacc as _bacc
    from concourse import mybir as _mybir
    from concourse.bass_utils import run_bass_kernel_spmd as _run

    nc = _bacc.Bacc("TRN2", target_bir_lowering=False, num_devices=1)
    arrays, args = {}, {}
    named = {name: _np.ascontiguousarray(inputs[name]) for name in _INS}
    named["const"], named["lsum"] = CONST, LSUM
    named["lpair"] = LPAIR.astype(_np.dtype("bfloat16"))
    for name, a in named.items():
        arrays[f"in_{name}_dram"] = a
        args[name] = nc.dram_tensor(f"in_{name}_dram", a.shape, _mybir.dt.from_np(a.dtype), kind="ExternalInput").ap()
    for i, (shape, dtype) in enumerate(_OUTS):
        dt = _mybir.dt.from_np(_np.dtype(dtype))
        args["out"] = nc.dram_tensor(f"out_{i}_dram", shape, dt, kind="ExternalOutput").ap()
    build(nc, args)
    r = _run(nc, [arrays], core_ids=[0])
    got = tuple(r.results[0][f"out_{i}_dram"] for i in range(len(_OUTS)))
    return got[0]
```
